# Optimizing a Trainium2 kernel written in Bass

```python
import math
import jax, jax.numpy as jnp
from jax import lax
import numpy as np

D_MODEL = 2048
BATCH = 1
SEQ = 256
DEPTH = 1

CTX_LEN = 256
GRID_W = 64

HEAD_DIM = 128
DA_HEADS = 8
DA_HALF = HEAD_DIM // 2
MLA_HEADS = 8
MLA_NOPE = 128
MLA_ROPE = 64
MLA_V = 128
Q_RANK = 384
KV_RANK = 256
ROPE_DIM = 64
ROPE_BASE = 10000.0
D_FF = 5632
CONV_W = 3
N_MOD = 6
EPS = 1e-6
Q_BLOCK = 128

DA_WIDTH = DA_HEADS * HEAD_DIM
MLA_WIDTH = MLA_HEADS * MLA_V
MIX_WIDTH = DA_WIDTH + MLA_WIDTH
MLA_QK = MLA_NOPE + MLA_ROPE
IN_WIDTH = 3 * DA_WIDTH + Q_RANK + KV_RANK + MLA_ROPE
DA_SCALE = 1.0 / math.sqrt(DA_HALF)
MLA_SCALE = 1.0 / math.sqrt(MLA_QK)


def _rmsnorm(x, w):
    xf = x.astype(jnp.float32)
    y = xf * lax.rsqrt(jnp.mean(xf * xf, axis=-1, keepdims=True) + EPS)
    return y.astype(x.dtype) * w

def _modulate(h, shift, scale):
    return h * (1.0 + scale) + shift

def _axial_rope_tables(n_tokens):
    rows = n_tokens // GRID_W
    row = jnp.broadcast_to(jnp.arange(rows)[:, None], (rows, GRID_W)).reshape(-1).astype(jnp.float32)
    col = jnp.broadcast_to(jnp.arange(GRID_W)[None, :], (rows, GRID_W)).reshape(-1).astype(jnp.float32)
    nf = ROPE_DIM // 4
    inv = ROPE_BASE ** (-jnp.arange(nf, dtype=jnp.float32) / nf)
    ang_r = row[:, None] * inv
    ang_c = col[:, None] * inv
    return (jnp.cos(ang_r), jnp.sin(ang_r), jnp.cos(ang_c), jnp.sin(ang_c))

def _rot(x, cos, sin):
    cos = cos.astype(x.dtype)
    sin = sin.astype(x.dtype)
    x1, x2 = jnp.split(x, 2, axis=-1)
    return jnp.concatenate([x1 * cos - x2 * sin, x2 * cos + x1 * sin], axis=-1)

def _axial_rope(x, tabs):
    cos_r, sin_r, cos_c, sin_c = tabs
    xr, xc = jnp.split(x, 2, axis=-1)
    return jnp.concatenate([_rot(xr, cos_r, sin_r), _rot(xc, cos_c, sin_c)], axis=-1)

def _mixer_inputs(h, tabs, w_in, q_norm_w, kv_norm_w, w_uq, w_ukv):
    B, T, _ = h.shape
    p = h @ w_in
    o1, o2, o3 = DA_WIDTH, 2 * DA_WIDTH, 3 * DA_WIDTH
    o4 = o3 + Q_RANK
    o5 = o4 + KV_RANK

    def heads(a, n):
        return a.reshape(B, T, n, -1).transpose(0, 2, 1, 3)

    q_da = heads(p[..., :o1], DA_HEADS)
    k_da = heads(p[..., o1:o2], DA_HEADS)
    v_da = heads(p[..., o2:o3], DA_HEADS)
    c_q = _rmsnorm(p[..., o3:o4], q_norm_w)
    c_kv = _rmsnorm(p[..., o4:o5], kv_norm_w)
    k_rope = p[..., o5:][:, None]
    q_mla = heads(c_q @ w_uq, MLA_HEADS)
    kv = heads(c_kv @ w_ukv, MLA_HEADS)
    q_nope, q_rope = q_mla[..., :MLA_NOPE], q_mla[..., MLA_NOPE:]
    k_nope, v_mla = kv[..., :MLA_NOPE], kv[..., MLA_NOPE:]
    if tabs is not None:
        q_da = jnp.concatenate([_axial_rope(q_da[..., :DA_HALF], tabs), _axial_rope(q_da[..., DA_HALF:], tabs)], -1)
        k_da = jnp.concatenate([_axial_rope(k_da[..., :DA_HALF], tabs), _axial_rope(k_da[..., DA_HALF:], tabs)], -1)
        q_rope = _axial_rope(q_rope, tabs)
        k_rope = _axial_rope(k_rope, tabs)
    q_mla = jnp.concatenate([q_nope, q_rope], axis=-1)
    k_mla = jnp.concatenate([k_nope, jnp.broadcast_to(k_rope, (B, MLA_HEADS, T, MLA_ROPE))], axis=-1)
    return q_da, k_da, v_da, q_mla, k_mla, v_mla

def _diff_attend(q, k, v, lam):
    q1, q2 = jnp.split(q, 2, axis=-1)
    k1, k2 = jnp.split(k, 2, axis=-1)
    s1 = jnp.einsum('bhqd,bhkd->bhqk', q1, k1).astype(jnp.float32) * DA_SCALE
    s2 = jnp.einsum('bhqd,bhkd->bhqk', q2, k2).astype(jnp.float32) * DA_SCALE
    w = jax.nn.softmax(s1, axis=-1) - lam * jax.nn.softmax(s2, axis=-1)
    return jnp.einsum('bhqk,bhkd->bhqd', w.astype(v.dtype), v)

def _softmax_attend(q, k, v, scale):
    s = jnp.einsum('bhqd,bhkd->bhqk', q, k).astype(jnp.float32) * scale
    p = jax.nn.softmax(s, axis=-1)
    return jnp.einsum('bhqk,bhkd->bhqd', p.astype(v.dtype), v)

def _sweep(block_fn, q):
    B, H, S, d = q.shape
    nb = S // Q_BLOCK
    qb = q.reshape(B, H, nb, Q_BLOCK, d).transpose(2, 0, 1, 3, 4)
    out = lax.map(block_fn, qb)
    return out.transpose(1, 2, 0, 3, 4).reshape(B, H, S, out.shape[-1])

def _merge_heads(o_da, o_mla, subln_w, lambda_init):
    o_da = _rmsnorm(o_da, subln_w) * (1.0 - lambda_init)
    B, _, T, _ = o_da.shape
    o_da = o_da.transpose(0, 2, 1, 3).reshape(B, T, DA_WIDTH)
    o_mla = o_mla.transpose(0, 2, 1, 3).reshape(B, T, MLA_WIDTH)
    return jnp.concatenate([o_da, o_mla], axis=-1)

def _conv_ffn(h, w_up, conv_w, conv_b, w_down):
    g, u = jnp.split(h @ w_up, 2, axis=-1)
    T = g.shape[1]
    pad = CONV_W // 2
    gp = jnp.pad(g, ((0, 0), (pad, pad), (0, 0)))
    g = sum(gp[:, j:j + T] * conv_w[j] for j in range(CONV_W)) + conv_b
    return (jax.nn.silu(g) * u) @ w_down

def first_inputs(seed: int = 0) -> dict:
    key = jax.random.key(seed)
    ks = jax.random.split(key, 24)
    f32 = jnp.float32

    def nrm(k, shape, fan_in, gain=1.0):
        return (gain * fan_in ** -0.5) * jax.random.normal(k, shape, f32)

    def gain(k, shape):
        return 1.0 + 0.05 * jax.random.normal(k, shape, f32)

    L = DEPTH
    return {
        "x": jax.random.normal(ks[0], (BATCH, SEQ, D_MODEL), f32),
        "c": jax.random.normal(ks[1], (BATCH, D_MODEL), f32),
        "ctx": jax.random.normal(ks[2], (BATCH, CTX_LEN, D_MODEL), f32),
        "c_ctx": jax.random.normal(ks[3], (D_MODEL,), f32),
        "w_ada": nrm(ks[4], (L, D_MODEL, N_MOD * D_MODEL), D_MODEL, 0.5),
        "b_ada": 0.02 * jax.random.normal(ks[5], (L, N_MOD * D_MODEL), f32),
        "norm1_w": gain(ks[6], (L, D_MODEL)),
        "w_in": nrm(ks[7], (L, D_MODEL, IN_WIDTH), D_MODEL),
        "q_norm_w": gain(ks[8], (L, Q_RANK)),
        "kv_norm_w": gain(ks[9], (L, KV_RANK)),
        "w_uq": nrm(ks[10], (L, Q_RANK, MLA_HEADS * MLA_QK), Q_RANK),
        "w_ukv": nrm(ks[11], (L, KV_RANK, MLA_HEADS * (MLA_NOPE + MLA_V)), KV_RANK),
        "lambda_q1": 0.1 * jax.random.normal(ks[12], (L, DA_HALF), f32),
        "lambda_k1": 0.1 * jax.random.normal(ks[13], (L, DA_HALF), f32),
        "lambda_q2": 0.1 * jax.random.normal(ks[14], (L, DA_HALF), f32),
        "lambda_k2": 0.1 * jax.random.normal(ks[15], (L, DA_HALF), f32),
        "subln_w": gain(ks[16], (L, HEAD_DIM)),
        "w_o": nrm(ks[17], (L, MIX_WIDTH, D_MODEL), MIX_WIDTH),
        "norm2_w": gain(ks[18], (L, D_MODEL)),
        "w_up": nrm(ks[19], (L, D_MODEL, 2 * D_FF), D_MODEL),
        "conv_w": nrm(ks[20], (L, CONV_W, D_FF), CONV_W),
        "conv_b": 0.02 * jax.random.normal(ks[21], (L, D_FF), f32),
        "w_down": nrm(ks[22], (L, D_FF, D_MODEL), D_FF),
        "final_w": gain(ks[23], (D_MODEL,)),
    }

def first_block(x, c, ctx, c_ctx, w_ada, b_ada, norm1_w, w_in, q_norm_w, kv_norm_w, w_uq, w_ukv,
              lambda_q1, lambda_k1, lambda_q2, lambda_k2, subln_w, w_o, norm2_w, w_up,
              conv_w, conv_b, w_down, final_w):
    B, S, D = x.shape
    tabs = _axial_rope_tables(S)
    xc = jnp.broadcast_to(ctx, ctx.shape)
    sc_ = jax.nn.silu(c)
    scc = jax.nn.silu(c_ctx)
    for l in range(DEPTH):
        mod_x = (sc_ @ w_ada[l] + b_ada[l])[:, None, :]
        mod_c = (scc @ w_ada[l] + b_ada[l])[None, None, :]
        sh1, s1, g1, sh2, s2, g2 = jnp.split(mod_x, N_MOD, axis=-1)
        sh1c, s1c, g1c, sh2c, s2c, g2c = jnp.split(mod_c, N_MOD, axis=-1)
        lambda_init = 0.8 - 0.6 * math.exp(-0.3 * l)
        lam = (jnp.exp(jnp.sum(lambda_q1[l].astype(jnp.float32) * lambda_k1[l].astype(jnp.float32)))
               - jnp.exp(jnp.sum(lambda_q2[l].astype(jnp.float32) * lambda_k2[l].astype(jnp.float32)))
               + lambda_init)
        proj = (w_in[l], q_norm_w[l], kv_norm_w[l], w_uq[l], w_ukv[l])

        h = _modulate(_rmsnorm(x, norm1_w[l]), sh1, s1)
        hc = _modulate(_rmsnorm(xc, norm1_w[l]), sh1c, s1c)
        q_da, k_da, v_da, q_mla, k_mla, v_mla = _mixer_inputs(h, tabs, *proj)
        qc_da, kc_da, vc_da, qc_mla, kc_mla, vc_mla = _mixer_inputs(hc, None, *proj)
        k_da_all = jnp.concatenate([kc_da, k_da], axis=2)
        v_da_all = jnp.concatenate([vc_da, v_da], axis=2)
        k_mla_all = jnp.concatenate([kc_mla, k_mla], axis=2)
        v_mla_all = jnp.concatenate([vc_mla, v_mla], axis=2)
        o_da = _sweep(lambda qb: _diff_attend(qb, k_da_all, v_da_all, lam), q_da)
        o_mla = _sweep(lambda qb: _softmax_attend(qb, k_mla_all, v_mla_all, MLA_SCALE), q_mla)
        x = x + g1 * (_merge_heads(o_da, o_mla, subln_w[l], lambda_init) @ w_o[l])

        h2 = _modulate(_rmsnorm(x, norm2_w[l]), sh2, s2)
        x = x + g2 * _conv_ffn(h2, w_up[l], conv_w[l], conv_b[l], w_down[l])

        if l < DEPTH - 1:
            oc_da = _diff_attend(qc_da, kc_da, vc_da, lam)
            oc_mla = _softmax_attend(qc_mla, kc_mla, vc_mla, MLA_SCALE)
            xc = xc + g1c * (_merge_heads(oc_da, oc_mla, subln_w[l], lambda_init) @ w_o[l])
            hc2 = _modulate(_rmsnorm(xc, norm2_w[l]), sh2c, s2c)
            xc = xc + g2c * _conv_ffn(hc2, w_up[l], conv_w[l], conv_b[l], w_down[l])
    return _rmsnorm(x, final_w)


DEPTH_2 = 2

DN_QK_HEADS = 8
DN_V_HEADS = 16
DN_DK = 128
DN_DV = 128
DN_CONV = 4
DN_CHUNK = 64
SW_HEADS = 8
SW_PATTERNS = ((128, 1), (512, 4), (2048, 16))
SW_GROUPS = 3
SW_BLOCK = 128
ROPE_THETA = 500000.0
ROPE_DIM_2 = HEAD_DIM // 4
SC_WIDTH = 3072
SC_CONV = 3

A_Q = DN_QK_HEADS * DN_DK
A_K = DN_QK_HEADS * DN_DK
A_V = DN_V_HEADS * DN_DV
A_Z = A_V
B_Q = SW_GROUPS * SW_HEADS * HEAD_DIM
B_K = SW_HEADS * HEAD_DIM
B_V = SW_HEADS * HEAD_DIM
B_Z = B_V
HYB_IN = A_Q + A_K + A_V + A_Z + 2 * DN_V_HEADS + B_Q + B_K + B_V + B_Z
HYB_MIX = A_V + B_V
N_EVEN = (DEPTH_2 + 1) // 2
N_ODD = DEPTH_2 // 2


def rmsnorm(x, w):
    xf = x.astype(jnp.float32)
    y = xf * lax.rsqrt(jnp.mean(xf * xf, axis=-1, keepdims=True) + EPS)
    return (y * w.astype(jnp.float32)).astype(x.dtype)

def causal_depthwise_conv(x, w):
    k = w.shape[1]
    rhs = jnp.transpose(w)[:, None, :].astype(x.dtype)
    return lax.conv_general_dilated(x, rhs, window_strides=(1,), padding=[(k - 1, 0)],
                                    dimension_numbers=('NWC', 'WIO', 'NWC'),
                                    feature_group_count=x.shape[-1])

def partial_rope(x, pos):
    half = ROPE_DIM_2 // 2
    inv = jnp.power(jnp.float32(ROPE_THETA), -jnp.arange(half, dtype=jnp.float32) * 2.0 / ROPE_DIM_2)
    ang = pos.astype(jnp.float32)[:, None] * inv[None, :]
    cos = jnp.cos(ang)[None, :, None, :]
    sin = jnp.sin(ang)[None, :, None, :]
    x1 = x[..., :half]
    x2 = x[..., half:ROPE_DIM_2]
    return jnp.concatenate([x1 * cos - x2 * sin, x2 * cos + x1 * sin, x[..., ROPE_DIM_2:]], axis=-1)

def l2norm(x):
    return x * lax.rsqrt(jnp.sum(x * x, axis=-1, keepdims=True) + EPS)

def gated_delta_chunked(q, k, v, beta, g):
    b, s, h, dk = q.shape
    dv = v.shape[-1]
    n = s // DN_CHUNK
    c = DN_CHUNK

    def chunks(t):
        return t.reshape(b, n, c, h, t.shape[-1]).transpose(0, 1, 3, 2, 4)

    q, k, v = chunks(q), chunks(k), chunks(v)
    beta = beta.reshape(b, n, c, h).transpose(0, 1, 3, 2)
    g = jnp.cumsum(g.reshape(b, n, c, h).transpose(0, 1, 3, 2), axis=-1)
    idx = jnp.arange(c)
    causal = idx[:, None] >= idx[None, :]
    strict = idx[:, None] > idx[None, :]
    diff = g[..., :, None] - g[..., None, :]
    decay = jnp.exp(jnp.where(causal, diff, -jnp.inf))
    kk = jnp.einsum('bnhik,bnhjk->bnhij', k, k)
    a_strict = jnp.where(strict, beta[..., :, None] * kk * decay, 0.0)
    rhs = jnp.concatenate([v * beta[..., None], k * (beta * jnp.exp(g))[..., None]], axis=-1)
    sol = lax.linalg.triangular_solve(a_strict, rhs, left_side=True, lower=True, unit_diagonal=True)
    u = sol[..., :dv]
    w = sol[..., dv:]
    qk = jnp.einsum('bnhik,bnhjk->bnhij', q, k) * decay

    def step(state, inp):
        q_c, k_c, u_c, w_c, g_c, qk_c = inp
        v_new = u_c - jnp.einsum('bhck,bhkv->bhcv', w_c, state)
        o = jnp.einsum('bhck,bhkv->bhcv', q_c * jnp.exp(g_c)[..., None], state) + \
            jnp.einsum('bhij,bhjv->bhiv', qk_c, v_new)
        g_last = g_c[..., -1]
        state = state * jnp.exp(g_last)[..., None, None] + jnp.einsum(
            'bhck,bhcv->bhkv', k_c * jnp.exp(g_last[..., None] - g_c)[..., None], v_new)
        return state, o

    xs = tuple(jnp.moveaxis(t, 1, 0) for t in (q, k, u, w, g, qk))
    state0 = jnp.zeros((b, h, dk, dv), jnp.float32)
    _, o = lax.scan(step, state0, xs)
    return o.transpose(1, 0, 3, 2, 4).reshape(b, s, h, dv)

def dilated_window_group(q, k, v, dil):
    b, s, h, dh = q.shape
    wb = SW_BLOCK
    ln = s // dil
    nb = -(-ln // wb)
    lp = nb * wb

    def strided(t):
        t = t.reshape(b, ln, dil, h, dh).transpose(0, 2, 3, 1, 4)
        t = jnp.pad(t, ((0, 0), (0, 0), (0, 0), (0, lp - ln), (0, 0)))
        return t.reshape(b, dil, h, nb, wb, dh)

    def with_prev(t):
        prev = jnp.concatenate([jnp.zeros_like(t[:, :, :, :1]), t[:, :, :, :-1]], axis=3)
        return jnp.concatenate([prev, t], axis=4)

    qs = strided(q)
    kb = with_prev(strided(k))
    vb = with_prev(strided(v))
    sc = jnp.einsum('brhnqc,brhnkc->brhnqk', qs, kb) * (dh ** -0.5)
    i = jnp.arange(wb)[:, None]
    j = jnp.arange(2 * wb)[None, :]
    dist = i + wb - j
    blk = jnp.arange(nb)[:, None, None]
    valid = (dist >= 0) & (dist <= wb) & (blk * wb - wb + j >= 0)
    sc = jnp.where(valid, sc, -jnp.inf)
    m = jnp.max(sc, axis=-1, keepdims=True)
    p = jnp.exp(sc - m)
    den = jnp.sum(p, axis=-1)
    num = jnp.einsum('brhnqk,brhnkc->brhnqc', p, vb)

    def unstride(t):
        rest = t.shape[5:]
        t = t.reshape((b, dil, h, lp) + rest)[:, :, :, :ln]
        return jnp.moveaxis(t, 3, 1).reshape((b, s, h) + rest)

    return unstride(num), unstride(den), unstride(m[..., 0])

def dilated_attention(q, k, v):
    nums, dens, maxs = [], [], []
    for gi, (window, dil) in enumerate(SW_PATTERNS):
        n_, d_, m_ = dilated_window_group(q[:, :, gi], k, v, dil)
        nums.append(n_)
        dens.append(d_)
        maxs.append(m_)
    mx = jnp.max(jnp.stack(maxs), axis=0)
    wts = [jnp.exp(m_ - mx) for m_ in maxs]
    num = sum(w_[..., None] * n_ for w_, n_ in zip(wts, nums))
    den = sum(w_ * d_ for w_, d_ in zip(wts, dens))
    return num / den[..., None]

def hybrid_layer(h, w_in, conv_w, a_log, dt_bias, dn_norm_w, w_out, pos):
    b, s, _ = h.shape
    f32 = jnp.float32
    proj = h @ w_in
    sizes = [A_Q, A_K, A_V, A_Z, DN_V_HEADS, DN_V_HEADS, B_Q, B_K, B_V, B_Z]
    offs = []
    acc = 0
    for sz in sizes[:-1]:
        acc += sz
        offs.append(acc)
    aq, ak, av, az, ab, aa, bq, bk, bv, bz = jnp.split(proj, offs, axis=-1)

    qkv = jax.nn.silu(causal_depthwise_conv(jnp.concatenate([aq, ak, av], axis=-1), conv_w)).astype(f32)
    q_a = l2norm(qkv[..., :A_Q].reshape(b, s, DN_QK_HEADS, DN_DK)) * (DN_DK ** -0.5)
    k_a = l2norm(qkv[..., A_Q:A_Q + A_K].reshape(b, s, DN_QK_HEADS, DN_DK))
    v_a = qkv[..., A_Q + A_K:].reshape(b, s, DN_V_HEADS, DN_DV)
    rep = DN_V_HEADS // DN_QK_HEADS
    q_a = jnp.repeat(q_a, rep, axis=2)
    k_a = jnp.repeat(k_a, rep, axis=2)
    beta = jax.nn.sigmoid(ab.astype(f32))
    g = -jnp.exp(a_log.astype(f32)) * jax.nn.softplus(aa.astype(f32) + dt_bias.astype(f32))
    o_a = gated_delta_chunked(q_a, k_a, v_a, beta, g)
    o_a = o_a * lax.rsqrt(jnp.mean(o_a * o_a, axis=-1, keepdims=True) + EPS) * dn_norm_w.astype(f32)
    y_a = (o_a.reshape(b, s, A_V) * jax.nn.silu(az.astype(f32))).astype(h.dtype)

    q_b = partial_rope(bq.astype(f32).reshape(b, s, SW_GROUPS * SW_HEADS, HEAD_DIM), pos)
    q_b = q_b.reshape(b, s, SW_GROUPS, SW_HEADS, HEAD_DIM)
    k_b = partial_rope(bk.astype(f32).reshape(b, s, SW_HEADS, HEAD_DIM), pos)
    v_b = bv.astype(f32).reshape(b, s, SW_HEADS, HEAD_DIM)
    o_b = dilated_attention(q_b, k_b, v_b)
    y_b = (o_b.reshape(b, s, B_V) * jax.nn.silu(bz.astype(f32))).astype(h.dtype)

    return jnp.concatenate([y_a, y_b], axis=-1) @ w_out

def shortconv_layer(h, w_in, conv_w, w_out):
    gate_b, gate_c, u, z = jnp.split(h @ w_in, 4, axis=-1)
    y = gate_b * causal_depthwise_conv(gate_c * u, conv_w)
    return (y * jax.nn.silu(z)) @ w_out

def second_inputs(seed: int = 0) -> dict:
    key = jax.random.key(seed)
    ks = jax.random.split(key, 14)
    f32 = jnp.float32

    def nrm(k, shape, scale):
        return jax.random.normal(k, shape, f32) * scale

    x = nrm(ks[0], (BATCH, SEQ, D_MODEL), 1.0)
    norm_w = 1.0 + nrm(ks[1], (DEPTH_2, D_MODEL), 0.05)
    hyb_w_in = nrm(ks[2], (N_EVEN, D_MODEL, HYB_IN), D_MODEL ** -0.5)
    dn_conv_w = nrm(ks[3], (N_EVEN, A_Q + A_K + A_V, DN_CONV), DN_CONV ** -0.5)
    dn_a_log = jnp.log(jax.random.uniform(ks[4], (N_EVEN, DN_V_HEADS), f32, 1.0, 16.0))
    dt = jnp.exp(jax.random.uniform(ks[5], (N_EVEN, DN_V_HEADS), f32, jnp.log(1e-3), jnp.log(1e-1)))
    dn_dt_bias = dt + jnp.log(-jnp.expm1(-dt))
    dn_norm_w = 1.0 + nrm(ks[6], (N_EVEN, DN_DV), 0.05)
    hyb_w_out = nrm(ks[7], (N_EVEN, HYB_MIX, D_MODEL), HYB_MIX ** -0.5)
    sc_w_in = nrm(ks[8], (N_ODD, D_MODEL, 4 * SC_WIDTH), D_MODEL ** -0.5)
    sc_conv_w = nrm(ks[9], (N_ODD, SC_WIDTH, SC_CONV), SC_CONV ** -0.5)
    sc_w_out = nrm(ks[10], (N_ODD, SC_WIDTH, D_MODEL), SC_WIDTH ** -0.5)
    final_norm_w = 1.0 + nrm(ks[11], (D_MODEL,), 0.05)
    return {"x": x, "norm_w": norm_w, "hyb_w_in": hyb_w_in, "dn_conv_w": dn_conv_w,
            "dn_a_log": dn_a_log, "dn_dt_bias": dn_dt_bias, "dn_norm_w": dn_norm_w,
            "hyb_w_out": hyb_w_out, "sc_w_in": sc_w_in, "sc_conv_w": sc_conv_w,
            "sc_w_out": sc_w_out, "final_norm_w": final_norm_w}

def second_block(x, norm_w, hyb_w_in, dn_conv_w, dn_a_log, dn_dt_bias, dn_norm_w, hyb_w_out,
              sc_w_in, sc_conv_w, sc_w_out, final_norm_w):
    pos = jnp.arange(x.shape[1], dtype=jnp.int32)
    h = x
    for layer in range(DEPTH_2):
        hn = rmsnorm(h, norm_w[layer])
        li = layer // 2
        if layer % 2 == 0:
            h = h + hybrid_layer(hn, hyb_w_in[li], dn_conv_w[li], dn_a_log[li], dn_dt_bias[li],
                                 dn_norm_w[li], hyb_w_out[li], pos)
        else:
            h = h + shortconv_layer(hn, sc_w_in[li], sc_conv_w[li], sc_w_out[li])
    return rmsnorm(h, final_norm_w)


def setup_inputs(seed=0):
    out = dict(first_inputs(seed))
    for name, value in second_inputs(seed + 1).items():
        if name != "x":
            out[name + "_2"] = value
    return out


def reference(
    x, c, ctx, c_ctx, w_ada, b_ada, norm1_w, w_in, q_norm_w, kv_norm_w, w_uq, w_ukv, lambda_q1,
    lambda_k1, lambda_q2, lambda_k2, subln_w, w_o, norm2_w, w_up, conv_w, conv_b, w_down,
    final_w, norm_w_2, hyb_w_in_2, dn_conv_w_2, dn_a_log_2, dn_dt_bias_2, dn_norm_w_2,
    hyb_w_out_2, sc_w_in_2, sc_conv_w_2, sc_w_out_2, final_norm_w_2,
):
    x = first_block(
        x, c, ctx, c_ctx, w_ada, b_ada, norm1_w, w_in, q_norm_w, kv_norm_w, w_uq, w_ukv,
        lambda_q1, lambda_k1, lambda_q2, lambda_k2, subln_w, w_o, norm2_w, w_up, conv_w, conv_b,
        w_down, final_w,
    )
    return second_block(
        x, norm_w_2, hyb_w_in_2, dn_conv_w_2, dn_a_log_2, dn_dt_bias_2, dn_norm_w_2,
        hyb_w_out_2, sc_w_in_2, sc_conv_w_2, sc_w_out_2, final_norm_w_2,
    )


_drawn_inputs = setup_inputs


def setup_inputs(seed=0):
    import zlib

    import numpy as np

    out = dict(_drawn_inputs(seed))
    spreads = {}
    factors = {'norm1_w': 4.827,
     'q_norm_w': 8.0,
     'kv_norm_w': 8.0,
     'lambda_q1': 4.41,
     'lambda_q2': 64.0,
     'lambda_k2': 3.883,
     'subln_w': 3.724,
     'conv_b': 8.0,
     'norm2_w': 4.902}
    for name, (base, spread) in spreads.items():
        noise = np.random.default_rng([zlib.crc32(name.encode()), seed]).standard_normal(out[name].shape)
        drawn = base * np.exp(spread * noise) if base else spread * noise
        out[name] = __import__('jax').numpy.asarray(drawn.astype(out[name].dtype))
    for name, factor in factors.items():
        out[name] = (out[name] * factor).astype(out[name].dtype)
    return out
```

```python
import math
from contextlib import ExitStack

import numpy as np

import concourse.bass as bass
from concourse import mybir

F32 = mybir.dt.float32
F32R = mybir.dt.float32r
ALU = mybir.AluOpType
ACT = mybir.ActivationFunctionType
AX = mybir.AxisListType.X

P = 128
SEQ = 256
TILES = SEQ // P
D = 2048
KT = D // P
CHUNK = 512
CT = CHUNK // P
GROUP = 4
RING = 4
EPS = 1e-6

HEADS = 8
HD = 128
HALF = HD // 2
DA_W = HEADS * HD
NOPE, ROPE, VD = 128, 64, 128
Q_RANK, KV_RANK = 384, 256
OFF_K, OFF_V, OFF_CQ = DA_W, 2 * DA_W, 3 * DA_W
OFF_CKV = OFF_CQ + Q_RANK
OFF_KR = OFF_CKV + KV_RANK
IN_W = OFF_KR + ROPE
D_FF = 5632
FT = D_FF // P
DA_SCALE = 1.0 / math.sqrt(HALF)
MLA_SCALE = 1.0 / math.sqrt(NOPE + ROPE)
LAMBDA_INIT = 0.8 - 0.6 * math.exp(-0.3 * 0)
N_MOD = 6
DN_QK, DN_V, DN_D = 8, 16, 128
DN_CHUNK = 64
SW_GROUPS, SW_HEADS = 3, 8
SW_PATTERNS = ((128, 1), (512, 4), (2048, 16))
A_QKV = 2 * DN_QK * DN_D + DN_V * DN_D
OFF_AZ = A_QKV
OFF_GATES = OFF_AZ + DN_V * DN_D
OFF_B = OFF_GATES + 2 * DN_V
W_BQ = SW_GROUPS * SW_HEADS * HD
W_RAW = DN_V * DN_D + W_BQ + 3 * SW_HEADS * HD
SW_SCALE = HD ** -0.5
SC_W = 3072
SC_KT = SC_W // P
MASKED = -1.0e30
FF_PARTS = ((0, 24), (24, 20))
MIX_KT = 24
SBUF_BYTES = 212800


def k_groups(n_k, n_groups):
    cuts = [n_k * g // n_groups for g in range(n_groups + 1)]
    out = [(a, b - a) for a, b in zip(cuts, cuts[1:])]
    assert all(0 < n <= GROUP for _, n in out)
    return out


class Count:

    def __init__(self, engine, sem):
        self.engine, self.sem, self.n, self.loop_at = engine, sem, 0, None

    def begin(self, i, first, per_turn):
        self.loop_at = (i, first, per_turn, self.n)

    def end(self, last):
        i, first, per_turn, start = self.loop_at
        assert self.n - start == per_turn, (self.n - start, per_turn)
        self.n = start + (last - first) * per_turn
        self.loop_at = None

    def done(self, instruction):
        self.n += 1
        instruction.then_inc(self.sem, 1)
        if self.loop_at is None:
            self.engine.wait_ge(self.sem, self.n)
        else:
            i, first, per_turn, _ = self.loop_at
            self.engine.wait_ge(self.sem, (i - first) * per_turn + self.n)


class Layer:

    def __init__(self, w, chunks, groups, pieces, accs, k0=0, both=False):
        self.w, self.chunks, self.groups, self.k0, self.both = w, chunks, groups, k0, both
        self.p0, self.c0 = pieces, accs
        self.per = len(groups)
        self.p1 = pieces + chunks * self.per
        self.c1 = accs + chunks * (2 if both else 1)


def at(v, i, step):
    return v if i is None else v + i * step


def build_program(nc, A, out):
    with ExitStack() as ctx:
        sems = {}

        def sem(name):
            if name not in sems:
                sems[name] = ctx.enter_context(nc.semaphore(name))
            return sems[name]

        ctx.enter_context(nc.sbuf_tensor("slab", [P, SBUF_BYTES // 4], F32))
        base = nc.sbuf_base - SBUF_BYTES
        top = [base]

        def place(name, shape, dt=F32, at=None):
            size = (int(np.prod(shape[1:])) * 4 + 31) // 32 * 32
            off = top[0] if at is None else at
            if at is None:
                top[0] += size
            assert off % 32 == 0 and off + size <= base + SBUF_BYTES, (name, off + size - base - SBUF_BYTES)
            return nc.alloc_sbuf_tensor_at(name, shape, dt, offset=off)

        def region(start, end):
            pos = [start]

            def put(name, shape, dt=F32):
                t = place(name, shape, dt, at=pos[0])
                pos[0] += (int(np.prod(shape[1:])) * 4 + 31) // 32 * 32
                assert pos[0] <= end, (name, pos[0] - end)
                return t
            return put

        raw = [place(f"raw{s}", [P, GROUP, CHUNK]) for s in range(RING)]
        w_hi = [place(f"w_hi{s}", [P, GROUP, CHUNK], F32R) for s in range(RING)]
        w_lo = [place(f"w_lo{s}", [P, GROUP, CHUNK], F32R) for s in range(RING)]
        A0 = top[0]
        a_hi = place("a_hi", [P, KT, SEQ], F32R)
        a_lo = place("a_lo", [P, KT, SEQ], F32R)
        B0 = top[0]
        b_hi = place("b_hi", [P, MIX_KT, SEQ], F32R)
        b_lo = place("b_lo", [P, MIX_KT, SEQ], F32R)
        X0 = top[0]
        X = place("X", [P, TILES, D])
        S0 = top[0]
        stg = [place(f"stg{i}", [P, TILES, CHUNK]) for i in range(2)]
        tmp = place("tmp", [P, 2, CHUNK])
        S1 = top[0]
        ident = place("ident_sb", [P, P])
        NCOL = 343 + 48 + 8
        col = place("col", [P, NCOL])
        stat = place("stat", [P, 32])
        diag = place("diag", [P, TILES, P])
        ps = ctx.enter_context(nc.psum_tensor("ps", [P, 8, CHUNK], F32))

        pos = 0
        C = {}
        row_tiles = [[("norm1_w", 16), ("norm2_w", 16), ("norm_w_2", 32), ("q_norm_w", 3), ("kv_norm_w", 2),
                      ("subln_w", 1), ("dn_norm_w_2", 1), ("conv_b", FT)],
                     [("conv_w0", FT), ("conv_w1", FT)], [("conv_w2", FT)],
                     [("sh1", 16), ("s1", 16), ("sh1c", 16), ("s1c", 16), ("sh2", 16), ("s2", 16)]]
        for tile in row_tiles:
            for name, n in tile:
                C[name] = col[:, pos:pos + n]
                pos += n
        for name in ("m1", "m1c", "m2"):
            C[name] = col[:, pos:pos + 16]
            pos += 16
        C["eps"] = col[:, pos:pos + 1]
        C["zero"] = col[:, pos + 1:pos + 2]
        C["lam"] = col[:, pos + 2:pos + 3]
        sub02 = col[:, pos + 3:pos + 4]

        def row_source(name):
            if name.startswith("conv_w"):
                tap = int(name[-1])
                v = A["conv_w"][0, tap:tap + 1, :].rearrange("a n -> (a n)")
            else:
                v = A[name].rearrange("a n -> (a n)")
            return v.rearrange("(r p) -> r p", p=P)

        layers = {}
        pieces = accs = 0

        def layer(name, w, chunks, n_k, n_groups, k0=0, both=False):
            nonlocal pieces, accs
            layers[name] = Layer(w, chunks, k_groups(n_k, n_groups), pieces, accs, k0, both)
            pieces, accs = layers[name].p1, layers[name].c1

        w_in = A["w_in"][0]
        layer("ada", A["w_ada"][0], N_MOD * D // CHUNK, KT, 4)
        layer("kv", w_in, 5, KT, 4, both=True)
        layer("q", w_in, 3, KT, 4)
        layer("uq", A["w_uq"][0], 3, Q_RANK // P, 1)
        layer("uk", A["w_ukv"][0], 4, KV_RANK // P, 1, both=True)
        accs += accs % 2
        layer("wo", A["w_o"][0], 4, KT, 4)
        layer("up0", A["w_up"][0], 12, KT, 4)
        layer("down0", A["w_down"][0], 4, 24, 8, k0=0)
        layer("up1", A["w_up"][0], 10, KT, 4)
        layer("down1", A["w_down"][0], 4, 20, 8, k0=24)
        hyb = A["hyb_w_in_2"][0]
        layer("conv", hyb, A_QKV // CHUNK, KT, 4)
        layer("az", hyb, DN_V * DN_D // CHUNK, KT, 4)
        layer("b", hyb, (W_RAW - DN_V * DN_D) // CHUNK, KT, 4)
        layer("gates", hyb, 1, KT, 4)
        layer("hout", A["hyb_w_out_2"][0], 4, 24, 8)
        layer("scin", A["sc_w_in_2"][0], 4 * SC_W // CHUNK, KT, 4)
        layer("scout", A["sc_w_out_2"][0], 4, SC_KT, 8)

        def dram(name, shape):
            return nc.dram_tensor(name, shape, F32, kind="Internal").ap()

        MOD = dram("mod_rows", (2, N_MOD * D))
        PROJ = dram("proj", (2 * SEQ, IN_W))
        PQ = dram("proj_q", (SEQ, HEADS * (NOPE + ROPE)))
        PKV = dram("proj_kv", (2 * SEQ, HEADS * (NOPE + VD)))

        def tok(ap):
            return ap.rearrange("(t p) n -> p t n", p=P)

        CONV = dram("conv_out", (SEQ, A_QKV))
        RAW = dram("raw_out", (SEQ, W_RAW + 2 * DN_V))
        GROW = dram("gate_rows", (DN_V, SEQ))
        n_sys = DN_V * SEQ // DN_CHUNK
        AM = dram("delta_a", (DN_V, TILES, P, DN_CHUNK))
        QM = dram("delta_qk", (DN_V, TILES, P, DN_CHUNK))
        UM = dram("delta_u", (DN_V, TILES, P, DN_CHUNK))

        def load_piece(sp, L, p, kt, n_k, c_at, ncols=CHUNK, i=None, step=0):
            s = p % RING
            if p >= RING or i is not None:
                sp.wait_ge(sem("lo_done"), at(p - RING + 1, i, step))
            k = (L.k0 + kt) * P
            sp.dma_start(raw[s][:, 0:n_k, 0:ncols],
                         L.w[k:k + n_k * P, bass.ds(c_at, ncols)].rearrange("(k p) n -> p k n", p=P)
                         ).then_inc(sem(f"landed{s}"), 16)

        def load_chunk(sp, L, n, c_at, ncols=CHUNK, i=None, step=0, skip=0):
            for g, (kt, n_k) in enumerate(L.groups):
                if g >= skip:
                    load_piece(sp, L, L.p0 + n * L.per + g, kt, n_k, c_at, ncols, i, step)

        def split_hi(act, L, n, g, ncols=CHUNK, i=None, step=0):
            p, n_k = L.p0 + n * L.per + g, L.groups[g][1]
            s = p % RING
            act.wait_ge(sem(f"landed{s}"), at(16 * (p // RING + 1), i, step * 16 // RING))
            if p >= RING or i is not None:
                act.wait_ge(sem("piece_used"), at(p - RING + 1, i, step))
            nc.scalar.activation(w_hi[s][:, 0:n_k, 0:ncols], raw[s][:, 0:n_k, 0:ncols], ACT.Copy
                                 ).then_inc(sem("hi_done"), 1)

        def split_lo(dve, L, n, g, ncols=CHUNK, i=None, step=0):
            p, n_k = L.p0 + n * L.per + g, L.groups[g][1]
            s = p % RING
            dve.wait_ge(sem("hi_done"), at(p + 1, i, step))
            nc.vector.tensor_tensor(w_lo[s][:, 0:n_k, 0:ncols], raw[s][:, 0:n_k, 0:ncols],
                                    w_hi[s][:, 0:n_k, 0:ncols].bitcast(F32), ALU.subtract
                                    ).then_inc(sem("lo_done"), 1)

        def split_chunk(split, eng, L, n, ncols=CHUNK, i=None, step=0, hooks={}, skip=0):
            for g in range(L.per):
                if g in hooks:
                    hooks[g]()
                if g >= skip:
                    split(eng, L, n, g, ncols, i, step)
            if "end" in hooks:
                hooks["end"]()

        def acc_pair(c):
            return 2 * (c % 2)

        def wait_acc_free(pe, c, i=None, cstep=0):
            if c // 2 > 0 or i is not None:
                pe.wait_ge(sem(f"acc_free{c % 2}"), at(c // 2, i, cstep // 2))

        def matmul_chunk(pe, L, n, c, acts, ncols=CHUNK, i=None, step=0, cstep=0, hooks={}):
            for j in range(len(acts)):
                wait_acc_free(pe, c + j, i, cstep)
            for g, (kt0, n_k) in enumerate(L.groups):
                if g in hooks:
                    hooks[g]()
                p = L.p0 + n * L.per + g
                s = p % RING
                pe.wait_ge(sem("lo_done"), at(p + 1, i, step))
                for k in range(n_k):
                    kt = kt0 + k
                    for j, (hi, lo) in enumerate(acts):
                        for t in range(TILES):
                            o = ps[:, acc_pair(c + j) + t, 0:ncols]
                            h, l = hi(kt, t), lo(kt, t)
                            nc.tensor.matmul(o, h, w_hi[s][:, k, 0:ncols], start=kt == 0, stop=False)
                            nc.tensor.matmul(o, h, w_lo[s][:, k, 0:ncols], start=False, stop=False)
                            last = nc.tensor.matmul(o, l, w_hi[s][:, k, 0:ncols], start=False,
                                                    stop=kt == L.groups[-1][0] + L.groups[-1][1] - 1)
                last.then_inc(sem("piece_used"), 1)
            if "end" in hooks:
                hooks["end"]()

        def chunk_done(eng, L, n, i=None, step=0):
            eng.wait_ge(sem("piece_used"), at(L.p0 + (n + 1) * L.per, i, step))

        def tile_of(buf, first=0):
            return lambda kt, t: buf[:, first + kt, t * P:(t + 1) * P]

        putA = region(A0, B0)
        putB = region(B0, X0)
        cond = putA("cond", [P, KT, P], F32R)
        condf = putA("condf", [P, KT, 2])
        condr = putA("condr", [P, 2, KT])
        mrow = [putA(f"mrow{i}", [P, CHUNK]) for i in range(2)]
        mout = [putA(f"mout{i}", [P, CHUNK]) for i in range(2)]
        sel = putA("sel_sb", [P, P])
        brow = putB("brow", [P, N_MOD * D])
        rows = [place(f"rows{i}", [P, P], at=S0 + i * P * 4) for i in range(4)]
        L_ada = layers["ada"]

        def vec_loads(sp):
            for ti in range(3):
                r = 0
                for name, n in row_tiles[ti]:
                    sp.dma_start(rows[ti][r:r + n, :], row_source(name)).then_inc(sem("rows_in"), 16)
                    r += n

        n_row_dmas = sum(len(t) for t in row_tiles[:3])

        def ada_sp(sp):
            with nc.allow_non_contiguous_dma(reason="two short vectors into columns"):
                sp.dma_start(condr[:, 0, :], A["c"][0].rearrange("(k p) -> p k", p=P)).then_inc(sem("cond_in"), 16)
                sp.dma_start(condr[:, 1, :], A["c_ctx"].rearrange("(k p) -> p k", p=P)).then_inc(sem("cond_in"), 16)
            sp.dma_start(sel[0:4, :], A["const_sel"]).then_inc(sem("cond_in"), 16)
            load_chunk(sp, L_ada, 0, 0)
            sp.dma_start(brow[0:2, :], A["b_ada"].to_broadcast([2, N_MOD * D])).then_inc(sem("brow_in"), 16)
            sp.dma_start(ident[:], A["const_ident"]).then_inc(sem("rows_in"), 16)
            load_chunk(sp, L_ada, 1, CHUNK)
            with sp.Fori(1, L_ada.chunks // 2) as i:
                for h in range(2):
                    load_chunk(sp, L_ada, h, i * (2 * CHUNK) + h * CHUNK, i=i, step=2 * L_ada.per)
            sp.dma_start(X[:], tok(A["x"][0])).then_inc(sem("x_in"), 16)
            vec_loads(sp)

        def ada_act(act):
            act.wait_ge(sem("cond_in"), 48)
            nc.scalar.activation(condf[:, :, 0:2].rearrange("p k j -> p j k"), condr[:], ACT.Silu).then_inc(sem("cond_act"), 1)
            act.wait_ge(sem("cond_act"), 1)
            act.wait_ge(sem("cond_dve"), 1)
            nc.scalar.activation(cond[:, :, 0:2], condf[:], ACT.Copy).then_inc(sem("cond_act"), 1)

            def store(n, i=None):
                act.wait_ge(sem("mout_ready"), at(n + 1, i, 2))
                act.dma_start(MOD[:, bass.ds(at(n * CHUNK, i, 2 * CHUNK), CHUNK)], mout[n % 2][0:2, :]
                              ).then_inc(sem(f"mod_stored{n % 2}"), 16)
            split_chunk(split_hi, act, L_ada, 0)
            split_chunk(split_hi, act, L_ada, 1, hooks={"end": lambda: store(0)})
            with act.Fori(1, L_ada.chunks // 2) as i:
                for h in range(2):
                    split_chunk(split_hi, act, L_ada, h, i=i, step=2 * L_ada.per,
                                hooks={"end": lambda: store(h - 1, i)})
            store(L_ada.chunks - 1)

        def ada_dve(dve, chain):
            nc.vector.memset(cond[:].bitcast(F32), 0.0).then_inc(sem("cond_dve"), 1)
            dve.wait_ge(sem("cond_act"), 2)
            nc.vector.tensor_tensor(cond[:, :, 2:4], condf[:], cond[:, :, 0:2].bitcast(F32), ALU.subtract
                                    ).then_inc(sem("cond_dve"), 1)

            def copy_row(n, i=None):
                chunk_done(dve, L_ada, n, i, 2 * L_ada.per)
                nc.vector.tensor_copy(mrow[n % 2][0:4, :], ps[0:4, acc_pair(n), :]).then_inc(sem(f"acc_free{n % 2}"), 1)

            def copy_out(n, i=None):
                dve.wait_ge(sem("msum"), at(n + 1, i, 2))
                if n >= 2 or i is not None:
                    dve.wait_ge(sem(f"mod_stored{n % 2}"), at(16 * (n // 2), i, 16))
                nc.vector.tensor_tensor(mout[n % 2][0:2, :], ps[0:2, 4 + n % 2, :],
                                        brow[0:2, bass.ds(at(n * CHUNK, i, 2 * CHUNK), CHUNK)], ALU.add
                                        ).then_inc(sem("mout_ready"), 1)
            split_chunk(split_lo, dve, L_ada, 0)
            dve.wait_ge(sem("brow_in"), 16)
            split_chunk(split_lo, dve, L_ada, 1, hooks={3: lambda: copy_row(0), "end": lambda: copy_out(0)})
            with dve.Fori(1, L_ada.chunks // 2) as i:
                for h in range(2):
                    split_chunk(split_lo, dve, L_ada, h, i=i, step=2 * L_ada.per,
                                hooks={3: lambda: copy_row(h - 1, i), "end": lambda: copy_out(h - 1, i)})
            copy_row(L_ada.chunks - 1)
            copy_out(L_ada.chunks - 1)

        def ada_pe(pe):
            pe.wait_ge(sem("cond_dve"), 2)

            def chunk(n, i=None, hooks={}):
                if i is not None:
                    pe.wait_ge(sem(f"acc_free{n % 2}"), i)
                for g, (kt0, n_k) in enumerate(L_ada.groups):
                    if g in hooks:
                        hooks[g]()
                    p = L_ada.p0 + n * L_ada.per + g
                    pe.wait_ge(sem("lo_done"), at(p + 1, i, 2 * L_ada.per))
                    for k in range(n_k):
                        kt = kt0 + k
                        o = ps[:, acc_pair(n), :]
                        nc.tensor.matmul(o, cond[:, kt, :], w_hi[p % RING][:, k, :], start=kt == 0, stop=False)
                        last = nc.tensor.matmul(o, cond[:, kt, :], w_lo[p % RING][:, k, :], start=False, stop=kt == KT - 1)
                    last.then_inc(sem("piece_used"), 1)

            def total(n, i=None):
                pe.wait_ge(sem(f"acc_free{n % 2}"), at(n // 2 + 1, i, 1))
                o = ps[:, 4 + n % 2, :]
                if n >= 2 or i is not None:
                    pe.wait_ge(sem("mout_ready"), at(n - 1, i, 2))
                nc.tensor.matmul(o, sel[0:4, :], mrow[n % 2][0:4, :], start=True, stop=True).then_inc(sem("msum"), 1)
            chunk(0)
            chunk(1, hooks={2: lambda: total(0)})
            with pe.Fori(1, L_ada.chunks // 2) as i:
                for h in range(2):
                    chunk(h, i, hooks={2: lambda: total(h - 1, i)})
            total(L_ada.chunks - 1)

        ctx_in = [place(f"ctx_in{t}", [P, D], at=B0 + (16 * SEQ + t * MIX_KT * SEQ) * 4) for t in range(2)]

        def cols_sp(sp):
            for t in range(2):
                if t == 0:
                    sp.wait_ge(sem("mout_ready"), L_ada.chunks)
                sp.dma_start(ctx_in[t][:], A["ctx"][0, t * P:(t + 1) * P, :]).then_inc(sem("ctx_in"), 16)
            for par in range(2):
                sp.wait_ge(sem(f"mod_stored{par}"), 16 * L_ada.chunks // 2)
            for r, j, c0 in ((0, 0, 0), (32, 1, 0), (64, 0, 3 * D)):
                sp.dma_start(rows[3][r:r + 32, :], MOD[j, c0:c0 + 2 * D].rearrange("(r p) -> r p", p=P)
                             ).then_inc(sem("rows_in"), 16)

        def cols_pe(pe):
            for ti in range(4):
                n = sum(n for _, n in row_tiles[ti])
                if ti == 0:
                    pe.wait_ge(sem("rows_in"), 16 * (n_row_dmas + 4))
                nc.tensor.transpose(ps[:, 6, ti * P:ti * P + n], rows[ti][0:n, :], ident[0:n, 0:n]
                                    ).then_inc(sem("col_t"), 1)

        def cols_dve(dve, chain):
            at_col = 0
            for ti in range(4):
                n = sum(n for _, n in row_tiles[ti])
                if ti == 0:
                    dve.wait_ge(sem("col_t"), 4)
                last = nc.vector.tensor_copy(col[:, at_col:at_col + n], ps[:, 6, ti * P:ti * P + n])
                at_col += n
            nc.vector.memset(C["eps"], EPS)
            nc.vector.memset(C["zero"], 0.0)
            chain.done(nc.vector.memset(sub02, LAMBDA_INIT))
            for m, s, w in (("m1", "s1", "norm1_w"), ("m1c", "s1c", "norm1_w"), ("m2", "s2", "norm2_w")):
                last = nc.vector.scalar_tensor_tensor(C[m], C[s], 1.0, C[w], ALU.add, ALU.mult)
            last.then_inc(sem("cols"), 1)
            dve.wait_ge(sem("cols"), 1)

        NORMS = ("n1", "n1c", "n2", "fn", "n3", "n4", "ln")
        DIAGS = ("n1", "n1c", "n2", "n3", "n4")
        FLIPS = {"n1": KT // 2, "n1c": KT // 2, "lat": 7, "mix": KT // 2, "n2": KT // 2, "n3": KT // 2,
                 "mix2": MIX_KT // 2, "n4": KT // 2}

        def flips_before(name):
            return sum(list(FLIPS.values())[:list(FLIPS).index(name)])

        def wait_rms(eng, name):
            eng.wait_ge(sem("norm_rms"), NORMS.index(name) + 1)

        def wait_diag(eng, name):
            eng.wait_ge(sem("norm_diag"), DIAGS.index(name) + 1)

        def wait_flipped(eng, name):
            eng.wait_ge(sem("flip_lo"), flips_before(name) + FLIPS[name])

        def norm_stats_act(act, name, srcs, n_ch, s_at):
            for t, src in enumerate(srcs):
                nc.scalar.activation(sq_scratch(n_ch), src, ACT.Square, accum_out=stat[:, s_at + t:s_at + t + 1]
                                     ).then_inc(sem("norm_ss"), 1)
                act.wait_ge(sem("norm_ss"), TILES * NORMS.index(name) + t + 1)
            nc.scalar.activation(stat[:, s_at:s_at + len(srcs)], stat[:, s_at:s_at + len(srcs)], ACT.Sqrt,
                                 bias=C["eps"], scale=1.0 / n_ch).then_inc(sem("norm_rms"), 1)

        sq = place("sq_scratch", [P, D], at=S0)

        def sq_scratch(n):
            return sq[:, 0:n]

        def norm_diag_dve(dve, name, n, s_at, chain):
            wait_rms(dve, name)
            chain.done(nc.vector.reciprocal(stat[:, s_at:s_at + n], stat[:, s_at:s_at + n]))
            for t in range(n):
                last = nc.vector.tensor_scalar(diag[:, t, :], ident[:], stat[:, s_at + t:s_at + t + 1], None, ALU.mult)
            last.then_inc(sem("norm_diag"), 1)

        def flip_pe(pe, name, src, n_pairs, right, first_wait):
            first_wait()
            m = flips_before(name)
            for j in range(n_pairs):
                if j >= 2:
                    pe.wait_ge(sem("flip_f"), m + j - 1)
                for k in range(2):
                    for t in range(TILES):
                        last = nc.tensor.matmul(ps[:, 4 + j % 2, (k * TILES + t) * P:(k * TILES + t + 1) * P],
                                                src(2 * j + k, t), right(t), start=True, stop=True)
                last.then_inc(sem("flip_t"), 1)

        def flip_dve(dve, name, n_pairs, scale, shift, hi, lo):
            m = flips_before(name)

            def low(j):
                dve.wait_ge(sem("flip_hi"), m + j + 1)
                nc.vector.tensor_tensor(lo[:, 2 * j:2 * j + 2, :], tmp_f(j), hi[:, 2 * j:2 * j + 2, :].bitcast(F32),
                                        ALU.subtract).then_inc(sem("flip_lo"), 1)
            for j in range(n_pairs):
                dve.wait_ge(sem("flip_t"), m + j + 1)
                if j >= 2:
                    dve.wait_ge(sem("flip_lo"), m + j - 1)
                for k in range(2):
                    kt = 2 * j + k
                    f = tmp_f(j)[:, k, :]
                    src = ps[:, 4 + j % 2, k * SEQ:(k + 1) * SEQ]
                    if shift is None:
                        last = nc.vector.tensor_scalar(f, src, scale(kt), None, ALU.mult)
                    else:
                        last = nc.vector.tensor_scalar(f, src, scale(kt), shift(kt), ALU.mult, ALU.add)
                last.then_inc(sem("flip_f"), 1)
                if j >= 1:
                    low(j - 1)
            low(n_pairs - 1)

        def flip_act(act, name, n_pairs, hi):
            for j in range(n_pairs):
                act.wait_ge(sem("flip_f"), flips_before(name) + j + 1)
                nc.scalar.activation(hi[:, 2 * j:2 * j + 2, :], tmp_f(j), ACT.Copy).then_inc(sem("flip_hi"), 1)

        def tmp_f(j):
            return tmp[:, j % 2, :].rearrange("p (k s) -> p k s", k=2)

        def c_of(name, first=0):
            return lambda kt: C[name][:, first + kt:first + kt + 1]

        KV, Q, UQ, UK = layers["kv"], layers["q"], layers["uq"], layers["uk"]
        LAT = Q_RANK
        kv_cols = [(OFF_K, CHUNK), (OFF_K + CHUNK, CHUNK), (OFF_V, CHUNK), (OFF_V + CHUNK, CHUNK),
                   (OFF_CKV, KV_RANK + ROPE)]
        q_cols = [(0, CHUNK), (CHUNK, CHUNK), (OFF_CQ, Q_RANK)]

        def proj_sp(sp):
            for n, (c0, w) in enumerate(kv_cols):
                load_chunk(sp, KV, n, c0, w)
            for n, (c0, w) in enumerate(q_cols):
                load_chunk(sp, Q, n, c0, w)

        def copy_pair(eng, L, n, c, buf, w, count):
            if eng is nc.scalar:
                nc.scalar.activation(buf[:, :, 0:w], ps[:, acc_pair(c):acc_pair(c) + 2, 0:w], ACT.Copy
                                     ).then_inc(sem(f"acc_free{c % 2}"), 1)
            else:
                nc.vector.tensor_copy(buf[:, :, 0:w], ps[:, acc_pair(c):acc_pair(c) + 2, 0:w]
                                      ).then_inc(sem(f"acc_free{c % 2}"), 1)

        stores = []
        for n, (c0, w) in enumerate(kv_cols):
            stores.append((KV, n, KV.c0 + 2 * n, True, PROJ, c0, w))
        for n, (c0, w) in enumerate(q_cols):
            stores.append((Q, n, Q.c0 + n, False, PROJ[SEQ:2 * SEQ], c0, w))
        for n in range(3):
            stores.append((UQ, n, UQ.c0 + n, False, PQ, n * CHUNK, CHUNK))
        for n in range(4):
            stores.append((UK, n, UK.c0 + 2 * n, True, PKV, n * CHUNK, CHUNK))

        def store_act(act, m):
            L, n, c, both, dst, c0, w = stores[m]
            chunk_done(act, L, n)
            if m >= 1:
                act.wait_ge(sem("stored_x"), 16 * m)
            copy_pair(nc.scalar, L, n, c, stg[0], w, m)
            act.wait_ge(sem(f"acc_free{c % 2}"), c // 2 + 1)
            x_rows = dst[SEQ:2 * SEQ] if both else dst
            act.dma_start(tok(x_rows[:, c0:c0 + w]), stg[0][:, :, 0:w]).then_inc(sem("stored_x"), 16)
            if both:
                act.wait_ge(sem(f"acc_free{(c + 1) % 2}"), (c + 1) // 2 + 1)
                act.dma_start(tok(dst[0:SEQ, c0:c0 + w]), stg[1][:, :, 0:w]).then_inc(sem("stored_c"), 16)

        def store_dve(dve, m):
            L, n, c, both, dst, c0, w = stores[m]
            if both:
                chunk_done(dve, L, n)
                before = sum(s[3] for s in stores[:m])
                if before:
                    dve.wait_ge(sem("stored_c"), 16 * before)
                copy_pair(nc.vector, L, n, c + 1, stg[1], w, m)

        def proj_stream(eng, split, store):
            m = 0
            for L, cols in ((KV, kv_cols), (Q, q_cols)):
                for n, (c0, w) in enumerate(cols):
                    hooks = {} if m == 0 else {3: (lambda m=m: store(eng, m - 1))}
                    split_chunk(split, eng, L, n, w, hooks=hooks, skip=3 if m == 0 else 0)
                    m += 1

        def presplit(split, eng, L, n=3, w=CHUNK):
            for g in range(n):
                split(eng, L, 0, g, w)

        def proj_pe(pe):
            hx = (tile_of(a_hi), tile_of(a_lo))
            hc = (tile_of(b_hi), tile_of(b_lo))
            wait_flipped(pe, "n1")
            wait_flipped(pe, "n1c")
            for n, (c0, w) in enumerate(kv_cols):
                matmul_chunk(pe, KV, n, KV.c0 + 2 * n, [hx, hc], w)
            for n, (c0, w) in enumerate(q_cols):
                matmul_chunk(pe, Q, n, Q.c0 + n, [hx], w)

        put = region(B0, X0)
        LAT0 = flips_before("lat")
        lat_q = put("lat_q", [P, TILES, Q_RANK])
        lat_kv = put("lat_kv", [P, 2 * TILES, KV_RANK])
        n_stored_proj = len(kv_cols) + len(q_cols)

        def lat_sp(sp):
            for n in range(3):
                load_chunk(sp, UQ, n, n * CHUNK)
            load_chunk(sp, UK, 0, 0)
            sp.wait_ge(sem("stored_x"), 16 * n_stored_proj)
            sp.wait_ge(sem("stored_c"), 16 * len(kv_cols))
            sp.dma_start(lat_q[:], tok(PROJ[SEQ:2 * SEQ, OFF_CQ:OFF_CQ + Q_RANK])).then_inc(sem("lat_in"), 16)
            sp.dma_start(lat_kv[:], tok(PROJ[:, OFF_CKV:OFF_CKV + KV_RANK])).then_inc(sem("lat_in"), 16)
            for n in range(1, 4):
                load_chunk(sp, UK, n, n * CHUNK)

        def lat_act(act):
            store_act(act, n_stored_proj - 1)
            act.wait_ge(sem("lat_in"), 32)
            for t in range(2):
                nc.scalar.activation(sq_scratch(Q_RANK), lat_q[:, t, :], ACT.Square, accum_out=stat[:, 4 + t:5 + t]
                                     ).then_inc(sem("lat_ss"), 1)
                act.wait_ge(sem("lat_ss"), t + 1)
            for t in range(4):
                nc.scalar.activation(sq_scratch(KV_RANK), lat_kv[:, t, :], ACT.Square, accum_out=stat[:, 6 + t:7 + t]
                                     ).then_inc(sem("lat_ss"), 1)
                act.wait_ge(sem("lat_ss"), 3 + t)
            nc.scalar.activation(stat[:, 4:6], stat[:, 4:6], ACT.Sqrt, bias=C["eps"], scale=1.0 / Q_RANK).then_inc(sem("lat_rms"), 1)
            nc.scalar.activation(stat[:, 6:10], stat[:, 6:10], ACT.Sqrt, bias=C["eps"], scale=1.0 / KV_RANK).then_inc(sem("lat_rms"), 1)
            for m in range(7):
                act.wait_ge(sem("flip_f"), LAT0 + m + 1)
                nc.scalar.activation(lat_hi(m), lat_f(m), ACT.Copy).then_inc(sem("flip_hi"), 1)
            for n in range(3):
                split_hi(act, UQ, n, 0)
            split_hi(act, UK, 0, 0)
            for n in range(3):
                store_act(act, n_stored_proj + n)
            for n in range(4):
                if n:
                    split_hi(act, UK, n, 0)
                store_act(act, n_stored_proj + 3 + n)

        lat_t = [("q", 0, 0), ("q", 1, 0), ("q", 2, 0), ("kv", 0, 0), ("kv", 1, 0), ("kv", 0, 1), ("kv", 1, 1)]

        def lat_f(m):
            return tmp[:, m % 2, 0:SEQ]

        def lat_hi(m):
            return a_hi[:, m, :]

        def lat_pe(pe):
            pe.wait_ge(sem("lat_scaled"), 1)
            for m, (kind, r, is_ctx) in enumerate(lat_t):
                if m >= 2:
                    pe.wait_ge(sem("flip_f"), LAT0 + m - 1)
                for t in range(TILES):
                    if kind == "q":
                        src = lat_q[:, t, r * P:(r + 1) * P]
                    else:
                        src = lat_kv[:, (0 if is_ctx else TILES) + t, r * P:(r + 1) * P]
                    last = nc.tensor.transpose(ps[:, 4 + m % 2, t * P:(t + 1) * P], src, ident[:])
                last.then_inc(sem("flip_t"), 1)
            wait_flipped(pe, "lat")
            hx = (tile_of(a_hi), tile_of(a_lo))
            for n in range(3):
                matmul_chunk(pe, UQ, n, UQ.c0 + n, [hx])
            kx = (tile_of(a_hi, 3), tile_of(a_lo, 3))
            kc = (tile_of(a_hi, 5), tile_of(a_lo, 5))
            for n in range(4):
                matmul_chunk(pe, UK, n, UK.c0 + 2 * n, [kx, kc])

        def lat_dve(dve, chain):
            store_dve(dve, n_stored_proj - 1)
            dve.wait_ge(sem("lat_rms"), 2)
            chain.done(nc.vector.reciprocal(stat[:, 4:10], stat[:, 4:10]))
            for t in range(2):
                nc.vector.tensor_scalar(lat_q[:, t, :], lat_q[:, t, :], stat[:, 4 + t:5 + t], None, ALU.mult)
            for t in range(4):
                last = nc.vector.tensor_scalar(lat_kv[:, t, :], lat_kv[:, t, :], stat[:, 6 + t:7 + t], None, ALU.mult)
            last.then_inc(sem("lat_scaled"), 1)

            def low(m):
                dve.wait_ge(sem("flip_hi"), LAT0 + m + 1)
                nc.vector.tensor_tensor(a_lo[:, m, :], lat_f(m), lat_hi(m).bitcast(F32), ALU.subtract
                                        ).then_inc(sem("flip_lo"), 1)
            for m, (kind, r, is_ctx) in enumerate(lat_t):
                dve.wait_ge(sem("flip_t"), LAT0 + m + 1)
                if m >= 2:
                    dve.wait_ge(sem("flip_lo"), LAT0 + m - 1)
                w = C["q_norm_w" if kind == "q" else "kv_norm_w"][:, r:r + 1]
                nc.vector.tensor_scalar(lat_f(m), ps[:, 4 + m % 2, 0:SEQ], w, None, ALU.mult).then_inc(sem("flip_f"), 1)
                if m:
                    low(m - 1)
            low(len(lat_t) - 1)
            for n in range(3):
                split_lo(dve, UQ, n, 0)
            split_lo(dve, UK, 0, 0)
            for n in range(4):
                if n:
                    split_lo(dve, UK, n, 0)
                store_dve(dve, n_stored_proj + 3 + n)

        put = region(B0, X0)
        put_a = region(A0, B0)
        n_keys = 2 * TILES
        q_in = [put(f"q_in{i}", [P, TILES, NOPE + ROPE]) for i in range(2)]
        k_in = [put(f"k_in{i}", [P, n_keys, HD]) for i in range(2)]
        v_in = [put(f"v_in{i}", [P, n_keys, HD]) for i in range(2)]
        qT = [put(f"qT{i}", [P, SEQ]) for i in range(2)]
        qrT = [put(f"qrT{i}", [P, SEQ]) for i in range(2)]
        kT = [put(f"kT{i}", [P, CHUNK]) for i in range(2)]
        krT = put("krT", [P, CHUNK])
        ex = [put(f"ex{i}", [P, 2, CHUNK]) for i in range(2)]
        wt = [put(f"wt{i}", [P, CHUNK]) for i in range(2)]
        wT = [put(f"wT{i}", [P, n_keys, P]) for i in range(2)]
        o_all = put_a("o_all", [P, TILES, D])
        rope_c = put_a("rope_c", [P, TILES, HD])
        rope_s = put_a("rope_s", [P, TILES, HD])
        rm = [put_a(f"rope_m{i}", [P, 2, TILES * HD]) for i in range(2)]
        kr_in = put_a("kr_in", [P, n_keys, ROPE])
        lam_in = put_a("lam_in", [P, 4, HALF])
        mx = [put_a(f"mx{i}", [P, 8]) for i in range(2)]
        ssum = put_a("ssum", [P, TILES * HEADS])
        lamt = put_a("lamt", [P, 4])
        WO = layers["wo"]

        def ev(v, i):
            return v if i is None else v + i * 2

        def ev2(v, i):
            return v if i is None else v + i * 4

        def head_col(h, i, width):
            return h * width if i is None else h * width + i * (2 * width)

        def att_load(sp, h, i=None):
            par = h % 2
            if h < HEADS:
                w = head_col(h, i, HD)
                w = w if i is None else sp.snap(w)
                srcs = (PROJ[SEQ:2 * SEQ, bass.ds(w, HD)], PROJ[:, OFF_K:][:, bass.ds(w, HD)],
                        PROJ[:, OFF_V:][:, bass.ds(w, HD)])
                dsts = (q_in[par][:, :, 0:HD], k_in[par][:], v_in[par][:])
            else:
                wq, wk = head_col(h - HEADS, i, NOPE + ROPE), head_col(h - HEADS, i, NOPE + VD)
                if i is not None:
                    wq, wk = sp.snap(wq), sp.snap(wk)
                srcs = (PQ[:, bass.ds(wq, NOPE + ROPE)], PKV[:, bass.ds(wk, NOPE)], PKV[:, NOPE:][:, bass.ds(wk, VD)])
                dsts = (q_in[par][:], k_in[par][:], v_in[par][:])
            if i is not None:
                sp.wait_ge(sem("at_pv"), ev2(2 * (h - 1), i))
            for d, s_ in zip(dsts, srcs):
                sp.dma_start(d, tok(s_)).then_inc(sem(f"at_in{par}"), 16)

        def att_sp(sp):
            sp.wait_ge(sem("stored_x"), 16 * len(stores))
            sp.wait_ge(sem("stored_c"), 16 * (len(kv_cols) + 4))
            sp.dma_start(rope_c[:], tok(A["const_rope_c"])).then_inc(sem("at_tab"), 16)
            sp.dma_start(rope_s[:], tok(A["const_rope_s"])).then_inc(sem("at_tab"), 16)
            for j, name in enumerate(("lambda_q1", "lambda_k1", "lambda_q2", "lambda_k2")):
                sp.dma_start(lam_in[:, j, :], A[name].to_broadcast([P, HALF])).then_inc(sem("at_tab"), 16)
            sp.dma_start(kr_in[:], tok(PROJ[:, OFF_KR:OFF_KR + ROPE])).then_inc(sem("at_tab"), 16)
            att_load(sp, 0)
            att_load(sp, 1)
            load_chunk(sp, WO, 0, 0)
            with sp.Fori(0, 3) as i:
                att_load(sp, 2, i)
                att_load(sp, 3, i)
            with sp.Fori(0, 4) as i:
                att_load(sp, 8, i)
                att_load(sp, 9, i)

        def rotate(chain, name, parts, i=None):
            for b, (x, c, s_) in enumerate(parts):
                n = x.shape[1] * x.shape[2]
                m = rm[b][:, :, 0:n]

                def halves(v):
                    return v.rearrange("p t (b h f) -> p t b h f", h=2, f=16)
                m0 = m[:, 0, :].rearrange("p (t n) -> p t n", t=x.shape[1])
                m1 = halves(m[:, 1, :].rearrange("p (t n) -> p t n", t=x.shape[1]))
                nc.gpsimd.tensor_tensor(m0, x, c, ALU.mult)
                for h in range(2):
                    for t in range(x.shape[1]):
                        last = nc.gpsimd.tensor_tensor(m1[:, t, :, h, :], halves(x)[:, t, :, 1 - h, :],
                                                       halves(s_)[:, t, :, h, :], ALU.mult)
            chain.done(last)
            for b, (x, c, s_) in enumerate(parts):
                n = x.shape[1] * x.shape[2]
                last = nc.gpsimd.tensor_tensor(x, rm[b][:, 0, 0:n].rearrange("p (t n) -> p t n", t=x.shape[1]),
                                               rm[b][:, 1, 0:n].rearrange("p (t n) -> p t n", t=x.shape[1]), ALU.add)
            last.then_inc(sem(name), 1)

        def att_rope(pool, chain, h, i=None):
            par = h % 2
            pool.wait_ge(sem(f"at_in{par}"), 48 * (h // 2 + 1) if i is None else 48 * (h // 2 + 1) + i * 48)
            if h >= 1 or i is not None:
                pool.wait_ge(sem("at_roped"), ev(h, i))
            if h < HEADS:
                rotate(chain, "at_roped", [(q_in[par][:, :, 0:HD], rope_c[:], rope_s[:]),
                                           (k_in[par][:, TILES:n_keys, :], rope_c[:], rope_s[:])])
            else:
                rotate(chain, "at_roped", [(q_in[par][:, :, NOPE:], rope_c[:, :, 0:ROPE], rope_s[:, :, 0:ROPE])])

        def att_pool(pool, chain):
            pool.wait_ge(sem("at_tab"), 16 * 7)
            rotate(chain, "kr_roped", [(kr_in[:, TILES:n_keys, :], rope_c[:, :, 0:ROPE], rope_s[:, :, 0:ROPE])])
            pool.wait_ge(sem("kr_roped"), 1)
            att_rope(pool, chain, 0)
            att_rope(pool, chain, 1)
            with pool.Fori(0, 3) as i:
                chain.begin(i, 0, 2)
                att_rope(pool, chain, 2, i)
                att_rope(pool, chain, 3, i)
                chain.end(3)
            with pool.Fori(0, 4) as i:
                chain.begin(i, 0, 2)
                att_rope(pool, chain, 8, i)
                att_rope(pool, chain, 9, i)
                chain.end(4)

        def att_flip(pe, h, i=None):
            par = h % 2
            pe.wait_ge(sem("at_roped"), ev(h + 1, i))
            if h >= 1 or i is not None:
                pe.wait_ge(sem("at_qT"), ev(h, i))
                pe.wait_ge(sem("at_kT"), ev(h, i))
            for t in range(TILES):
                nc.tensor.transpose(ps[:, 4, t * P:(t + 1) * P], q_in[par][:, t, 0:HD], ident[:])
                if h >= HEADS:
                    nc.tensor.transpose(ps[0:ROPE, 4, SEQ + t * P:SEQ + (t + 1) * P], q_in[par][:, t, NOPE:], ident[:])
            for t in range(n_keys):
                last = nc.tensor.transpose(ps[:, 5, t * P:(t + 1) * P], k_in[par][:, t, :], ident[:])
            last.then_inc(sem("at_flip"), 1)

        def att_scores(pe, h, t, i=None):
            par, u = h % 2, 2 * h + t
            if t == 0:
                pe.wait_ge(sem("at_qT"), ev(h + 1, i))
                pe.wait_ge(sem("at_kT"), ev(h + 1, i))
            if u >= 2:
                pe.wait_ge(sem("at_exp"), ev2(u - 1, i))
            cols = slice(t * P, (t + 1) * P)
            if h < HEADS:
                nc.tensor.matmul(ps[:, 2 * t, :], qT[par][0:HALF, cols], kT[par][0:HALF, :], start=True, stop=True)
                nc.tensor.matmul(ps[:, 2 * t + 1, :], qT[par][HALF:HD, cols], kT[par][HALF:HD, :], start=True,
                                 stop=True).then_inc(sem("at_sc"), 1)
            else:
                if h == HEADS and t == 0:
                    pe.wait_ge(sem("krT"), 1)
                nc.tensor.matmul(ps[:, 2 * t, :], qT[par][:, cols], kT[par][:], start=True, stop=False)
                nc.tensor.matmul(ps[:, 2 * t, :], qrT[par][:, cols], krT[:], start=False, stop=True
                                 ).then_inc(sem("at_sc"), 1)

        def att_wt(pe, u, i=None):
            latent = u >= 2 * HEADS
            pe.wait_ge(sem("at_w"), ev2(u + 1, i))
            if u >= 1:
                pe.wait_ge(sem("at_wT"), ev2(u, i))
            src = ex[u % 2][:, 0, :] if latent else wt[u % 2][:]
            for k in range(n_keys):
                last = nc.tensor.transpose(ps[:, 6, k * P:(k + 1) * P], src[:, k * P:(k + 1) * P], ident[:])
            last.then_inc(sem("at_wflip"), 1)

        def att_pv(pe, u, i=None):
            par = (u // 2) % 2
            pe.wait_ge(sem("at_wT"), ev2(u + 1, i))
            if u >= 1:
                pe.wait_ge(sem("at_o"), ev2(u, i))
            for k in range(n_keys):
                last = nc.tensor.matmul(ps[:, 7, 0:HD], wT[u % 2][:, k, :], v_in[par][:, k, :], start=k == 0,
                                        stop=k == n_keys - 1)
            last.then_inc(sem("at_pv"), 1)

        def att_head_pe(pe, h, i=None, flip_next=True):
            att_scores(pe, h, 0, i)
            if h >= 1:
                att_wt(pe, 2 * h - 1, i)
                att_pv(pe, 2 * h - 1, i)
            att_scores(pe, h, 1, i)
            if flip_next:
                att_flip(pe, h + 1, i)
            att_wt(pe, 2 * h, i)
            att_pv(pe, 2 * h, i)

        def over_heads(eng, emit, chain=None, per=0):
            for first in (0, HEADS):
                emit(first)
                with eng.Fori(0, 3) as i:
                    if chain:
                        chain.begin(i, 0, per[first])
                    emit(first + 1, i)
                    emit(first + 2, i)
                    if chain:
                        chain.end(3)
                emit(first + 7)

        def att_pe(pe):
            pe.wait_ge(sem("kr_roped"), 1)
            for t in range(n_keys):
                last = nc.tensor.transpose(ps[0:ROPE, 5, t * P:(t + 1) * P], kr_in[:, t, :], ident[:])
            last.then_inc(sem("kr_flip"), 1)
            pe.wait_ge(sem("krT"), 1)
            att_flip(pe, 0)
            over_heads(pe, lambda h, i=None: att_head_pe(pe, h, i, h != 2 * HEADS - 1))
            att_wt(pe, 4 * HEADS - 1)
            att_pv(pe, 4 * HEADS - 1)

        def att_qT(act, h, i=None):
            par = h % 2
            act.wait_ge(sem("at_flip"), ev(h + 1, i))
            if h >= 2:
                act.wait_ge(sem("at_sc"), ev2(2 * (h - 1), i))
            first = nc.scalar.activation(qT[par][:], ps[:, 4, 0:SEQ], ACT.Copy)
            if h >= HEADS:
                first = nc.scalar.activation(qrT[par][0:ROPE, :], ps[0:ROPE, 4, SEQ:2 * SEQ], ACT.Copy)
            first.then_inc(sem("at_qT"), 1)

        def att_exp(act, u, i=None):
            latent = u >= 2 * HEADS
            par = u % 2
            act.wait_ge(sem("at_max"), ev2(u + 1, i))
            if u >= 2:
                act.wait_ge(sem("at_wflip"), ev2(u - 1, i))
            for j in range(1 if latent else 2):
                last = nc.scalar.activation(ex[par][:, j, :], ps[:, 2 * par + j, :], ACT.Exp,
                                            bias=mx[par][:, 2 + j:3 + j], scale=MLA_SCALE if latent else DA_SCALE,
                                            accum_out=mx[par][:, 4 + j:5 + j])
            last.then_inc(sem("at_exp"), 1)

        def att_wT(act, u, i=None):
            act.wait_ge(sem("at_wflip"), ev2(u + 1, i))
            if u >= 2:
                act.wait_ge(sem("at_pv"), ev2(u - 1, i))
            nc.scalar.activation(wT[u % 2][:].rearrange("p k q -> p (k q)"), ps[:, 6, :], ACT.Copy
                                 ).then_inc(sem("at_wT"), 1)

        def att_head_act(act, h, i=None):
            if h >= 1:
                att_wT(act, 2 * h - 1, i)
            att_exp(act, 2 * h, i)
            att_exp(act, 2 * h + 1, i)
            if h != 2 * HEADS - 1:
                att_qT(act, h + 1, i)
            att_wT(act, 2 * h, i)

        def att_act(act):
            act.wait_ge(sem("lam_sums"), 1)
            nc.scalar.activation(lamt[:, 0:2], lamt[:, 2:4], ACT.Exp).then_inc(sem("lam_exp"), 1)
            att_qT(act, 0)
            over_heads(act, lambda h, i=None: att_head_act(act, h, i))
            att_wT(act, 4 * HEADS - 1)
            act.wait_ge(sem("o_ss"), 1)
            nc.scalar.activation(ssum[:], ssum[:], ACT.Sqrt, bias=C["eps"], scale=1.0 / HD).then_inc(sem("o_rms"), 1)

        def att_kT(dve, h, i=None):
            par = h % 2
            dve.wait_ge(sem("at_flip"), ev(h + 1, i))
            if h >= 2:
                dve.wait_ge(sem("at_sc"), ev2(2 * (h - 1), i))
            nc.vector.tensor_copy(kT[par][:], ps[:, 5, :]).then_inc(sem("at_kT"), 1)

        def att_max(dve, chain, u, i=None):
            latent = u >= 2 * HEADS
            par = u % 2
            n = 1 if latent else 2
            dve.wait_ge(sem("at_sc"), ev2(u + 1, i))
            chain.done(nc.vector.reduce_max(mx[par][:, 0:n], ps[:, 2 * par:2 * par + n, :], AX))
            nc.vector.tensor_scalar(mx[par][:, 2:2 + n], mx[par][:, 0:n], -(MLA_SCALE if latent else DA_SCALE), None,
                                    ALU.mult).then_inc(sem("at_max"), 1)

        def att_weights(dve, chain, u, i=None):
            latent = u >= 2 * HEADS
            par = u % 2
            dve.wait_ge(sem("at_exp"), ev2(u + 1, i))
            n = 1 if latent else 2
            if latent:
                nc.vector.reciprocal(mx[par][:, 6:7], mx[par][:, 4:5]).then_inc(sem("at_w"), 1)
                return
            chain.done(nc.vector.reciprocal(mx[par][:, 6:8], mx[par][:, 4:6]))
            chain.done(nc.vector.tensor_scalar(mx[par][:, 7:8], mx[par][:, 7:8], C["lam"], None, ALU.mult))
            if u >= 2:
                dve.wait_ge(sem("at_wflip"), ev2(u - 1, i))
            chain.done(nc.vector.tensor_scalar(wt[par][:], ex[par][:, 1, :], mx[par][:, 7:8], None, ALU.mult))
            nc.vector.scalar_tensor_tensor(wt[par][:], ex[par][:, 0, :], mx[par][:, 6:7], wt[par][:], ALU.mult, ALU.add
                                           ).then_inc(sem("at_w"), 1)

        def att_out(dve, u, i=None):
            h, t = u // 2, u % 2
            dve.wait_ge(sem("at_pv"), ev2(u + 1, i))
            dst = o_all[:, t, bass.ds(head_col(h, i, HD), HD)]
            if u < 2 * HEADS:
                nc.vector.tensor_copy(dst, ps[:, 7, 0:HD]).then_inc(sem("at_o"), 1)
            else:
                nc.vector.tensor_scalar(dst, ps[:, 7, 0:HD], mx[t][:, 6:7], None, ALU.mult).then_inc(sem("at_o"), 1)

        def att_head_dve(dve, chain, h, i=None):
            att_max(dve, chain, 2 * h, i)
            if h >= 1:
                att_out(dve, 2 * h - 1, i)
            att_weights(dve, chain, 2 * h, i)
            att_max(dve, chain, 2 * h + 1, i)
            if h != 2 * HEADS - 1:
                att_kT(dve, h + 1, i)
            att_weights(dve, chain, 2 * h + 1, i)
            att_out(dve, 2 * h, i)

        def att_dve(dve, chain):
            dve.wait_ge(sem("at_tab"), 16 * 7)
            chain.done(nc.vector.tensor_tensor(lam_in[:, 0:4:2, :], lam_in[:, 0:4:2, :], lam_in[:, 1:4:2, :], ALU.mult))
            nc.vector.reduce_sum(lamt[:, 2:4], lam_in[:, 0:4:2, :], AX).then_inc(sem("lam_sums"), 1)
            for i in range(2):
                nc.vector.memset(qrT[i][:], 0.0)
            chain.done(nc.vector.memset(krT[:], 0.0))
            dve.wait_ge(sem("kr_flip"), 1)
            nc.vector.tensor_copy(krT[0:ROPE, :], ps[0:ROPE, 5, :]).then_inc(sem("krT"), 1)
            dve.wait_ge(sem("lam_exp"), 1)
            chain.done(nc.vector.tensor_tensor(lamt[:, 2:3], lamt[:, 1:2], lamt[:, 0:1], ALU.subtract))
            chain.done(nc.vector.tensor_scalar(C["lam"], lamt[:, 2:3], -LAMBDA_INIT, None, ALU.add))
            att_kT(dve, 0)
            over_heads(dve, lambda h, i=None: att_head_dve(dve, chain, h, i), chain, {0: 16, HEADS: 4})
            att_out(dve, 4 * HEADS - 1)
            dve.wait_ge(sem("at_o"), 4 * HEADS)
            da = o_all[:, :, 0:DA_W]
            chain.done(nc.vector.tensor_tensor(sq[:].rearrange("p (t n) -> p t n", t=TILES), da, da, ALU.mult))
            nc.vector.reduce_sum(ssum[:], sq[:].rearrange("p (h d) -> p h d", d=HD), AX).then_inc(sem("o_ss"), 1)
            dve.wait_ge(sem("o_rms"), 1)
            chain.done(nc.vector.reciprocal(ssum[:], ssum[:]))
            for t in range(TILES):
                v = o_all[:, t, 0:DA_W].rearrange("p (h d) -> p h d", d=HD)
                r = ssum[:, t * HEADS:(t + 1) * HEADS].unsqueeze(2).to_broadcast([P, HEADS, HD])
                last = nc.vector.tensor_tensor(v, v, r, ALU.mult)
            chain.done(last)
            nc.vector.tensor_scalar(C["subln_w"], C["subln_w"], 1.0 - LAMBDA_INIT, None, ALU.mult
                                    ).then_inc(sem("o_scaled"), 1)
            dve.wait_ge(sem("o_scaled"), 1)

        gate = [place(f"gate{i}", [P, CHUNK], at=S0 + i * CHUNK * 4) for i in range(2)]
        gated = tmp

        def gate_load(sp, m, first, n):
            if m >= 2:
                sp.wait_ge(sem("res_mul"), m - 1)
            sp.dma_start(gate[m % 2][:], MOD[0:1, first + n * CHUNK:first + (n + 1) * CHUNK].to_broadcast([P, CHUNK])
                         ).then_inc(sem(f"gate_in{m % 2}"), 16)

        def residual(dve, chain, L, n, m):
            c = L.c0 + n
            chunk_done(dve, L, n)
            dve.wait_ge(sem(f"gate_in{m % 2}"), 16 * (m // 2 + 1))
            g = gate[m % 2][:].unsqueeze(1).to_broadcast([P, TILES, CHUNK])
            nc.vector.tensor_tensor(gated[:], ps[:, acc_pair(c):acc_pair(c) + 2, :], g, ALU.mult
                                    ).then_inc(sem("res_mul"), 1)
            dve.wait_ge(sem("res_mul"), m + 1)
            cols = slice(n * CHUNK, (n + 1) * CHUNK)
            nc.vector.tensor_tensor(X[:, :, cols], X[:, :, cols], gated[:], ALU.add
                                    ).then_inc(sem(f"acc_free{c % 2}"), 1)

        def x_ready(eng, L):
            c = L.c0 + L.chunks
            for k in (c - 2, c - 1):
                eng.wait_ge(sem(f"acc_free{k % 2}"), k // 2 + 1)

        mix = (tile_of(b_hi), tile_of(b_lo))
        hx = (tile_of(a_hi), tile_of(a_lo))

        def wo_sp(sp):
            sp.wait_ge(sem("o_ss"), 1)
            for n in range(4):
                gate_load(sp, n, 2 * D, n)
                if n:
                    load_chunk(sp, WO, n, n * CHUNK)

        def wo_pe(pe):
            wait_flipped(pe, "mix")
            for n in range(4):
                matmul_chunk(pe, WO, n, WO.c0 + n, [mix])

        def wo_act(act):
            for n in range(4):
                split_chunk(split_hi, act, WO, n, skip=3 if n == 0 else 0)

        def wo_dve(dve, chain):
            for n in range(4):
                hooks = {3: lambda: residual(dve, chain, WO, n - 1, n - 1)} if n else {}
                split_chunk(split_lo, dve, WO, n, hooks=hooks, skip=3 if n == 0 else 0)

        UP = [layers["up0"], layers["up1"]]
        DOWN = [layers["down0"], layers["down1"]]
        for L in UP:
            assert L.c0 % 2 == 0
        ff = tmp[:].rearrange("p a (k s) -> p (a k) s", s=SEQ)

        def ff_pair(q, j):
            return j + (UP[0].chunks // 2 if q else 0)

        def up_load(sp, q):
            L = UP[q]
            for h in range(2):
                load_chunk(sp, L, h, FF_PARTS[q][0] * P + h * D_FF)
            with sp.Fori(1, L.chunks // 2) as i:
                for h in range(2):
                    load_chunk(sp, L, h, i * CHUNK + (FF_PARTS[q][0] * P + h * D_FF), i=i, step=2 * L.per)

        def up_copy(act, q, n, i=None):
            L = UP[q]
            chunk_done(act, L, n, i, 2 * L.per)
            done = ff_pair(q, n // 2)
            if done >= 1 or i is not None:
                act.wait_ge(sem(f"ff_flip{n % 2}"), at(done, i, 1))
            if q == 1 and n == 0 and i is None:
                act.wait_ge(sem("res_mul"), 8)
            c = L.c0 + n
            nc.scalar.activation(stg[n % 2][:], ps[:, acc_pair(c):acc_pair(c) + 2, :], ACT.Copy
                                 ).then_inc(sem(f"acc_free{c % 2}"), 1)

        def up_flip(pe, q, n, i=None):
            c = UP[q].c0 + n
            done = ff_pair(q, n // 2)
            pe.wait_ge(sem(f"acc_free{c % 2}"), at(c // 2 + 1, i, 1))
            if done >= 1 or i is not None:
                pe.wait_ge(sem(("ff_conv", "ff_mul")[n % 2]), at(done, i, 1))
            for k in range(CT):
                for t in range(TILES):
                    last = nc.tensor.transpose(ps[:, 4 + 2 * (n % 2) + k // 2, (k % 2) * SEQ + t * P:(k % 2) * SEQ + (t + 1) * P],
                                               stg[n % 2][:, t, k * P:(k + 1) * P], ident[:])
            last.then_inc(sem(f"ff_flip{n % 2}"), 1)

        def up_conv(dve, chain, q, j, i=None):
            done = ff_pair(q, j)
            dve.wait_ge(sem("ff_flip0"), at(done + 1, i, 1))
            if done >= 1 or i is not None:
                dve.wait_ge(sem("ff_lo"), at(done, i, 1))
            kt = FF_PARTS[q][0] + j * CT if i is None else i * CT + (FF_PARTS[q][0] + j * CT)

            def w(name, k):
                a = kt + k
                return C[name][:, bass.ds(a, 1)]
            src = [ps[:, 4 + k // 2, (k % 2) * SEQ:(k % 2 + 1) * SEQ] for k in range(CT)]
            for k in range(CT):
                last = nc.vector.tensor_scalar(ff[:, k, :], src[k], w("conv_w1", k), w("conv_b", k), ALU.mult, ALU.add)
            chain.done(last)
            for k in range(CT):
                last = nc.vector.scalar_tensor_tensor(ff[:, k, 1:SEQ], src[k][:, 0:SEQ - 1], w("conv_w0", k),
                                                      ff[:, k, 1:SEQ], ALU.mult, ALU.add)
            chain.done(last)
            for k in range(CT):
                last = nc.vector.scalar_tensor_tensor(ff[:, k, 0:SEQ - 1], src[k][:, 1:SEQ], w("conv_w2", k),
                                                      ff[:, k, 0:SEQ - 1], ALU.mult, ALU.add)
            last.then_inc(sem("ff_conv"), 1)

        def up_silu(act, q, j, i=None):
            act.wait_ge(sem("ff_conv"), at(ff_pair(q, j) + 1, i, 1))
            nc.scalar.activation(ff, ff, ACT.Silu).then_inc(sem("ff_silu"), 1)

        def up_mul(dve, q, j, i=None):
            done = ff_pair(q, j)
            dve.wait_ge(sem("ff_silu"), at(done + 1, i, 1))
            dve.wait_ge(sem("ff_flip1"), at(done + 1, i, 1))
            nc.vector.tensor_tensor(tmp[:], tmp[:], ps[:, 6:8, :], ALU.mult).then_inc(sem("ff_mul"), 1)

        def b_tiles(buf, j, i):
            a = j * CT if i is None else i * CT + j * CT
            return buf[:, bass.ds(a, CT), :]

        def up_hi(act, q, j, i=None):
            if j == 0 and i is None and q == 1:
                chunk_done(act, DOWN[0], 3)
            act.wait_ge(sem("ff_mul"), at(ff_pair(q, j) + 1, i, 1))
            nc.scalar.activation(b_tiles(b_hi, j, i), ff, ACT.Copy).then_inc(sem("ff_hi"), 1)

        def up_lo(dve, q, j, i=None):
            dve.wait_ge(sem("ff_hi"), at(ff_pair(q, j) + 1, i, 1))
            nc.vector.tensor_tensor(b_tiles(b_lo, j, i), ff, b_tiles(b_hi, j, i).bitcast(F32), ALU.subtract
                                    ).then_inc(sem("ff_lo"), 1)

        def up_pe(pe, q):
            L = UP[q]
            for h in range(2):
                matmul_chunk(pe, L, h, L.c0 + h, [hx])
            with pe.Fori(1, L.chunks // 2) as i:
                kw = dict(i=i, step=2 * L.per, cstep=2)
                matmul_chunk(pe, L, 0, L.c0, [hx], hooks={2: lambda: up_flip(pe, q, -2, i), "end": lambda: up_flip(pe, q, -1, i)}, **kw)
                matmul_chunk(pe, L, 1, L.c0 + 1, [hx], **kw)

        def up_act(act, q, skip, first_hook=None):
            L = UP[q]
            split_chunk(split_hi, act, L, 0, skip=skip)
            split_chunk(split_hi, act, L, 1, hooks={3: lambda: up_copy(act, q, 0)})
            with act.Fori(1, L.chunks // 2) as i:
                kw = dict(i=i, step=2 * L.per)
                split_chunk(split_hi, act, L, 0, hooks={3: lambda: up_copy(act, q, -1, i)}, **kw)
                split_chunk(split_hi, act, L, 1, hooks={
                    1: lambda: up_silu(act, q, -1, i),
                    3: lambda: (up_hi(act, q, -1, i), up_copy(act, q, 0, i))}, **kw)

        def up_dve(dve, chain, q, skip, first_hooks={}):
            L = UP[q]
            split_chunk(split_lo, dve, L, 0, skip=skip, hooks=first_hooks)
            split_chunk(split_lo, dve, L, 1)
            with dve.Fori(1, L.chunks // 2) as i:
                kw = dict(i=i, step=2 * L.per)
                chain.begin(i, 1, 2)
                split_chunk(split_lo, dve, L, 0, hooks={"end": lambda: up_conv(dve, chain, q, -1, i)}, **kw)
                split_chunk(split_lo, dve, L, 1, hooks={2: lambda: up_mul(dve, q, -1, i), "end": lambda: up_lo(dve, q, -1, i)}, **kw)
                chain.end(L.chunks // 2)

        def down_pe(pe, q):
            L, U = DOWN[q], UP[q]
            last = U.chunks // 2 - 1
            up_flip(pe, q, U.chunks - 2)
            up_flip(pe, q, U.chunks - 1)

            def own_inputs():
                pe.wait_ge(sem("ff_lo"), ff_pair(q, last) + 1)
            first = next(g for g, (kt, n) in enumerate(L.groups) if kt + n > last * CT)
            pe.wait_ge(sem("ff_lo"), ff_pair(q, last))
            for n in range(4):
                matmul_chunk(pe, L, n, L.c0 + n, [mix], hooks={first: own_inputs} if n == 0 else {})

        def down_act(act, q):
            L, U = DOWN[q], UP[q]
            last = U.chunks // 2 - 1
            split_chunk(split_hi, act, L, 0, hooks={
                3: lambda: (up_copy(act, q, U.chunks - 1), up_silu(act, q, last)), 4: lambda: up_hi(act, q, last)})
            for n in range(1, 4):
                split_chunk(split_hi, act, L, n)

        def down_dve(dve, chain, q):
            L, U = DOWN[q], UP[q]
            last = U.chunks // 2 - 1
            split_chunk(split_lo, dve, L, 0, hooks={
                3: lambda: (up_conv(dve, chain, q, last), up_mul(dve, q, last)), 4: lambda: up_lo(dve, q, last)})
            for n in range(1, 4):
                split_chunk(split_lo, dve, L, n, hooks={3: lambda: residual(dve, chain, L, n - 1, 4 + 4 * q + n - 1)})

        def down_sp(sp, q):
            L = DOWN[q]
            for n in range(4):
                load_chunk(sp, L, n, n * CHUNK)
                if n == 0:
                    sp.wait_ge(sem("ff_flip0"), ff_pair(q, UP[q].chunks // 2 - 1) + 1)
                    sp.wait_ge(sem("ff_flip1"), ff_pair(q, UP[q].chunks // 2 - 1) + 1)
                gate_load(sp, 4 + 4 * q + n, 5 * D, n)

        final_w = place("final_w_sb", [P, D], at=B0)

        def final_sp(sp):
            chunk_done(sp, DOWN[1], 3)
            sp.dma_start(final_w[:], A["final_w"].rearrange("(a n) -> a n", a=1).to_broadcast([P, D])
                         ).then_inc(sem("norm_w_in"), 16)

        def final_dve(dve, chain):
            wait_rms(dve, "fn")
            chain.done(nc.vector.reciprocal(stat[:, 12:14], stat[:, 12:14]))
            dve.wait_ge(sem("norm_w_in"), 16)
            for t in range(TILES):
                last = nc.vector.scalar_tensor_tensor(X[:, t, :], X[:, t, :], stat[:, 12 + t:13 + t], final_w[:],
                                                      ALU.mult, ALU.mult)
            last.then_inc(sem("x3"), 1)

        CV, AZ, BL, GT, HO = (layers[n] for n in ("conv", "az", "b", "gates", "hout"))
        SI, SO = layers["scin"], layers["scout"]
        dn_w = place("dn_conv", [P, A_QKV // P, 4], at=B0)
        N_RAW = AZ.chunks + BL.chunks
        assert BL.p0 == AZ.p1 and GT.p0 == BL.p1 and CV.p1 == AZ.p0

        def hyb_sp(sp):
            sp.wait_ge(sem("x3"), 1)
            sp.dma_start(dn_w[:], A["dn_conv_w_2"][0].rearrange("(k p) j -> p k j", p=P)).then_inc(sem("conv_w_in"), 16)
            for n in range(2):
                load_chunk(sp, CV, n, n * CHUNK)
            with sp.Fori(1, CV.chunks // 2) as i:
                for h in range(2):
                    load_chunk(sp, CV, h, i * (2 * CHUNK) + h * CHUNK, i=i, step=2 * CV.per)
            for n in range(AZ.chunks):
                load_chunk(sp, AZ, n, OFF_AZ + n * CHUNK)
            with sp.Fori(0, BL.chunks // 2) as i:
                for h in range(2):
                    load_chunk(sp, BL, h, i * (2 * CHUNK) + (OFF_B + h * CHUNK), i=i, step=2 * BL.per)
            load_chunk(sp, GT, 0, OFF_GATES, 2 * DN_V)

        def cv_copy(act, n, i=None):
            chunk_done(act, CV, n, i, 2 * CV.per)
            if n >= 2 or i is not None:
                act.wait_ge(sem(f"cv_stored{n % 2}"), at(16 * (n // 2), i, 16))
            c = CV.c0 + n
            nc.scalar.activation(stg[n % 2][:], ps[:, acc_pair(c):acc_pair(c) + 2, :], ACT.Copy
                                 ).then_inc(sem(f"acc_free{c % 2}"), 1)

        def cv_flip(pe, n, i=None):
            c = CV.c0 + n
            pe.wait_ge(sem(f"acc_free{c % 2}"), at(c // 2 + 1, i, 1))
            if n >= 1 or i is not None:
                pe.wait_ge(sem("cv_conv"), at(n, i, 2))
            for k in range(CT):
                for t in range(TILES):
                    last = nc.tensor.transpose(ps[:, 4 + k // 2, (k % 2) * SEQ + t * P:(k % 2) * SEQ + (t + 1) * P],
                                               stg[n % 2][:, t, k * P:(k + 1) * P], ident[:])
            last.then_inc(sem("cv_flip"), 1)

        def causal_conv(dve, chain, weights, taps):
            src = [ps[:, 4 + k // 2, (k % 2) * SEQ:(k % 2 + 1) * SEQ] for k in range(CT)]
            for back in range(taps):
                for k in range(CT):
                    w = weights(k, taps - 1 - back)
                    if back == 0:
                        last = nc.vector.tensor_scalar(ff[:, k, :], src[k], w, None, ALU.mult)
                    else:
                        last = nc.vector.scalar_tensor_tensor(ff[:, k, back:SEQ], src[k][:, 0:SEQ - back], w,
                                                              ff[:, k, back:SEQ], ALU.mult, ALU.add)
                if back < taps - 1:
                    chain.done(last)
            return last

        def cv_conv(dve, chain, n, i=None):
            dve.wait_ge(sem("cv_flip"), at(n + 1, i, 2))
            if n >= 1 or i is not None:
                dve.wait_ge(sem("cv_back"), at(n, i, 2))
            kt = n * CT if i is None else i * (2 * CT) + n * CT

            def w(k, tap):
                a = kt + k
                return dn_w[:, bass.ds(a, 1), tap]
            causal_conv(dve, chain, w, 4).then_inc(sem("cv_conv"), 1)

        def cv_silu(act, n, i=None):
            act.wait_ge(sem("cv_conv"), at(n + 1, i, 2))
            nc.scalar.activation(ff, ff, ACT.Silu).then_inc(sem("cv_silu"), 1)

        def cv_back(pe, n, i=None):
            pe.wait_ge(sem("cv_silu"), at(n + 1, i, 2))
            if n >= 1 or i is not None:
                pe.wait_ge(sem("cv_out"), at(n, i, 2))
            for t in range(TILES):
                for k in range(CT):
                    last = nc.tensor.transpose(ps[:, 6 + t, k * P:(k + 1) * P], ff[:, k, t * P:(t + 1) * P], ident[:])
            last.then_inc(sem("cv_back"), 1)

        def cv_out(dve, n, i=None):
            dve.wait_ge(sem("cv_back"), at(n + 1, i, 2))
            nc.vector.tensor_copy(stg[n % 2][:], ps[:, 6:8, :]).then_inc(sem("cv_out"), 1)

        def cv_store(act, n, i=None):
            act.wait_ge(sem("cv_out"), at(n + 1, i, 2))
            c0 = n * CHUNK if i is None else i * (2 * CHUNK) + n * CHUNK
            act.dma_start(tok(CONV[:, bass.ds(c0, CHUNK)]), stg[n % 2][:]).then_inc(sem(f"cv_stored{n % 2}"), 16)

        def raw_store(act, m, i=None, w=CHUNK):
            act.wait_ge(sem("piece_used"), at(AZ.p0 + (m + 1) * AZ.per, i, 2 * AZ.per))
            par = m % 2
            if m < 2 and i is None:
                act.wait_ge(sem(f"cv_stored{par}"), 16 * CV.chunks // 2)
            else:
                act.wait_ge(sem(f"raw_stored{par}"), at(16 * (m // 2), i, 16))
            c = AZ.c0 + m
            nc.scalar.activation(stg[par][:, :, 0:w], ps[:, acc_pair(c):acc_pair(c) + 2, 0:w], ACT.Copy
                                 ).then_inc(sem(f"acc_free{c % 2}"), 1)
            c0 = m * CHUNK if i is None else i * (2 * CHUNK) + m * CHUNK
            act.wait_ge(sem(f"acc_free{c % 2}"), at(c // 2 + 1, i, 1))
            act.dma_start(tok(RAW[:, bass.ds(c0, w)]), stg[par][:, :, 0:w]).then_inc(sem(f"raw_stored{par}"), 16)

        def hyb_act(act):
            split_chunk(split_hi, act, CV, 0, skip=3)
            split_chunk(split_hi, act, CV, 1, hooks={3: lambda: cv_copy(act, 0)})
            with act.Fori(1, CV.chunks // 2) as i:
                for h in range(2):
                    first = {2: lambda: cv_silu(act, h - 2, i), 3: lambda: cv_copy(act, h - 1, i),
                             "end": lambda: cv_store(act, h - 2, i)}
                    split_chunk(split_hi, act, CV, h, i=i, step=2 * CV.per, hooks=first)
            n = CV.chunks
            split_chunk(split_hi, act, AZ, 0, hooks={2: lambda: cv_silu(act, n - 2), 3: lambda: cv_copy(act, n - 1),
                                                     "end": lambda: cv_store(act, n - 2)})
            split_chunk(split_hi, act, AZ, 1, hooks={2: lambda: cv_silu(act, n - 1), 3: lambda: cv_store(act, n - 1),
                                                     "end": lambda: raw_store(act, 0)})
            for m in range(2, AZ.chunks):
                split_chunk(split_hi, act, AZ, m, hooks={3: lambda: raw_store(act, m - 1)})
            with act.Fori(0, BL.chunks // 2) as i:
                for h in range(2):
                    split_chunk(split_hi, act, BL, h, i=i, step=2 * BL.per,
                                hooks={3: lambda: raw_store(act, AZ.chunks + h - 1, i)})
            split_chunk(split_hi, act, GT, 0, 2 * DN_V, hooks={3: lambda: raw_store(act, N_RAW - 1)})
            raw_store(act, N_RAW, w=2 * DN_V)

        def hyb_dve(dve, chain):
            split_chunk(split_lo, dve, CV, 0, skip=3)
            dve.wait_ge(sem("conv_w_in"), 32)
            split_chunk(split_lo, dve, CV, 1)
            with dve.Fori(1, CV.chunks // 2) as i:
                chain.begin(i, 1, 6)
                for h in range(2):
                    split_chunk(split_lo, dve, CV, h, i=i, step=2 * CV.per, hooks={
                        1: lambda: cv_conv(dve, chain, h - 2, i), "end": lambda: cv_out(dve, h - 2, i)})
                chain.end(CV.chunks // 2)
            n = CV.chunks
            for m in range(2):
                split_chunk(split_lo, dve, AZ, m, hooks={
                    1: lambda: cv_conv(dve, chain, n - 2 + m), (3 if m else "end"): lambda: cv_out(dve, n - 2 + m)})
            for m in range(2, AZ.chunks):
                split_chunk(split_lo, dve, AZ, m)
            with dve.Fori(0, BL.chunks // 2) as i:
                for h in range(2):
                    split_chunk(split_lo, dve, BL, h, i=i, step=2 * BL.per)
            split_chunk(split_lo, dve, GT, 0, 2 * DN_V)

        def hyb_pe(pe):
            matmul_chunk(pe, CV, 0, CV.c0, [hx])
            matmul_chunk(pe, CV, 1, CV.c0 + 1, [hx], hooks={"end": lambda: cv_flip(pe, 0)})
            with pe.Fori(1, CV.chunks // 2) as i:
                for h in range(2):
                    matmul_chunk(pe, CV, h, CV.c0 + h, [hx], i=i, step=2 * CV.per, cstep=2, hooks={
                        3: lambda: cv_back(pe, h - 2, i), "end": lambda: cv_flip(pe, h - 1, i)})
            n = CV.chunks
            matmul_chunk(pe, AZ, 0, AZ.c0, [hx], hooks={3: lambda: cv_back(pe, n - 2), "end": lambda: cv_flip(pe, n - 1)})
            matmul_chunk(pe, AZ, 1, AZ.c0 + 1, [hx], hooks={3: lambda: cv_back(pe, n - 1)})
            for m in range(2, AZ.chunks):
                matmul_chunk(pe, AZ, m, AZ.c0 + m, [hx])
            with pe.Fori(0, BL.chunks // 2) as i:
                for h in range(2):
                    matmul_chunk(pe, BL, h, BL.c0 + h, [hx], i=i, step=2 * BL.per, cstep=2)
            matmul_chunk(pe, GT, 0, GT.c0, [hx], 2 * DN_V)

        def load_chunk_first(sp, L):
            for g in range(RING):
                load_piece(sp, L, L.p0 + g, *L.groups[g], 0)

        put = region(B0, X0)
        put_s = region(S0, S1)
        NH = DN_V
        qk_all = put("qk_all", [P, TILES, 2 * DN_QK * DN_D])
        g_in = put_s("g_in", [P, TILES, 2 * NH])
        a_log = put_s("a_log", [P, NH])
        dt_b = put_s("dt_b", [P, NH])
        tri = put_s("tri", [P, P])
        ones_half = [put_s(f"ones_half{b}", [P, P]) for b in range(2)]
        tri_t = put_s("tri_t", [P, DN_CHUNK])
        names = ("beta", "z", "az_", "sp", "g", "gc", "gl", "eg", "ekd", "f_qg", "f_kb", "f_kd", "t0", "t1")
        G = {n: put_s("gate_" + n, [P, TILES, NH]) for n in names}
        r_qk = put_s("r_qk", [P, TILES, 2 * DN_QK])
        egl = put_s("egl", [P, 2 * TILES, NH])
        gcT = put_s("gcT", [NH, SEQ])

        def gates_sp(sp):
            n = 16 * (N_RAW // 2)
            sp.wait_ge(sem("raw_stored0"), n + 16)
            sp.wait_ge(sem("raw_stored1"), n)
            for par in range(2):
                sp.wait_ge(sem(f"cv_stored{par}"), 16 * CV.chunks // 2)
            sp.dma_start(qk_all[:], tok(CONV[:, 0:2 * DN_QK * DN_D])).then_inc(sem("qk_all_in"), 16)
            sp.dma_start(g_in[:], tok(RAW[:, W_RAW:])).then_inc(sem("gates_in"), 16)
            sp.dma_start(a_log[:], A["dn_a_log_2"].to_broadcast([P, NH])).then_inc(sem("gates_in"), 16)
            sp.dma_start(dt_b[:], A["dn_dt_bias_2"].to_broadcast([P, NH])).then_inc(sem("gates_in"), 16)
            sp.dma_start(tri[:], A["const_tri"]).then_inc(sem("gates_in"), 16)
            for b in range(2):
                sp.dma_start(ones_half[b][:], A["const_half"][b]).then_inc(sem("gates_in"), 16)
            sp.dma_start(tri_t[:], A["const_tri_t"]).then_inc(sem("gates_in"), 16)

        def gates_act(act):
            act.wait_ge(sem("g_dve"), 1)
            nc.scalar.activation(G["beta"][:], g_in[:, :, 0:NH], ACT.Sigmoid).then_inc(sem("g_act"), 1)
            nc.scalar.activation(G["az_"][:], G["z"][:], ACT.Abs).then_inc(sem("g_act"), 1)
            act.wait_ge(sem("g_act"), 2)
            nc.scalar.activation(G["t0"][:], G["az_"][:], ACT.Exp, scale=-1.0).then_inc(sem("g_act"), 1)
            nc.scalar.activation(a_log[:], a_log[:], ACT.Exp).then_inc(sem("g_act"), 1)
            act.wait_ge(sem("g_act"), 3)
            nc.scalar.activation(G["sp"][:], G["t0"][:], ACT.Ln, bias=1.0).then_inc(sem("g_act"), 1)
            act.wait_ge(sem("g_dve"), 4)
            nc.scalar.activation(G["eg"][:], G["gc"][:], ACT.Exp).then_inc(sem("g_act"), 1)
            nc.scalar.activation(egl[:], egl[:], ACT.Exp).then_inc(sem("g_act"), 1)
            nc.scalar.activation(G["ekd"][:], G["t1"][:], ACT.Exp).then_inc(sem("g_act"), 1)
            act.wait_ge(sem("g_dve"), 2)
            nc.scalar.activation(r_qk[:], r_qk[:], ACT.Sqrt, bias=C["eps"]).then_inc(sem("g_act"), 1)
            act.wait_ge(sem("g_dve"), 5)
            act.dma_start(GROW, gcT[:]).then_inc(sem("grow_stored"), 16)

        def gates_pe(pe):
            pe.wait_ge(sem("g_dve"), 3)
            for t in range(TILES):
                nc.tensor.matmul(ps[:, 4, t * NH:(t + 1) * NH], tri[:], G["g"][:, t, :], start=True, stop=True)
                for b in range(2):
                    last = nc.tensor.matmul(ps[:, 5, (2 * t + b) * NH:(2 * t + b + 1) * NH], ones_half[b][:], G["g"][:, t, :],
                                            start=True, stop=True)
            last.then_inc(sem("g_pe"), 1)
            pe.wait_ge(sem("g_dve"), 4)
            for t in range(TILES):
                last = nc.tensor.transpose(ps[0:NH, 6, t * P:(t + 1) * P], G["gc"][:, t, :], ident[:])
            last.then_inc(sem("g_pe"), 1)

        def gates_dve(dve, chain):
            dve.wait_ge(sem("gates_in"), 16 * 7)
            dt = dt_b[:].unsqueeze(1).to_broadcast([P, TILES, NH])
            nc.vector.tensor_tensor(G["z"][:], g_in[:, :, NH:], dt, ALU.add).then_inc(sem("g_dve"), 1)
            dve.wait_ge(sem("qk_all_in"), 16)
            chain.done(nc.vector.tensor_tensor(qk_all[:], qk_all[:], qk_all[:], ALU.mult))
            nc.vector.reduce_sum(r_qk[:].rearrange("p t h -> p (t h)"),
                                 qk_all[:].rearrange("p t (h d) -> p (t h) d", d=DN_D), AX).then_inc(sem("g_dve"), 1)
            dve.wait_ge(sem("g_act"), 5)
            chain.done(nc.vector.scalar_tensor_tensor(G["sp"][:], G["z"][:], 0.0, G["sp"][:], ALU.max, ALU.add))
            al = a_log[:].unsqueeze(1).to_broadcast([P, TILES, NH])
            chain.done(nc.vector.tensor_tensor(G["g"][:], G["sp"][:], al, ALU.mult))
            nc.vector.tensor_scalar(G["g"][:], G["g"][:], -1.0, None, ALU.mult).then_inc(sem("g_dve"), 1)
            dve.wait_ge(sem("g_pe"), 1)
            nc.vector.tensor_copy(G["gc"][:].rearrange("p t h -> p (t h)"), ps[:, 4, 0:TILES * NH])
            chain.done(nc.vector.tensor_copy(egl[:].rearrange("p n h -> p (n h)"), ps[:, 5, 0:2 * TILES * NH]))
            for b in range(2):
                half = slice(b * DN_CHUNK, (b + 1) * DN_CHUNK)
                last = nc.vector.tensor_tensor(G["t1"][half], egl[half, b::2, :], G["gc"][half], ALU.subtract)
            last.then_inc(sem("g_dve"), 1)
            dve.wait_ge(sem("g_pe"), 2)
            nc.vector.tensor_copy(gcT[:], ps[0:NH, 6, 0:SEQ]).then_inc(sem("g_dve"), 1)
            dve.wait_ge(sem("g_act"), 9)
            chain.done(nc.vector.reciprocal(r_qk[:], r_qk[:]))
            chain.done(nc.vector.tensor_scalar(r_qk[:, :, 0:DN_QK], r_qk[:, :, 0:DN_QK], DN_D ** -0.5, None, ALU.mult))

            def pairs(v):
                return v.rearrange("p t (h v) -> p t h v", v=2)

            def both(v):
                return v.unsqueeze(3).to_broadcast([P, TILES, DN_QK, 2])
            rq, rk = r_qk[:, :, 0:DN_QK], r_qk[:, :, DN_QK:]
            for t in range(TILES):
                def v(n):
                    return pairs(G[n][:])[:, t]
                nc.vector.tensor_tensor(v("f_qg"), v("eg"), both(rq)[:, t], ALU.mult)
                nc.vector.tensor_tensor(v("f_kd"), v("ekd"), both(rk)[:, t], ALU.mult)
                nc.vector.tensor_tensor(v("f_kb"), v("eg"), both(rk)[:, t], ALU.mult)
            chain.done(nc.vector.tensor_copy(G["t0"][:], G["beta"][:]))
            nc.vector.tensor_tensor(G["f_kb"][:], G["f_kb"][:], G["beta"][:], ALU.mult).then_inc(sem("g_dve"), 1)
            dve.wait_ge(sem("g_dve"), 6)

        put = region(B0 + TILES * 2 * DN_QK * DN_D * 4, X0)
        dq = [put(f"dq{i}", [P, 2, TILES, DN_D]) for i in range(2)]
        grow = [put(f"grow{i}", [P, 2, TILES, DN_CHUNK]) for i in range(2)]
        dqkT = [put(f"dqkT{i}", [P, 2, SEQ]) for i in range(2)]
        dd, dmax, dmin, dec, decT = (put(n, [P, 2, TILES, DN_CHUNK]) for n in ("dd", "dmax", "dmin", "dec", "decT"))
        am = [put(f"am{i}", [P, 2, TILES, DN_CHUNK]) for i in range(2)]
        qm = [put(f"qm{i}", [P, 2, TILES, DN_CHUNK]) for i in range(2)]

        def pairs_of_heads(eng, emit, chain=None, per=0):
            emit(0)
            emit(1)
            with eng.Fori(1, 4) as i:
                if chain:
                    chain.begin(i, 1, per)
                emit(0, i)
                emit(1, i)
                if chain:
                    chain.end(4)

        def nth(h, i, unit):
            return h * unit if i is None else i * (2 * unit) + h * unit

        def blk_load(sp, h, i=None):
            par = h % 2
            if i is not None:
                sp.wait_ge(sem("blk_done"), at(h - 1, i, 2))
            for j in range(2):
                sp.dma_start(dq[par][:, j], tok(CONV[:, j * DN_QK * DN_D:][:, bass.ds(nth(h, i, DN_D), DN_D)])
                             ).then_inc(sem(f"blk_in{par}"), 16)
            for b in range(2):
                src = GROW[bass.ds(nth(h, i, 2), 2), :].rearrange("v (t b j) -> b v t j", t=TILES, b=2)[b:b + 1]
                sp.dma_start(grow[par][b * DN_CHUNK:(b + 1) * DN_CHUNK], src.to_broadcast([DN_CHUNK, 2, TILES, DN_CHUNK])
                             ).then_inc(sem(f"blk_in{par}"), 16)

        def head_pair(v, h, i):
            return v[:, :, bass.ds(nth(h, i, 2), 2)].rearrange("p t v -> p v t")

        def blk_scale(pool, h, i=None):
            par = h % 2
            pool.wait_ge(sem(f"blk_in{par}"), at(64 * (h // 2 + 1), i, 64))
            for j in range(2):
                r_ = r_qk[:, :, bass.ds(at(j * DN_QK + h, i, 2), 1)].to_broadcast([P, TILES, DN_D])
                last = nc.gpsimd.tensor_tensor(dq[par][:, j], dq[par][:, j], r_, ALU.mult)
            last.then_inc(sem("blk_scaled"), 1)

        def blk_pe(pe, h, i=None):
            par = h % 2
            pe.wait_ge(sem("blk_scaled"), at(h + 1, i, 2))
            if h >= 1 or i is not None:
                pe.wait_ge(sem("blk_T"), at(h, i, 2))
            for j in range(2):
                for t in range(TILES):
                    last = nc.tensor.transpose(ps[:, 4, (2 * j + t) * P:(2 * j + t + 1) * P], dq[par][:, j, t], ident[:])
            last.then_inc(sem("blk_flip"), 1)
            pe.wait_ge(sem("blk_T"), at(h + 1, i, 2))
            if h >= 1 or i is not None:
                pe.wait_ge(sem("blk_done"), at(h, i, 2))
            for t in range(TILES):
                for b in range(2):
                    c = slice(t * P + b * DN_CHUNK, t * P + (b + 1) * DN_CHUNK)
                    o = slice(b * DN_CHUNK, (b + 1) * DN_CHUNK)
                    f = slice(t * DN_CHUNK, (t + 1) * DN_CHUNK)
                    nc.tensor.matmul(ps[o, 5, f], dqkT[par][:, 1, c], dqkT[par][:, 1, c], start=True, stop=True)
                    last = nc.tensor.matmul(ps[o, 6, f], dqkT[par][:, 1, c], dqkT[par][:, 0, c], start=True, stop=True)
            last.then_inc(sem("blk_prod"), 1)

        def blk_act(act, h, i=None):
            par = h % 2
            act.wait_ge(sem("blk_flip"), at(h + 1, i, 2))
            if i is not None:
                act.wait_ge(sem("blk_prod"), at(h - 1, i, 2))
            nc.scalar.activation(dqkT[par][:].rearrange("p j s -> p (j s)"), ps[:, 4, :], ACT.Copy).then_inc(sem("blk_T"), 1)
            act.wait_ge(sem("blk_diff"), at(h + 1, i, 2))
            nc.scalar.activation(dec[:], dmax[:], ACT.Exp, scale=-1.0)
            nc.scalar.activation(decT[:], dmin[:], ACT.Exp).then_inc(sem("blk_dec"), 1)
            act.wait_ge(sem("blk_done"), at(h + 1, i, 2))
            rows = bass.ds(nth(h, i, 2), 2)
            act.dma_start(AM[rows].rearrange("v t p j -> p v t j"), am[par][:]).then_inc(sem(f"blk_stored{par}"), 16)
            act.dma_start(QM[rows].rearrange("v t p j -> p v t j"), qm[par][:]).then_inc(sem(f"blk_stored{par}"), 16)

        def blk_dve(dve, chain, h, i=None):
            par = h % 2
            shape = [P, 2, TILES, DN_CHUNK]
            dve.wait_ge(sem(f"blk_in{par}"), at(64 * (h // 2 + 1), i, 64))
            gc = head_pair(G["gc"], h, i).unsqueeze(3).to_broadcast(shape)
            chain.done(nc.vector.tensor_tensor(dd[:], grow[par][:], gc, ALU.subtract))
            nc.vector.tensor_scalar(dmax[:], dd[:], 0.0, None, ALU.max)
            nc.vector.tensor_scalar(dmin[:], dd[:], 0.0, None, ALU.min).then_inc(sem("blk_diff"), 1)
            dve.wait_ge(sem("blk_prod"), at(h + 1, i, 2))
            dve.wait_ge(sem("blk_dec"), at(h + 1, i, 2))
            if i is not None:
                dve.wait_ge(sem(f"blk_stored{par}"), at(32 * (h // 2), i, 32))

            def prod(bank):
                return ps[:, bank, 0:P].rearrange("p (t j) -> p t j", t=TILES).unsqueeze(1).to_broadcast(shape)
            mask = tri_t[:].unsqueeze(1).unsqueeze(1).to_broadcast(shape)
            beta = head_pair(G["beta"], h, i).unsqueeze(3).to_broadcast(shape)
            nc.vector.tensor_tensor(am[par][:], prod(5), dec[:], ALU.mult)
            chain.done(nc.vector.tensor_tensor(qm[par][:], prod(6), decT[:], ALU.mult))
            nc.vector.tensor_tensor(am[par][:], am[par][:], beta, ALU.mult)
            nc.vector.tensor_tensor(qm[par][:], qm[par][:], mask, ALU.mult).then_inc(sem("blk_done"), 1)

        put = region(B0, X0)
        a_sys = put("a_sys", [P, DN_CHUNK, DN_CHUNK])
        u_sys = put("u_sys", [P, DN_CHUNK // 2, DN_CHUNK])
        upd = put("upd", [P, 560])

        def solve_sp(sp):
            for par in range(2):
                sp.wait_ge(sem(f"blk_stored{par}"), 32 * 4)
            src = AM.rearrange("h t (b i) j -> (h t b) (i j)", b=2)
            for b in range(2):
                sp.dma_start(a_sys[b * n_sys:(b + 1) * n_sys].rearrange("s i j -> s (i j)"), src).then_inc(sem("a_in"), 16)
            sp.dma_start(u_sys[:], A["const_u"]).then_inc(sem("a_in"), 16)

        def solve_dve(dve, chain):
            dve.wait_ge(sem("a_in"), 48)
            for j in range(DN_CHUNK - 1):
                n_c, n_i = j // 2 + 1, DN_CHUNK - 1 - j
                a = a_sys[:, j + 1:, j].unsqueeze(1).to_broadcast([P, n_c, n_i])
                u = u_sys[:, 0:n_c, j:j + 1].to_broadcast([P, n_c, n_i])
                o = upd[:, 0:n_c * n_i].rearrange("p (c i) -> p c i", c=n_c)
                chain.done(nc.vector.tensor_tensor(o, a, u, ALU.mult))
                chain.done(nc.vector.tensor_tensor(u_sys[:, 0:n_c, j + 1:], u_sys[:, 0:n_c, j + 1:], o, ALU.subtract))
            nc.vector.memset(stat[:, 20:21], 0.0).then_inc(sem("solved"), 1)

        def solve_act(act):
            act.wait_ge(sem("solved"), 1)
            dst = UM.rearrange("h t (s c b) i -> b (h t s) c i", s=2, b=2)
            for b in range(2):
                act.dma_start(dst[b], u_sys[b * n_sys:(b + 1) * n_sys]).then_inc(sem("u_stored"), 16)

        put = region(B0, X0)
        put_a = region(A0 + D * TILES * 4, B0)
        y_b = put_a("y_b", [P, TILES, SW_HEADS * HD])
        sc_q = [put(f"sc_q{i}", [P, 2, TILES, DN_D]) for i in range(2)]
        sc_v = [put(f"sc_v{i}", [P, TILES, 2, DN_D]) for i in range(2)]
        ub = [put(f"ub{i}", [P, 2, TILES, P]) for i in range(2)]
        qb = [put(f"qb{i}", [P, 2, TILES, P]) for i in range(2)]
        q_g, k_b, k_d, v_b = (put(n, [P, 2, TILES, DN_D]) for n in ("q_g", "k_b", "k_d", "v_b"))
        q_gT = put("q_gT", [P, 2, TILES, P])
        wTn = put("wTn", [P, 2, TILES, P])
        st = put("state", [P, 2, DN_D])
        vn = [put(f"vn{b}", [P, 2, DN_D]) for b in range(2)]
        fshape = [P, 2, TILES, DN_D]

        def dl_load(sp, h, i=None):
            par = h % 2
            if i is not None:
                sp.wait_ge(sem("dl_used"), at(h - 1, i, 2))
            for j in range(2):
                sp.dma_start(sc_q[par][:, j], tok(CONV[:, j * DN_QK * DN_D:][:, bass.ds(nth(h, i, DN_D), DN_D)])
                             ).then_inc(sem(f"dl_in{par}"), 16)
            sp.dma_start(sc_v[par][:].rearrange("p t v d -> p t (v d)"),
                         tok(CONV[:, 2 * DN_QK * DN_D:][:, bass.ds(nth(h, i, 2 * DN_D), 2 * DN_D)])
                         ).then_inc(sem(f"dl_in{par}"), 16)
            for dst, m in ((ub[par], UM), (qb[par], QM)):
                for b in range(2):
                    half = slice(b * DN_CHUNK, (b + 1) * DN_CHUNK)
                    sp.dma_start(dst[half, :, :, half],
                                 m[bass.ds(nth(h, i, 2), 2), :, half, :].rearrange("v t p j -> p v t j")
                                 ).then_inc(sem(f"dl_in{par}"), 16)

        def delta_sp(sp):
            sp.wait_ge(sem("u_stored"), 32)
            sp.wait_ge(sem("dl_zero"), 1)
            pairs_of_heads(sp, lambda h, i=None: dl_load(sp, h, i))

        def dl_pool(pool, h, i=None):
            par = h % 2
            pool.wait_ge(sem(f"dl_in{par}"), at(16 * 7 * (h // 2 + 1), i, 16 * 7))
            if h >= 1 or i is not None:
                pool.wait_ge(sem("dl_used"), at(h, i, 2))

            def f(n):
                return head_pair(G[n], h, i).unsqueeze(3).to_broadcast(fshape)
            q_, k_ = (sc_q[par][:, j].unsqueeze(1).to_broadcast(fshape) for j in range(2))
            nc.gpsimd.tensor_tensor(k_b[:], k_, f("f_kb"), ALU.mult)
            nc.gpsimd.tensor_tensor(q_g[:], q_, f("f_qg"), ALU.mult)
            nc.gpsimd.tensor_tensor(v_b[:], sc_v[par][:].rearrange("p t v d -> p v t d"), f("beta"), ALU.mult)
            nc.gpsimd.tensor_tensor(k_d[:], k_, f("f_kd"), ALU.mult).then_inc(sem("dl_scaled"), 1)

        def dl_pe(pe, h, i=None):
            par = h % 2
            n0 = 2 * TILES
            pe.wait_ge(sem("dl_scaled"), at(h + 1, i, 2))
            if h >= 1 or i is not None:
                pe.wait_ge(sem("dl_T"), at(h, i, 2))
            for v in range(2):
                for t in range(TILES):
                    c = slice((2 * v + t) * P, (2 * v + t + 1) * P)
                    nc.tensor.transpose(ps[:, 4, c], q_g[:, v, t], ident[:])
                    last = nc.tensor.matmul(ps[:, 5, c], k_b[:, v, t], ub[par][:, v, t], start=True, stop=True)
            last.then_inc(sem("dl_flip"), 1)
            for n in range(n0):
                t, b = n // 2, n % 2
                B3 = (6, 7, 0) if n % 2 == 0 else (1, 2, 3)
                if n == 0:
                    pe.wait_ge(sem("dl_T"), at(h + 1, i, 2))
                for v in range(2):
                    o = ps[:, B3[0], v * P:(v + 1) * P]
                    nc_last = nc.tensor.matmul(o, ub[par][:, v, t], v_b[:, v, t], start=True, stop=n == 0)
                    if n:
                        if v == 0:
                            pe.wait_ge(sem("dl_state"), at(n0 * h + n, i, 2 * n0))
                        nc_last = nc.tensor.matmul(o, wTn[:, v, t], st[:, v], start=False, stop=True)
                nc_last.then_inc(sem("dl_new"), 1)
                if n >= 2 or h >= 1 or i is not None:
                    pe.wait_ge(sem("dl_out"), at(n0 * h + n - 1, i, 2 * n0))
                pe.wait_ge(sem("dl_vn"), at(n0 * h + n + 1, i, 2 * n0))
                for v in range(2):
                    up = nc.tensor.matmul(ps[:, B3[2], v * P:(v + 1) * P], k_d[:, v, t], vn[b][:, v], start=True, stop=True)
                up.then_inc(sem("dl_up"), 1)
                for v in range(2):
                    o = ps[:, B3[1], v * P:(v + 1) * P]
                    if n:
                        nc.tensor.matmul(o, q_gT[:, v, t], st[:, v], start=True, stop=False)
                    last = nc.tensor.matmul(o, qb[par][:, v, t], vn[b][:, v], start=n == 0, stop=True)
                last.then_inc(sem("dl_o"), 1)

        def dl_act(act, h, i=None):
            n0 = 2 * TILES
            act.wait_ge(sem("dl_flip"), at(h + 1, i, 2))
            if h >= 1 or i is not None:
                act.wait_ge(sem("dl_o"), at(n0 * h, i, 2 * n0))
            nc.scalar.activation(q_gT[:].rearrange("p v t s -> p (v t s)"), ps[:, 4, :], ACT.Copy)
            nc.scalar.activation(wTn[:].rearrange("p v t s -> p (v t s)"), ps[:, 5, :], ACT.Copy, scale=-1.0
                                 ).then_inc(sem("dl_T"), 1)
            for n in range(n0):
                t, b = n // 2, n % 2
                half = slice(b * DN_CHUNK, (b + 1) * DN_CHUNK)
                bank = 7 if n % 2 == 0 else 2
                act.wait_ge(sem("dl_o"), at(n0 * h + n + 1, i, 2 * n0))
                nc.scalar.activation(o_all[half, t, bass.ds(nth(h, i, 2 * DN_D), 2 * DN_D)], ps[half, bank, 0:2 * DN_D],
                                     ACT.Copy).then_inc(sem("dl_out"), 1)
            nc.scalar.activation(stat[:, 21:22], stat[:, 20:21], ACT.Copy).then_inc(sem("dl_used"), 1)

        def dl_dve(dve, h, i=None):
            n0 = 2 * TILES
            for n in range(n0):
                t, b = n // 2, n % 2
                half = slice(b * DN_CHUNK, (b + 1) * DN_CHUNK)
                B3 = (6, 7, 0) if n % 2 == 0 else (1, 2, 3)
                dve.wait_ge(sem("dl_new"), at(n0 * h + n + 1, i, 2 * n0))
                if n >= 2 or h >= 1 or i is not None:
                    dve.wait_ge(sem("dl_o"), at(n0 * h + n - 1, i, 2 * n0))
                nc.vector.tensor_copy(vn[b][half].rearrange("p v d -> p (v d)"), ps[half, B3[0], 0:2 * DN_D]
                                      ).then_inc(sem("dl_vn"), 1)
                dve.wait_ge(sem("dl_up"), at(n0 * h + n + 1, i, 2 * n0))
                if n:
                    dve.wait_ge(sem("dl_o"), at(n0 * h + n + 1, i, 2 * n0))
                elif h >= 1 or i is not None:
                    dve.wait_ge(sem("dl_o"), at(n0 * h, i, 2 * n0))
                for v in range(2):
                    u = ps[:, B3[2], v * P:(v + 1) * P]
                    if n == 0:
                        last = nc.vector.tensor_copy(st[:, v], u)
                    else:
                        decay = egl[:, n, bass.ds(at(2 * h + v, i, 4), 1)]
                        last = nc.vector.scalar_tensor_tensor(st[:, v], st[:, v], decay, u, ALU.mult, ALU.add)
                last.then_inc(sem("dl_state"), 1)

        z_a = place("z_a", [P, TILES, D], at=B0)
        sq_a = place("sq_a", [P, TILES, D], at=B0 + TILES * D * 4)
        ss_a = place("ss_a", [P, TILES * NH], at=B0 + 2 * TILES * D * 4)
        z_b = place("z_b", [P, TILES, SW_HEADS * HD], at=B0 + 2 * TILES * D * 4 + 256)

        def out_sp(sp):
            sp.wait_ge(sem("sw_o"), 4 * 4)
            sp.dma_start(z_a[:], tok(RAW[:, 0:D])).then_inc(sem("z_in"), 16)
            sp.dma_start(z_b[:], tok(RAW[:, W_RAW - SW_HEADS * HD:W_RAW])).then_inc(sem("z_in"), 16)

        def out_act(act):
            act.wait_ge(sem("z_in"), 32)
            nc.scalar.activation(z_a[:], z_a[:], ACT.Silu)
            nc.scalar.activation(z_b[:], z_b[:], ACT.Silu).then_inc(sem("z_silu"), 1)
            act.wait_ge(sem("oa_ss"), 1)
            nc.scalar.activation(ss_a[:], ss_a[:], ACT.Sqrt, bias=C["eps"], scale=1.0 / DN_D).then_inc(sem("oa_rms"), 1)

        def out_dve(dve, chain):
            dve.wait_ge(sem("z_in"), 32)
            dve.wait_ge(sem("dl_out"), 4 * DN_QK)
            chain.done(nc.vector.tensor_tensor(sq_a[:], o_all[:], o_all[:], ALU.mult))
            nc.vector.reduce_sum(ss_a[:], sq_a[:].rearrange("p t (h d) -> p (t h) d", d=DN_D), AX).then_inc(sem("oa_ss"), 1)
            dve.wait_ge(sem("z_silu"), 1)
            nc.vector.tensor_tensor(z_a[:], z_a[:], o_all[:], ALU.mult)
            chain.done(nc.vector.tensor_tensor(y_b[:], y_b[:], z_b[:], ALU.mult))
            dve.wait_ge(sem("oa_rms"), 1)
            chain.done(nc.vector.reciprocal(ss_a[:], ss_a[:]))
            v = z_a[:].rearrange("p t (h d) -> p (t h) d", d=DN_D)
            nc.vector.tensor_tensor(o_all[:].rearrange("p t (h d) -> p (t h) d", d=DN_D), v,
                                    ss_a[:].unsqueeze(2).to_broadcast([P, TILES * NH, DN_D]), ALU.mult
                                    ).then_inc(sem("y_ready"), 1)
            dve.wait_ge(sem("y_ready"), 1)

        put = region(B0, X0)
        KEYS = SEQ
        WQ = SW_GROUPS * SEQ
        sq_in = [put(f"sw_q{i}", [P, TILES, SW_GROUPS, HD]) for i in range(2)]
        sk_in = [put(f"sw_k{i}", [P, TILES, HD]) for i in range(2)]
        sv_in = [put(f"sw_v{i}", [P, TILES, HD]) for i in range(2)]
        sqkT = [put(f"sw_T{i}", [P, 2 * CHUNK]) for i in range(2)]
        sw_mask = put("sw_mask", [P, TILES, WQ])
        sw_s = [put(f"sw_s{i}", [P, WQ]) for i in range(2)]
        sw_pT = [put(f"sw_pT{i}", [P, TILES, P]) for i in range(2)]
        put_s2 = region(S0, S1)
        RD = 32
        sw_c = put_s2("sw_c", [P, TILES, RD])
        sw_n = put_s2("sw_n", [P, TILES, RD])
        sw_m0 = put_s2("sw_m0", [P, TILES, SW_GROUPS + 1, RD])
        sw_m1 = put_s2("sw_m1", [P, TILES, SW_GROUPS + 1, RD])
        smx = [put_s2(f"smx{i}", [P, 8]) for i in range(2)]

        def sw_load(sp, h, i=None):
            par = h % 2
            if i is not None:
                sp.wait_ge(sem("sw_pv"), at(2 * (h - 1), i, 4))
            for g in range(SW_GROUPS):
                c0 = D + g * SW_HEADS * HD
                sp.dma_start(sq_in[par][:, :, g], tok(RAW[:, c0:][:, bass.ds(nth(h, i, HD), HD)])
                             ).then_inc(sem(f"sw_in{par}"), 16)
            for dst, c0 in ((sk_in, D + W_BQ), (sv_in, D + W_BQ + SW_HEADS * HD)):
                sp.dma_start(dst[par][:], tok(RAW[:, c0:][:, bass.ds(nth(h, i, HD), HD)])).then_inc(sem(f"sw_in{par}"), 16)

        def sw_sp(sp):
            sp.wait_ge(sem("dl_out"), 4 * DN_QK)
            sp.wait_ge(sem("dl_used"), DN_QK)
            sp.wait_ge(sem("dl_state"), 4 * DN_QK)
            sp.dma_start(sw_mask[:], A["const_sw_mask"]).then_inc(sem("sw_tab"), 16)
            sp.dma_start(sw_c[:], tok(A["const_sw_c"])).then_inc(sem("sw_tab"), 16)
            sp.dma_start(sw_n[:], tok(A["const_sw_s"])).then_inc(sem("sw_tab"), 16)
            pairs_of_heads(sp, lambda h, i=None: sw_load(sp, h, i))

        def sw_rope(pool, chain, h, i=None):
            par = h % 2
            pool.wait_ge(sem(f"sw_in{par}"), at(80 * (h // 2 + 1), i, 80))
            if h >= 1 or i is not None:
                pool.wait_ge(sem("sw_roped"), at(h, i, 2))
            f = RD // 2
            for t in range(TILES):
                q_, k_ = sq_in[par][:, t, :, 0:RD], sk_in[par][:, t, 0:RD]
                cq = sw_c[:, t, :].unsqueeze(1).to_broadcast([P, SW_GROUPS, RD])
                nc.gpsimd.tensor_tensor(sw_m0[:, t, 0:SW_GROUPS], q_, cq, ALU.mult)
                nc.gpsimd.tensor_tensor(sw_m0[:, t, SW_GROUPS], k_, sw_c[:, t, :], ALU.mult)
                for j in range(2):
                    a, b = slice(j * f, (j + 1) * f), slice((1 - j) * f, (2 - j) * f)
                    sn = sw_n[:, t, a].unsqueeze(1).to_broadcast([P, SW_GROUPS, f])
                    nc.gpsimd.tensor_tensor(sw_m1[:, t, 0:SW_GROUPS, a], q_[:, :, b], sn, ALU.mult)
                    last = nc.gpsimd.tensor_tensor(sw_m1[:, t, SW_GROUPS, a], k_[:, b], sw_n[:, t, a], ALU.mult)
            chain.done(last)
            for t in range(TILES):
                nc.gpsimd.tensor_tensor(sq_in[par][:, t, :, 0:RD], sw_m0[:, t, 0:SW_GROUPS], sw_m1[:, t, 0:SW_GROUPS], ALU.add)
                last = nc.gpsimd.tensor_tensor(sk_in[par][:, t, 0:RD], sw_m0[:, t, SW_GROUPS], sw_m1[:, t, SW_GROUPS], ALU.add)
            last.then_inc(sem("sw_roped"), 1)

        def sw_flip(pe, h, i=None):
            par = h % 2
            pe.wait_ge(sem("sw_roped"), at(h + 1, i, 2))
            if h >= 1 or i is not None:
                pe.wait_ge(sem("sw_T"), at(h, i, 2))
            for g in range(SW_GROUPS):
                for t in range(TILES):
                    nc.tensor.transpose(ps[:, 4 + g // 2, (g % 2) * SEQ + t * P:(g % 2) * SEQ + (t + 1) * P],
                                        sq_in[par][:, t, g], ident[:])
            for t in range(TILES):
                last = nc.tensor.transpose(ps[:, 5, SEQ + t * P:SEQ + (t + 1) * P], sk_in[par][:, t], ident[:])
            last.then_inc(sem("sw_flip"), 1)

        def sw_scores(pe, h, t, i=None):
            par, u = h % 2, 2 * h + t
            pe.wait_ge(sem("sw_T"), at(h + 1, i, 2))
            if u >= 2 or i is not None:
                pe.wait_ge(sem("sw_masked"), at(u - 1, i, 4))
            kT_ = sqkT[par][:, SW_GROUPS * SEQ:]
            for g in range(SW_GROUPS):
                last = nc.tensor.matmul(ps[:, 2 * t + g // 2, (g % 2) * SEQ:(g % 2 + 1) * SEQ],
                                        sqkT[par][:, g * SEQ + t * P:g * SEQ + (t + 1) * P], kT_, start=True, stop=True)
            last.then_inc(sem("sw_sc"), 1)

        def sw_pv(pe, u, i=None):
            par = (u // 2) % 2
            pe.wait_ge(sem("sw_w"), at(u + 1, i, 4))
            if u >= 1 or i is not None:
                pe.wait_ge(sem("sw_wT"), at(u, i, 4))
            for t in range(TILES):
                last = nc.tensor.transpose(ps[:, 6, t * P:(t + 1) * P], sw_s[u % 2][:, t * P:(t + 1) * P], ident[:])
            last.then_inc(sem("sw_wflip"), 1)
            pe.wait_ge(sem("sw_wT"), at(u + 1, i, 4))
            if u >= 1 or i is not None:
                pe.wait_ge(sem("sw_o"), at(u, i, 4))
            for t in range(TILES):
                last = nc.tensor.matmul(ps[:, 7, 0:HD], sw_pT[u % 2][:, t], sv_in[par][:, t], start=t == 0, stop=t == TILES - 1)
            last.then_inc(sem("sw_pv"), 1)

        def sw_pe(pe):
            def head(h, i=None):
                sw_flip(pe, h, i)
                sw_scores(pe, h, 0, i)
                if h >= 1 or i is not None:
                    sw_pv(pe, 2 * h - 1, i)
                sw_scores(pe, h, 1, i)
                sw_pv(pe, 2 * h, i)
            pairs_of_heads(pe, head)
            sw_pv(pe, 2 * SW_HEADS - 1)

        def sw_act(act):
            def sT(h, i=None):
                act.wait_ge(sem("sw_flip"), at(h + 1, i, 2))
                if i is not None:
                    act.wait_ge(sem("sw_sc"), at(2 * (h - 1), i, 4))
                nc.scalar.activation(sqkT[h % 2][:], ps[:, 4:6, :].rearrange("p a n -> p (a n)"), ACT.Copy
                                     ).then_inc(sem("sw_T"), 1)

            def ex_(u, i=None):
                act.wait_ge(sem("sw_max"), at(u + 1, i, 4))
                nc.scalar.activation(sw_s[u % 2][:], sw_s[u % 2][:], ACT.Exp, bias=smx[u % 2][:, 1:2], scale=SW_SCALE,
                                     accum_out=smx[u % 2][:, 2:3]).then_inc(sem("sw_exp"), 1)

            def pT(u, i=None):
                act.wait_ge(sem("sw_wflip"), at(u + 1, i, 4))
                if u >= 2 or i is not None:
                    act.wait_ge(sem("sw_pv"), at(u - 1, i, 4))
                nc.scalar.activation(sw_pT[u % 2][:].rearrange("p k q -> p (k q)"), ps[:, 6, 0:SEQ], ACT.Copy
                                     ).then_inc(sem("sw_wT"), 1)

            def head(h, i=None):
                sT(h, i)
                if h >= 1 or i is not None:
                    pT(2 * h - 1, i)
                ex_(2 * h, i)
                pT(2 * h, i)
                ex_(2 * h + 1, i)
            pairs_of_heads(act, head)
            pT(2 * SW_HEADS - 1)

        def sw_dve(dve, chain):
            def scores(u, i=None):
                par = u % 2
                dve.wait_ge(sem("sw_sc"), at(u + 1, i, 4))
                if u >= 2 or i is not None:
                    dve.wait_ge(sem("sw_wflip"), at(u - 1, i, 4))
                nc.vector.tensor_tensor(sw_s[par][:], ps[:, 2 * par:2 * par + 2, :].rearrange("p a n -> p (a n)")[:, 0:WQ],
                                        sw_mask[:, par, :], ALU.add).then_inc(sem("sw_masked"), 1)
                dve.wait_ge(sem("sw_masked"), at(u + 1, i, 4))
                chain.done(nc.vector.reduce_max(smx[par][:, 0:1], sw_s[par][:], AX))
                nc.vector.tensor_scalar(smx[par][:, 1:2], smx[par][:, 0:1], -SW_SCALE, None, ALU.mult).then_inc(sem("sw_max"), 1)

            def weights(u, i=None):
                s_ = sw_s[u % 2]
                dve.wait_ge(sem("sw_exp"), at(u + 1, i, 4))
                nc.vector.reciprocal(smx[u % 2][:, 3:4], smx[u % 2][:, 2:3])
                chain.done(nc.vector.tensor_tensor(s_[:, 0:SEQ], s_[:, 0:SEQ], s_[:, SEQ:2 * SEQ], ALU.add))
                nc.vector.tensor_tensor(s_[:, 0:SEQ], s_[:, 0:SEQ], s_[:, 2 * SEQ:3 * SEQ], ALU.add).then_inc(sem("sw_w"), 1)

            def output(u, i=None):
                h, t = u // 2, u % 2
                dve.wait_ge(sem("sw_pv"), at(u + 1, i, 4))
                nc.vector.tensor_scalar(y_b[:, t, bass.ds(nth(h, i, HD), HD)], ps[:, 7, 0:HD], smx[t][:, 3:4], None,
                                        ALU.mult).then_inc(sem("sw_o"), 1)

            def head(h, i=None):
                scores(2 * h, i)
                if h >= 1 or i is not None:
                    output(2 * h - 1, i)
                weights(2 * h, i)
                scores(2 * h + 1, i)
                output(2 * h, i)
                weights(2 * h + 1, i)
            dve.wait_ge(sem("sw_tab"), 48)
            pairs_of_heads(dve, head, chain, 8)
            output(2 * SW_HEADS - 1)

        def plain_residual(dve, L, n):
            c = L.c0 + n
            chunk_done(dve, L, n)
            cols = slice(n * CHUNK, (n + 1) * CHUNK)
            nc.vector.tensor_tensor(X[:, :, cols], X[:, :, cols], ps[:, acc_pair(c):acc_pair(c) + 2, :], ALU.add
                                    ).then_inc(sem(f"acc_free{c % 2}"), 1)

        def plain_pe(pe, L, skip_wait=None):
            for n in range(4):
                matmul_chunk(pe, L, n, L.c0 + n, [mix], hooks=skip_wait if n == 0 and skip_wait else {})

        def plain_sp(sp, L, skip=0):
            for n in range(4):
                load_chunk(sp, L, n, n * CHUNK, skip=skip if n == 0 else 0)

        def plain_act(act, L, skip, hooks={}):
            for n in range(4):
                split_chunk(split_hi, act, L, n, skip=skip if n == 0 else 0, hooks=hooks if n == 0 else {})

        def plain_dve(dve, L, skip, hooks={}):
            for n in range(4):
                split_chunk(split_lo, dve, L, n, skip=skip if n == 0 else 0,
                            hooks={3: lambda: plain_residual(dve, L, n - 1)} if n else hooks)
            plain_residual(dve, L, 3)

        sc_w = place("sc_conv", [P, SC_KT, 3])
        SB = 4 * SI.per

        def sc_acc(n):
            a = acc_pair(SI.c0 + n)
            return ps[:, a:a + 2, :]

        def sc_freed(n):
            return sem(f"acc_free{(SI.c0 + n) % 2}")

        def sc_sp(sp):
            order = (SC_W, 2 * SC_W, 0, 3 * SC_W)
            for n, c0 in enumerate(order):
                load_chunk(sp, SI, n, c0)
            with sp.Fori(0, SC_W // CHUNK - 1) as i:
                for n, c0 in enumerate(order):
                    load_chunk(sp, SI, n + 4, i * CHUNK + (CHUNK + c0), i=i, step=SB)

        def sc_c(act, i=None):
            chunk_done(act, SI, 0, i, SB)
            if i is not None:
                act.wait_ge(sem("sc_flip"), i)
            nc.scalar.activation(stg[0][:], sc_acc(0), ACT.Copy).then_inc(sc_freed(0), 1)

        def sc_u(dve, i=None):
            chunk_done(dve, SI, 1, i, SB)
            dve.wait_ge(sc_freed(0), at(SI.c0 // 2 + 1, i, 2))
            nc.vector.tensor_tensor(stg[0][:], stg[0][:], sc_acc(1), ALU.mult).then_inc(sc_freed(1), 1)

        def sc_b(act, i=None):
            chunk_done(act, SI, 2, i, SB)
            if i is not None:
                act.wait_ge(sem("sc_flip"), i)
            nc.scalar.activation(stg[1][:], sc_acc(2), ACT.Copy).then_inc(sc_freed(2), 1)

        def sc_z(act, i):
            act.wait_ge(sem("piece_used"), at(SI.p0, i, SB))
            nc.scalar.activation(tmp[:], sc_acc(3), ACT.Silu).then_inc(sc_freed(3), 1)

        def sc_bz(dve, i):
            dve.wait_ge(sc_freed(3), i * 2 + ((SI.c0 + 3) // 2 - 1))
            nc.vector.tensor_tensor(stg[1][:], stg[1][:], tmp[:], ALU.mult).then_inc(sem("sc_bz"), 1)

        def sc_flip(pe, i, first=False):
            pe.wait_ge(sem("sc_bz"), i)
            if not first:
                pe.wait_ge(sem("sc_mul"), i - 1)
            for j in range(2):
                for k in range(CT):
                    for t in range(TILES):
                        last = nc.tensor.transpose(
                            ps[:, 4 + 2 * j + k // 2, (k % 2) * SEQ + t * P:(k % 2) * SEQ + (t + 1) * P],
                            stg[j][:, t, k * P:(k + 1) * P], ident[:])
            last.then_inc(sem("sc_flip"), 1)

        def sc_conv(dve, chain, i):
            dve.wait_ge(sem("sc_flip"), i)

            def w(k, tap):
                a = i * CT + (k - CT)
                return sc_w[:, bass.ds(a, 1), tap]
            chain.done(causal_conv(dve, chain, w, 3))
            nc.vector.tensor_tensor(tmp[:], tmp[:], ps[:, 6:8, :], ALU.mult).then_inc(sem("sc_mul"), 1)

        def sc_hi(act, i):
            act.wait_ge(sem("sc_mul"), i)
            nc.scalar.activation(b_hi[:, bass.ds(i * CT - CT, CT), :], ff, ACT.Copy).then_inc(sem("sc_hi"), 1)

        def sc_lo(dve, i):
            dve.wait_ge(sem("sc_hi"), i)
            nc.vector.tensor_tensor(b_lo[:, bass.ds(i * CT - CT, CT), :], ff, b_hi[:, bass.ds(i * CT - CT, CT), :].bitcast(F32),
                                    ALU.subtract).then_inc(sem("sc_lo"), 1)

        N_SC = SC_W // CHUNK

        def sc_act(act):
            def turn(i, first_skip=0):
                kw = dict(i=i, step=SB)
                split_chunk(split_hi, act, SI, 0, skip=first_skip, hooks={} if i is None else {3: lambda: sc_z(act, i)}, **kw)
                split_chunk(split_hi, act, SI, 1, hooks={3: lambda: sc_c(act, i)}, **kw)
                split_chunk(split_hi, act, SI, 2, hooks={} if i is None else {1: lambda: sc_hi(act, i)}, **kw)
                split_chunk(split_hi, act, SI, 3, hooks={3: lambda: sc_b(act, i)}, **kw)
            turn(None, 3)
            with act.Fori(1, N_SC) as i:
                turn(i)

        def sc_dve(dve, chain):
            def turn(i, first_skip=0):
                kw = dict(i=i, step=SB)
                split_chunk(split_lo, dve, SI, 0, skip=first_skip, hooks={} if i is None else {"end": lambda: sc_bz(dve, i)}, **kw)
                split_chunk(split_lo, dve, SI, 1, hooks={} if i is None else {3: lambda: sc_conv(dve, chain, i)}, **kw)
                h = {3: lambda: sc_u(dve, i)}
                if i is not None:
                    h[2] = lambda: sc_lo(dve, i)
                split_chunk(split_lo, dve, SI, 2, hooks=h, **kw)
                split_chunk(split_lo, dve, SI, 3, **kw)
            turn(None, 3)
            with dve.Fori(1, N_SC) as i:
                chain.begin(i, 1, 3)
                turn(i)
                chain.end(N_SC)

        def sc_pe(pe):
            def turn(i):
                kw = dict(i=i, step=SB, cstep=4)
                for n in range(4):
                    h = {1: lambda: sc_flip(pe, i)} if n == 1 and i is not None else {}
                    matmul_chunk(pe, SI, n, SI.c0 + n, [hx], hooks=h, **kw)
            turn(None)
            with pe.Fori(1, 2) as i:
                kw = dict(i=i, step=SB, cstep=4)
                for n in range(4):
                    h = {1: lambda: sc_flip(pe, i, True)} if n == 1 else {}
                    matmul_chunk(pe, SI, n, SI.c0 + n, [hx], hooks=h, **kw)
            with pe.Fori(2, N_SC) as i:
                turn(i)

        def sc_last_pe(pe):
            sc_flip(pe, N_SC)

            def own_inputs():
                pe.wait_ge(sem("sc_lo"), N_SC)
            pe.wait_ge(sem("sc_lo"), N_SC - 1)
            first = next(g for g, (kt, n) in enumerate(SO.groups) if kt + n > (N_SC - 1) * CT)
            plain_pe(pe, SO, {first: own_inputs})

        put = region(A0, B0)
        w_last = put("w_last", [P, D])
        y_out = put("y_out", [P, TILES, D])

        def last_sp(sp):
            chunk_done(sp, SI, SI.chunks - 1)
            sp.dma_start(w_last[:], A["final_norm_w_2"].rearrange("(a n) -> a n", a=1).to_broadcast([P, D])
                         ).then_inc(sem("norm_w_in"), 16)
            for t in range(TILES):
                sp.wait_ge(sem("y_out"), t + 1)
                sp.dma_start(out[t * P:(t + 1) * P, :], y_out[:, t, :]).then_inc(sem("out_stored"), 16)
            sp.wait_ge(sem("out_stored"), 16 * TILES)

        def last_dve(dve, chain):
            wait_rms(dve, "ln")
            chain.done(nc.vector.reciprocal(stat[:, 18:20], stat[:, 18:20]))
            dve.wait_ge(sem("norm_w_in"), 32)
            for t in range(TILES):
                nc.vector.scalar_tensor_tensor(y_out[:, t, :], X[:, t, :], stat[:, 18 + t:19 + t], w_last[:],
                                               ALU.mult, ALU.mult).then_inc(sem("y_out"), 1)

        x_tiles = [X[:, t, :] for t in range(TILES)]
        x_at = lambda kt, t: X[:, t, kt * P:(kt + 1) * P]

        block = ctx.enter_context(nc.Block())

        @block.sync
        def _(sp):
            ada_sp(sp)
            cols_sp(sp)
            proj_sp(sp)
            lat_sp(sp)
            att_sp(sp)
            wo_sp(sp)
            up_load(sp, 0)
            down_sp(sp, 0)
            up_load(sp, 1)
            down_sp(sp, 1)
            final_sp(sp)
            sp.dma_start(sc_w[:], A["sc_conv_w_2"][0].rearrange("(k p) j -> p k j", p=P)).then_inc(sem("conv_w_in"), 16)
            hyb_sp(sp)
            gates_sp(sp)
            load_chunk_first(sp, HO)
            sp.wait_ge(sem("grow_stored"), 16)
            sp.wait_ge(sem("g_dve"), 2)
            pairs_of_heads(sp, lambda h, i=None: blk_load(sp, h, i))
            solve_sp(sp)
            delta_sp(sp)
            sw_sp(sp)
            out_sp(sp)
            plain_sp(sp, HO, RING)
            sc_sp(sp)
            plain_sp(sp, SO)
            last_sp(sp)

        @block.gpsimd
        def _(pool):
            chain = Count(pool, sem("pool_chain"))
            att_pool(pool, chain)
            pool.wait_ge(sem("g_dve"), 6)
            pairs_of_heads(pool, lambda h, i=None: blk_scale(pool, h, i))
            pairs_of_heads(pool, lambda h, i=None: dl_pool(pool, h, i))
            pool.wait_ge(sem("sw_tab"), 48)

            def swr(h, i=None):
                sw_rope(pool, chain, h, i)
            swr(0)
            swr(1)
            with pool.Fori(1, 4) as i:
                chain.begin(i, 1, 2)
                swr(0, i)
                swr(1, i)
                chain.end(4)

        @block.scalar
        def _(act):
            ada_act(act)
            presplit(split_hi, act, KV)
            act.wait_ge(sem("x_in"), 16)
            act.wait_ge(sem("cols"), 1)
            norm_stats_act(act, "n1", [X[:, t, :] for t in range(TILES)], D, 0)
            flip_act(act, "n1", KT // 2, a_hi)
            act.wait_ge(sem("ctx_in"), 32)
            norm_stats_act(act, "n1c", [ctx_in[t][:] for t in range(TILES)], D, 2)
            flip_act(act, "n1c", KT // 2, b_hi)
            proj_stream(act, split_hi, store_act)
            lat_act(act)
            att_act(act)
            presplit(split_hi, act, WO)
            flip_act(act, "mix", KT // 2, b_hi)
            wo_act(act)
            presplit(split_hi, act, UP[0])
            x_ready(act, WO)
            norm_stats_act(act, "n2", [X[:, t, :] for t in range(TILES)], D, 10)
            flip_act(act, "n2", KT // 2, a_hi)
            up_act(act, 0, 3)
            down_act(act, 0)
            up_act(act, 1, 0)
            down_act(act, 1)
            x_ready(act, DOWN[1])
            norm_stats_act(act, "fn", x_tiles, D, 12)
            presplit(split_hi, act, CV)
            act.wait_ge(sem("x3"), 1)
            norm_stats_act(act, "n3", x_tiles, D, 14)
            flip_act(act, "n3", KT // 2, a_hi)
            hyb_act(act)
            gates_act(act)
            pairs_of_heads(act, lambda h, i=None: blk_act(act, h, i))
            solve_act(act)
            pairs_of_heads(act, lambda h, i=None: dl_act(act, h, i))
            sw_act(act)
            out_act(act)
            presplit(split_hi, act, HO)
            flip_act(act, "mix2", MIX_KT // 2, b_hi)
            plain_act(act, HO, 3)
            presplit(split_hi, act, SI)
            x_ready(act, HO)
            norm_stats_act(act, "n4", x_tiles, D, 16)
            flip_act(act, "n4", KT // 2, a_hi)
            sc_act(act)
            plain_act(act, SO, 0, {3: lambda: sc_z(act, N_SC), 4: lambda: sc_hi(act, N_SC)})
            x_ready(act, SO)
            norm_stats_act(act, "ln", x_tiles, D, 18)

        @block.vector
        def _(dve):
            chain = Count(dve, sem("dve_chain"))
            ada_dve(dve, chain)
            presplit(split_lo, dve, KV)
            cols_dve(dve, chain)
            norm_diag_dve(dve, "n1", TILES, 0, chain)
            flip_dve(dve, "n1", KT // 2, c_of("m1"), c_of("sh1"), a_hi, a_lo)
            norm_diag_dve(dve, "n1c", TILES, 2, chain)
            flip_dve(dve, "n1c", KT // 2, c_of("m1c"), c_of("sh1c"), b_hi, b_lo)
            proj_stream(dve, split_lo, store_dve)
            lat_dve(dve, chain)
            att_dve(dve, chain)
            presplit(split_lo, dve, WO)
            flip_dve(dve, "mix", KT // 2, lambda kt: C["subln_w"] if kt < HEADS else 1.0, None, b_hi, b_lo)
            wo_dve(dve, chain)
            residual(dve, chain, WO, 3, 3)
            presplit(split_lo, dve, UP[0])
            norm_diag_dve(dve, "n2", TILES, 10, chain)
            flip_dve(dve, "n2", KT // 2, c_of("m2"), c_of("sh2"), a_hi, a_lo)
            up_dve(dve, chain, 0, 3)
            down_dve(dve, chain, 0)
            up_dve(dve, chain, 1, 0, first_hooks={3: lambda: residual(dve, chain, DOWN[0], 3, 7)})
            down_dve(dve, chain, 1)
            residual(dve, chain, DOWN[1], 3, 11)
            final_dve(dve, chain)
            presplit(split_lo, dve, CV)
            norm_diag_dve(dve, "n3", TILES, 14, chain)
            flip_dve(dve, "n3", KT // 2, c_of("norm_w_2"), None, a_hi, a_lo)
            hyb_dve(dve, chain)
            gates_dve(dve, chain)
            pairs_of_heads(dve, lambda h, i=None: blk_dve(dve, chain, h, i), chain, 4)
            solve_dve(dve, chain)
            dve.wait_ge(sem("u_stored"), 32)
            for par in range(2):
                nc.vector.memset(ub[par][:], 0.0)
                nc.vector.memset(qb[par][:], 0.0)
                last = nc.vector.memset(vn[par][:], 0.0)
            last.then_inc(sem("dl_zero"), 1)
            dve.wait_ge(sem("dl_zero"), 1)
            pairs_of_heads(dve, lambda h, i=None: dl_dve(dve, h, i))
            sw_dve(dve, chain)
            out_dve(dve, chain)
            presplit(split_lo, dve, HO)
            flip_dve(dve, "mix2", MIX_KT // 2, lambda kt: C["dn_norm_w_2"] if kt < DN_V else 1.0, None, b_hi, b_lo)
            plain_dve(dve, HO, 3)
            presplit(split_lo, dve, SI)
            norm_diag_dve(dve, "n4", TILES, 16, chain)
            flip_dve(dve, "n4", KT // 2, c_of("norm_w_2", 16), None, a_hi, a_lo)
            sc_dve(dve, chain)
            plain_dve(dve, SO, 0, {3: lambda: (sc_bz(dve, N_SC), sc_conv(dve, chain, N_SC)), 4: lambda: sc_lo(dve, N_SC)})
            last_dve(dve, chain)

        @block.tensor
        def _(pe):
            ada_pe(pe)
            cols_pe(pe)
            flip_pe(pe, "n1", lambda kt, t: X[:, t, kt * P:(kt + 1) * P], KT // 2, lambda t: diag[:, t, :],
                    lambda: wait_diag(pe, "n1"))
            flip_pe(pe, "n1c", lambda kt, t: ctx_in[t][:, kt * P:(kt + 1) * P], KT // 2, lambda t: diag[:, t, :],
                    lambda: wait_diag(pe, "n1c"))
            proj_pe(pe)
            lat_pe(pe)
            att_pe(pe)
            flip_pe(pe, "mix", lambda kt, t: o_all[:, t, kt * P:(kt + 1) * P], KT // 2, lambda t: ident[:],
                    lambda: pe.wait_ge(sem("o_scaled"), 1))
            wo_pe(pe)
            flip_pe(pe, "n2", lambda kt, t: X[:, t, kt * P:(kt + 1) * P], KT // 2, lambda t: diag[:, t, :],
                    lambda: wait_diag(pe, "n2"))
            wait_flipped(pe, "n2")
            up_pe(pe, 0)
            down_pe(pe, 0)
            up_pe(pe, 1)
            down_pe(pe, 1)
            flip_pe(pe, "n3", x_at, KT // 2, lambda t: diag[:, t, :], lambda: wait_diag(pe, "n3"))
            wait_flipped(pe, "n3")
            hyb_pe(pe)
            gates_pe(pe)
            pairs_of_heads(pe, lambda h, i=None: blk_pe(pe, h, i))
            pairs_of_heads(pe, lambda h, i=None: dl_pe(pe, h, i))
            sw_pe(pe)
            flip_pe(pe, "mix2", lambda kt, t: o_all[:, t, kt * P:(kt + 1) * P] if kt < DN_V else
                    y_b[:, t, (kt - DN_V) * P:(kt - DN_V + 1) * P], MIX_KT // 2, lambda t: ident[:],
                    lambda: pe.wait_ge(sem("y_ready"), 1))
            wait_flipped(pe, "mix2")
            plain_pe(pe, HO)
            flip_pe(pe, "n4", x_at, KT // 2, lambda t: diag[:, t, :], lambda: wait_diag(pe, "n4"))
            wait_flipped(pe, "n4")
            sc_pe(pe)
            sc_last_pe(pe)


def constants():
    sel = np.zeros((4, P), np.float32)
    sel[[0, 2], 0] = sel[[1, 3], 1] = 1.0
    n_f = ROPE // 4
    inv = np.float32(10000.0) ** (-np.arange(n_f, dtype=np.float32) / n_f)
    rows, cols = np.arange(SEQ) // 64, np.arange(SEQ) % 64
    ang = np.stack([rows[:, None].astype(np.float32) * inv, cols[:, None].astype(np.float32) * inv], 1)
    c = np.stack([np.cos(ang), np.cos(ang)], 2).reshape(SEQ, ROPE)
    s = np.stack([-np.sin(ang), np.sin(ang)], 2).reshape(SEQ, ROPE)
    i, j = np.arange(P)[:, None], np.arange(P)[None, :]
    tri = ((i <= j) & (i // DN_CHUNK == j // DN_CHUNK)).astype(np.float32)
    half = np.stack([np.broadcast_to(i // DN_CHUNK == b, (P, P)) for b in range(2)]).astype(np.float32)
    tri_t = (np.arange(DN_CHUNK)[None, :] >= i % DN_CHUNK).astype(np.float32)
    cc, ii = np.arange(DN_CHUNK // 2)[None, :, None], np.arange(DN_CHUNK)[None, None, :]
    u0 = (ii == 2 * cc + (np.arange(P) // DN_CHUNK)[:, None, None]).astype(np.float32)
    q_at = np.arange(SEQ)[:, None]
    back = q_at - np.arange(SEQ)[None, :]
    seen = [(back >= 0) & (back % dil == 0) & (back // dil <= 128) for _, dil in SW_PATTERNS]
    mask = np.where(np.stack(seen, 1), 0.0, MASKED).astype(np.float32).reshape(TILES, P, -1).transpose(1, 0, 2)
    n_r = 16
    inv2 = np.power(np.float32(500000.0), -np.arange(n_r, dtype=np.float32) * np.float32(2.0) / np.float32(2 * n_r))
    ang2 = np.arange(SEQ, dtype=np.float32)[:, None] * inv2[None, :].astype(np.float32)
    extra = {"const_tri": tri, "const_half": half, "const_tri_t": tri_t, "const_u": u0,
             "const_sw_mask": np.ascontiguousarray(mask),
             "const_sw_c": np.concatenate([np.cos(ang2)] * 2, 1).astype(np.float32),
             "const_sw_s": np.concatenate([-np.sin(ang2), np.sin(ang2)], 1).astype(np.float32)}
    return {**extra, "const_sel": sel, "const_ident": np.eye(P, dtype=np.float32),
            "const_rope_c": np.tile(c, 2).astype(np.float32), "const_rope_s": np.tile(s, 2).astype(np.float32)}


def kernel(**inputs):
    import concourse.bacc as bacc
    from concourse.bass_utils import run_bass_kernel_spmd

    nc = bacc.Bacc("TRN2", target_bir_lowering=False, num_devices=1)
    arrays, aps = {}, {}
    for name, a in {**inputs, **constants()}.items():
        a = np.ascontiguousarray(a)
        arrays[f"in_{name}"] = a
        aps[name] = nc.dram_tensor(f"in_{name}", a.shape, mybir.dt.from_np(a.dtype), kind="ExternalInput").ap()
    out = nc.dram_tensor("out_0", (1, SEQ, D), F32, kind="ExternalOutput").ap()
    build_program(nc, aps, out[0])
    r = run_bass_kernel_spmd(nc, [arrays], core_ids=[0])
    return r.results[0]["out_0"]
```

```python
import math
from contextlib import ExitStack

import numpy as np

import concourse.bass as bass
from concourse import mybir

F32 = mybir.dt.float32
F32R = mybir.dt.float32r
ALU = mybir.AluOpType
ACT = mybir.ActivationFunctionType
AX = mybir.AxisListType.X

P = 128
SEQ = 256
TILES = SEQ // P
D = 2048
KT = D // P
CHUNK = 512
CT = CHUNK // P
GROUP = 4
RING = 4
EPS = 1e-6

HEADS = 8
HD = 128
HALF = HD // 2
DA_W = HEADS * HD
NOPE, ROPE, VD = 128, 64, 128
Q_RANK, KV_RANK = 384, 256
OFF_K, OFF_V, OFF_CQ = DA_W, 2 * DA_W, 3 * DA_W
OFF_CKV = OFF_CQ + Q_RANK
OFF_KR = OFF_CKV + KV_RANK
IN_W = OFF_KR + ROPE
D_FF = 5632
FT = D_FF // P
DA_SCALE = 1.0 / math.sqrt(HALF)
MLA_SCALE = 1.0 / math.sqrt(NOPE + ROPE)
LAMBDA_INIT = 0.8 - 0.6 * math.exp(-0.3 * 0)
N_MOD = 6
DN_QK, DN_V, DN_D = 8, 16, 128
DN_CHUNK = 64
SW_GROUPS, SW_HEADS = 3, 8
SW_PATTERNS = ((128, 1), (512, 4), (2048, 16))
A_QKV = 2 * DN_QK * DN_D + DN_V * DN_D
OFF_AZ = A_QKV
OFF_GATES = OFF_AZ + DN_V * DN_D
OFF_B = OFF_GATES + 2 * DN_V
W_BQ = SW_GROUPS * SW_HEADS * HD
W_RAW = DN_V * DN_D + W_BQ + 3 * SW_HEADS * HD
SW_SCALE = HD ** -0.5
SC_W = 3072
SC_KT = SC_W // P
MASKED = -1.0e30
FF_PARTS = ((0, 24), (24, 20))
MIX_KT = 24
SBUF_BYTES = 212800


def k_groups(n_k, n_groups):
    cuts = [n_k * g // n_groups for g in range(n_groups + 1)]
    out = [(a, b - a) for a, b in zip(cuts, cuts[1:])]
    assert all(0 < n <= GROUP for _, n in out)
    return out


class Count:

    def __init__(self, engine, sem):
        self.engine, self.sem, self.n, self.loop_at = engine, sem, 0, None

    def begin(self, i, first, per_turn):
        self.loop_at = (i, first, per_turn, self.n)

    def end(self, last):
        i, first, per_turn, start = self.loop_at
        assert self.n - start == per_turn, (self.n - start, per_turn)
        self.n = start + (last - first) * per_turn
        self.loop_at = None

    def done(self, instruction):
        self.n += 1
        instruction.then_inc(self.sem, 1)
        if self.loop_at is None:
            self.engine.wait_ge(self.sem, self.n)
        else:
            i, first, per_turn, _ = self.loop_at
            self.engine.wait_ge(self.sem, (i - first) * per_turn + self.n)


class Layer:

    def __init__(self, w, chunks, groups, pieces, accs, k0=0, both=False):
        self.w, self.chunks, self.groups, self.k0, self.both = w, chunks, groups, k0, both
        self.p0, self.c0 = pieces, accs
        self.per = len(groups)
        self.p1 = pieces + chunks * self.per
        self.c1 = accs + chunks * (2 if both else 1)


def at(v, i, step):
    return v if i is None else v + i * step


def build_program(nc, A, out):
    with ExitStack() as ctx:
        sems = {}

        def sem(name):
            if name not in sems:
                sems[name] = ctx.enter_context(nc.semaphore(name))
            return sems[name]

        ctx.enter_context(nc.sbuf_tensor("slab", [P, SBUF_BYTES // 4], F32))
        base = nc.sbuf_base - SBUF_BYTES
        top = [base]

        def place(name, shape, dt=F32, at=None):
            size = (int(np.prod(shape[1:])) * 4 + 31) // 32 * 32
            off = top[0] if at is None else at
            if at is None:
                top[0] += size
            assert off % 32 == 0 and off + size <= base + SBUF_BYTES, (name, off + size - base - SBUF_BYTES)
            return nc.alloc_sbuf_tensor_at(name, shape, dt, offset=off)

        def region(start, end):
            pos = [start]

            def put(name, shape, dt=F32):
                t = place(name, shape, dt, at=pos[0])
                pos[0] += (int(np.prod(shape[1:])) * 4 + 31) // 32 * 32
                assert pos[0] <= end, (name, pos[0] - end)
                return t
            return put

        raw = [place(f"raw{s}", [P, GROUP, CHUNK]) for s in range(RING)]
        w_hi = [place(f"w_hi{s}", [P, GROUP, CHUNK], F32R) for s in range(RING)]
        w_lo = [place(f"w_lo{s}", [P, GROUP, CHUNK], F32R) for s in range(RING)]
        A0 = top[0]
        a_hi = place("a_hi", [P, KT, SEQ], F32R)
        a_lo = place("a_lo", [P, KT, SEQ], F32R)
        B0 = top[0]
        b_hi = place("b_hi", [P, MIX_KT, SEQ], F32R)
        b_lo = place("b_lo", [P, MIX_KT, SEQ], F32R)
        X0 = top[0]
        X = place("X", [P, TILES, D])
        S0 = top[0]
        stg = [place(f"stg{i}", [P, TILES, CHUNK]) for i in range(2)]
        tmp = place("tmp", [P, 2, CHUNK])
        S1 = top[0]
        ident = place("ident_sb", [P, P])
        NCOL = 343 + 48 + 8
        col = place("col", [P, NCOL])
        stat = place("stat", [P, 32])
        diag = place("diag", [P, TILES, P])
        condf = place("condf", [P, KT, 2])
        ps = ctx.enter_context(nc.psum_tensor("ps", [P, 8, CHUNK], F32))

        pos = 0
        C = {}
        row_tiles = [[("norm1_w", 16), ("norm2_w", 16), ("norm_w_2", 32), ("q_norm_w", 3), ("kv_norm_w", 2),
                      ("subln_w", 1), ("dn_norm_w_2", 1), ("conv_b", FT)],
                     [("conv_w0", FT), ("conv_w1", FT)], [("conv_w2", FT)],
                     [("sh1", 16), ("s1", 16), ("sh1c", 16), ("s1c", 16)], [("sh2", 16), ("s2", 16)]]
        for tile in row_tiles:
            for name, n in tile:
                C[name] = col[:, pos:pos + n]
                pos += n
        for name in ("m1", "m1c", "m2"):
            C[name] = col[:, pos:pos + 16]
            pos += 16
        C["eps"] = col[:, pos:pos + 1]
        C["zero"] = col[:, pos + 1:pos + 2]
        C["lam"] = col[:, pos + 2:pos + 3]
        sub02 = col[:, pos + 3:pos + 4]

        def row_source(name):
            if name.startswith("conv_w"):
                tap = int(name[-1])
                v = A["conv_w"][0, tap:tap + 1, :].rearrange("a n -> (a n)")
            else:
                v = A[name].rearrange("a n -> (a n)")
            return v.rearrange("(r p) -> r p", p=P)

        layers = {}
        pieces = accs = 0

        def layer(name, w, chunks, n_k, n_groups, k0=0, both=False):
            nonlocal pieces, accs
            layers[name] = Layer(w, chunks, k_groups(n_k, n_groups), pieces, accs, k0, both)
            pieces, accs = layers[name].p1, layers[name].c1

        w_in = A["w_in"][0]
        layer("ada", A["w_ada"][0], 2 * D // CHUNK, KT, 4)
        layer("kv", w_in, 5, KT, 4, both=True)
        layer("q", w_in, 3, KT, 4)
        layer("uq", A["w_uq"][0], 3, Q_RANK // P, 1)
        layer("uk", A["w_ukv"][0], 4, KV_RANK // P, 1, both=True)
        accs += accs % 2
        layer("wo", A["w_o"][0], 4, KT, 4)
        layer("up0", A["w_up"][0], 12, KT, 4)
        layer("down0", A["w_down"][0], 4, 24, 8, k0=0)
        layer("up1", A["w_up"][0], 10, KT, 4)
        layer("down1", A["w_down"][0], 4, 20, 8, k0=24)
        hyb = A["hyb_w_in_2"][0]
        layer("conv", hyb, A_QKV // CHUNK, KT, 4)
        layer("gates", hyb, 1, KT, 4)
        layer("raw", hyb, W_RAW // CHUNK, KT, 4)
        layer("hout", A["hyb_w_out_2"][0], 4, 24, 8)
        layer("scin", A["sc_w_in_2"][0], 4 * SC_W // CHUNK, KT, 4)
        layer("scout", A["sc_w_out_2"][0], 4, SC_KT, 8)

        def dram(name, shape):
            return nc.dram_tensor(name, shape, F32, kind="Internal").ap()

        MOD = dram("mod_rows", (2, N_MOD * D))
        PROJ = dram("proj", (2 * SEQ, IN_W))
        PQ = dram("proj_q", (SEQ, HEADS * (NOPE + ROPE)))
        PKV = dram("proj_kv", (2 * SEQ, HEADS * (NOPE + VD)))

        def tok(ap):
            return ap.rearrange("(t p) n -> p t n", p=P)

        CONV = dram("conv_out", (SEQ, A_QKV))
        RAW = dram("raw_out", (SEQ, W_RAW))
        GROW = dram("gate_rows", (DN_V, SEQ))
        n_sys = DN_V * SEQ // DN_CHUNK
        AM = dram("delta_a", (DN_V, TILES, P, DN_CHUNK))
        QM = dram("delta_qk", (DN_V, TILES, P, DN_CHUNK))
        UM = dram("delta_u", (DN_V, TILES, P, DN_CHUNK))

        def load_piece(sp, L, p, kt, n_k, c_at, ncols=CHUNK, i=None, step=0):
            s = p % RING
            if p >= RING or i is not None:
                sp.wait_ge(sem("lo_done"), at(p - RING + 1, i, step))
            k = (L.k0 + kt) * P
            sp.dma_start(raw[s][:, 0:n_k, 0:ncols],
                         L.w[k:k + n_k * P, bass.ds(c_at, ncols)].rearrange("(k p) n -> p k n", p=P)
                         ).then_inc(sem(f"landed{s}"), 16)

        def load_chunk(sp, L, n, c_at, ncols=CHUNK, i=None, step=0, skip=0):
            for g, (kt, n_k) in enumerate(L.groups):
                if g >= skip:
                    load_piece(sp, L, L.p0 + n * L.per + g, kt, n_k, c_at, ncols, i, step)

        def split_hi(act, L, n, g, ncols=CHUNK, i=None, step=0):
            p, n_k = L.p0 + n * L.per + g, L.groups[g][1]
            s = p % RING
            act.wait_ge(sem(f"landed{s}"), at(16 * (p // RING + 1), i, step * 16 // RING))
            if p >= RING or i is not None:
                act.wait_ge(sem("piece_used"), at(p - RING + 1, i, step))
            nc.scalar.activation(w_hi[s][:, 0:n_k, 0:ncols], raw[s][:, 0:n_k, 0:ncols], ACT.Copy
                                 ).then_inc(sem("hi_done"), 1)

        def split_lo(dve, L, n, g, ncols=CHUNK, i=None, step=0):
            p, n_k = L.p0 + n * L.per + g, L.groups[g][1]
            s = p % RING
            dve.wait_ge(sem("hi_done"), at(p + 1, i, step))
            nc.vector.tensor_tensor(w_lo[s][:, 0:n_k, 0:ncols], raw[s][:, 0:n_k, 0:ncols],
                                    w_hi[s][:, 0:n_k, 0:ncols].bitcast(F32), ALU.subtract
                                    ).then_inc(sem("lo_done"), 1)

        def split_chunk(split, eng, L, n, ncols=CHUNK, i=None, step=0, hooks={}, skip=0):
            for g in range(L.per):
                if g in hooks:
                    hooks[g]()
                if g >= skip:
                    split(eng, L, n, g, ncols, i, step)
            if "end" in hooks:
                hooks["end"]()

        def acc_pair(c):
            return 2 * (c % 2)

        def wait_acc_free(pe, c, i=None, cstep=0):
            if c // 2 > 0 or i is not None:
                pe.wait_ge(sem(f"acc_free{c % 2}"), at(c // 2, i, cstep // 2))

        def matmul_chunk(pe, L, n, c, acts, ncols=CHUNK, i=None, step=0, cstep=0, hooks={}):
            for j in range(len(acts)):
                wait_acc_free(pe, c + j, i, cstep)
            for g, (kt0, n_k) in enumerate(L.groups):
                if g in hooks:
                    hooks[g]()
                p = L.p0 + n * L.per + g
                s = p % RING
                pe.wait_ge(sem("lo_done"), at(p + 1, i, step))
                for k in range(n_k):
                    kt = kt0 + k
                    for j, (hi, lo) in enumerate(acts):
                        for t in range(TILES):
                            o = ps[:, acc_pair(c + j) + t, 0:ncols]
                            h, l = hi(kt, t), lo(kt, t)
                            nc.tensor.matmul(o, h, w_hi[s][:, k, 0:ncols], start=kt == 0, stop=False)
                            nc.tensor.matmul(o, h, w_lo[s][:, k, 0:ncols], start=False, stop=False)
                            last = nc.tensor.matmul(o, l, w_hi[s][:, k, 0:ncols], start=False,
                                                    stop=kt == L.groups[-1][0] + L.groups[-1][1] - 1)
                last.then_inc(sem("piece_used"), 1)
            if "end" in hooks:
                hooks["end"]()

        def chunk_done(eng, L, n, i=None, step=0):
            eng.wait_ge(sem("piece_used"), at(L.p0 + (n + 1) * L.per, i, step))

        def tile_of(buf, first=0):
            return lambda kt, t: buf[:, first + kt, t * P:(t + 1) * P]

        putA = region(A0, B0)
        putB = region(B0, X0)
        cond = putA("cond", [P, KT, P], F32R)
        condr = putA("condr", [P, 2, KT])
        mrow = [putA(f"mrow{i}", [P, CHUNK]) for i in range(2)]
        mout = [putA(f"mout{i}", [P, CHUNK]) for i in range(2)]
        sel = putA("sel_sb", [P, P])
        brow = putB("brow", [P, 2 * D])
        rows = [place(f"rows{i}", [P, P], at=S0 + i * P * 4) for i in range(4)]
        L_ada = layers["ada"]

        def vec_loads(sp):
            for ti in range(3):
                r = 0
                for name, n in row_tiles[ti]:
                    sp.dma_start(rows[ti][r:r + n, :], row_source(name)).then_inc(sem("rows_in"), 16)
                    r += n

        n_row_dmas = sum(len(t) for t in row_tiles[:3])

        def ada_sp(sp):
            with nc.allow_non_contiguous_dma(reason="two short vectors into columns"):
                sp.dma_start(condr[:, 0, :], A["c"][0].rearrange("(k p) -> p k", p=P)).then_inc(sem("cond_in"), 16)
                sp.dma_start(condr[:, 1, :], A["c_ctx"].rearrange("(k p) -> p k", p=P)).then_inc(sem("cond_in"), 16)
            sp.dma_start(sel[0:4, :], A["const_sel"]).then_inc(sem("cond_in"), 16)
            load_chunk(sp, L_ada, 0, 0)
            sp.dma_start(brow[0:2, :], A["b_ada"][:, 0:2 * D].to_broadcast([2, 2 * D])).then_inc(sem("brow_in"), 16)
            sp.dma_start(ident[:], A["const_ident"]).then_inc(sem("rows_in"), 16)
            load_chunk(sp, L_ada, 1, CHUNK)
            with sp.Fori(1, L_ada.chunks // 2) as i:
                for h in range(2):
                    load_chunk(sp, L_ada, h, i * (2 * CHUNK) + h * CHUNK, i=i, step=2 * L_ada.per)
            sp.dma_start(X[:], tok(A["x"][0])).then_inc(sem("x_in"), 16)
            vec_loads(sp)

        def ada_act(act):
            act.wait_ge(sem("cond_in"), 48)
            nc.scalar.activation(condf[:, :, 0:2].rearrange("p k j -> p j k"), condr[:], ACT.Silu).then_inc(sem("cond_act"), 1)
            act.wait_ge(sem("cond_act"), 1)
            act.wait_ge(sem("cond_dve"), 1)
            nc.scalar.activation(cond[:, :, 0:2], condf[:], ACT.Copy).then_inc(sem("cond_act"), 1)

            def store(n, i=None):
                act.wait_ge(sem("mout_ready"), at(n + 1, i, 2))
                act.dma_start(MOD[:, bass.ds(at(n * CHUNK, i, 2 * CHUNK), CHUNK)], mout[n % 2][0:2, :]
                              ).then_inc(sem(f"mod_stored{n % 2}"), 16)
            split_chunk(split_hi, act, L_ada, 0)
            split_chunk(split_hi, act, L_ada, 1, hooks={"end": lambda: store(0)})
            with act.Fori(1, L_ada.chunks // 2) as i:
                for h in range(2):
                    split_chunk(split_hi, act, L_ada, h, i=i, step=2 * L_ada.per,
                                hooks={"end": lambda: store(h - 1, i)})
            store(L_ada.chunks - 1)

        def ada_dve(dve, chain):
            nc.vector.memset(cond[:].bitcast(F32), 0.0).then_inc(sem("cond_dve"), 1)
            dve.wait_ge(sem("cond_act"), 2)
            nc.vector.tensor_tensor(cond[:, :, 2:4], condf[:], cond[:, :, 0:2].bitcast(F32), ALU.subtract
                                    ).then_inc(sem("cond_dve"), 1)

            def copy_row(n, i=None):
                chunk_done(dve, L_ada, n, i, 2 * L_ada.per)
                nc.vector.tensor_copy(mrow[n % 2][0:4, :], ps[0:4, acc_pair(n), :]).then_inc(sem(f"acc_free{n % 2}"), 1)

            def copy_out(n, i=None):
                dve.wait_ge(sem("msum"), at(n + 1, i, 2))
                if n >= 2 or i is not None:
                    dve.wait_ge(sem(f"mod_stored{n % 2}"), at(16 * (n // 2), i, 16))
                nc.vector.tensor_tensor(mout[n % 2][0:2, :], ps[0:2, 4 + n % 2, :],
                                        brow[0:2, bass.ds(at(n * CHUNK, i, 2 * CHUNK), CHUNK)], ALU.add
                                        ).then_inc(sem("mout_ready"), 1)
            split_chunk(split_lo, dve, L_ada, 0)
            dve.wait_ge(sem("brow_in"), 16)
            split_chunk(split_lo, dve, L_ada, 1, hooks={3: lambda: copy_row(0), "end": lambda: copy_out(0)})
            with dve.Fori(1, L_ada.chunks // 2) as i:
                for h in range(2):
                    split_chunk(split_lo, dve, L_ada, h, i=i, step=2 * L_ada.per,
                                hooks={3: lambda: copy_row(h - 1, i), "end": lambda: copy_out(h - 1, i)})
            copy_row(L_ada.chunks - 1)
            copy_out(L_ada.chunks - 1)

        def ada_pe(pe):
            pe.wait_ge(sem("cond_dve"), 2)

            def chunk(n, i=None, hooks={}):
                if i is not None:
                    pe.wait_ge(sem(f"acc_free{n % 2}"), i)
                for g, (kt0, n_k) in enumerate(L_ada.groups):
                    if g in hooks:
                        hooks[g]()
                    p = L_ada.p0 + n * L_ada.per + g
                    pe.wait_ge(sem("lo_done"), at(p + 1, i, 2 * L_ada.per))
                    for k in range(n_k):
                        kt = kt0 + k
                        o = ps[:, acc_pair(n), :]
                        nc.tensor.matmul(o, cond[:, kt, :], w_hi[p % RING][:, k, :], start=kt == 0, stop=False)
                        last = nc.tensor.matmul(o, cond[:, kt, :], w_lo[p % RING][:, k, :], start=False, stop=kt == KT - 1)
                    last.then_inc(sem("piece_used"), 1)

            def total(n, i=None):
                pe.wait_ge(sem(f"acc_free{n % 2}"), at(n // 2 + 1, i, 1))
                o = ps[:, 4 + n % 2, :]
                if n >= 2 or i is not None:
                    pe.wait_ge(sem("mout_ready"), at(n - 1, i, 2))
                nc.tensor.matmul(o, sel[0:4, :], mrow[n % 2][0:4, :], start=True, stop=True).then_inc(sem("msum"), 1)
            chunk(0)
            chunk(1, hooks={2: lambda: total(0)})
            with pe.Fori(1, L_ada.chunks // 2) as i:
                for h in range(2):
                    chunk(h, i, hooks={2: lambda: total(h - 1, i)})
            total(L_ada.chunks - 1)

        ctx_in = [place(f"ctx_in{t}", [P, D], at=B0 + (16 * SEQ + t * MIX_KT * SEQ) * 4) for t in range(2)]

        def cols_sp(sp):
            for t in range(2):
                if t == 0:
                    sp.wait_ge(sem("mout_ready"), L_ada.chunks)
                sp.dma_start(ctx_in[t][:], A["ctx"][0, t * P:(t + 1) * P, :]).then_inc(sem("ctx_in"), 16)
            for par in range(2):
                sp.wait_ge(sem(f"mod_stored{par}"), 16 * L_ada.chunks // 2)
            for r, j in ((0, 0), (32, 1)):
                sp.dma_start(rows[3][r:r + 32, :], MOD[j, 0:2 * D].rearrange("(r p) -> r p", p=P)
                             ).then_inc(sem("rows_in"), 16)

        def cols_pe(pe):
            for ti in range(4):
                n = sum(n for _, n in row_tiles[ti])
                if ti == 0:
                    pe.wait_ge(sem("rows_in"), 16 * (n_row_dmas + 3))
                nc.tensor.transpose(ps[:, 6, ti * P:ti * P + n], rows[ti][0:n, :], ident[0:n, 0:n]
                                    ).then_inc(sem("col_t"), 1)

        def cols_dve(dve, chain):
            at_col = 0
            for ti in range(4):
                n = sum(n for _, n in row_tiles[ti])
                if ti == 0:
                    dve.wait_ge(sem("col_t"), 4)
                last = nc.vector.tensor_copy(col[:, at_col:at_col + n], ps[:, 6, ti * P:ti * P + n])
                at_col += n
            nc.vector.memset(C["eps"], EPS)
            nc.vector.memset(C["zero"], 0.0)
            chain.done(nc.vector.memset(sub02, LAMBDA_INIT))
            for m, s, w in (("m1", "s1", "norm1_w"), ("m1c", "s1c", "norm1_w")):
                last = nc.vector.scalar_tensor_tensor(C[m], C[s], 1.0, C[w], ALU.add, ALU.mult)
            last.then_inc(sem("cols"), 1)
            dve.wait_ge(sem("cols"), 1)

        NORMS = ("n1", "n1c", "n2", "fn", "n3", "n4", "ln")
        DIAGS = ("n1", "n1c", "n2", "n3", "n4")
        FLIPS = {"n1": KT // 2, "n1c": KT // 2, "lat": 7, "mix": KT // 2, "n2": KT // 2, "n3": KT // 2,
                 "mix2": MIX_KT // 2, "n4": KT // 2}

        def flips_before(name):
            return sum(list(FLIPS.values())[:list(FLIPS).index(name)])

        def wait_rms(eng, name):
            eng.wait_ge(sem("norm_rms"), NORMS.index(name) + 1)

        def wait_diag(eng, name):
            eng.wait_ge(sem("norm_diag"), DIAGS.index(name) + 1)

        def wait_flipped(eng, name):
            eng.wait_ge(sem("flip_lo"), flips_before(name) + FLIPS[name])

        def norm_stats_act(act, name, srcs, n_ch, s_at):
            for t, src in enumerate(srcs):
                nc.scalar.activation(sq_scratch(n_ch), src, ACT.Square, accum_out=stat[:, s_at + t:s_at + t + 1]
                                     ).then_inc(sem("norm_ss"), 1)
                act.wait_ge(sem("norm_ss"), TILES * NORMS.index(name) + t + 1)
            nc.scalar.activation(stat[:, s_at:s_at + len(srcs)], stat[:, s_at:s_at + len(srcs)], ACT.Sqrt,
                                 bias=C["eps"], scale=1.0 / n_ch).then_inc(sem("norm_rms"), 1)

        sq = place("sq_scratch", [P, D], at=S0)

        def sq_scratch(n):
            return sq[:, 0:n]

        def norm_diag_dve(dve, name, n, s_at, chain):
            wait_rms(dve, name)
            chain.done(nc.vector.reciprocal(stat[:, s_at:s_at + n], stat[:, s_at:s_at + n]))
            for t in range(n):
                last = nc.vector.tensor_scalar(diag[:, t, :], ident[:], stat[:, s_at + t:s_at + t + 1], None, ALU.mult)
            last.then_inc(sem("norm_diag"), 1)

        def flip_pair(pe, name, src, right, j):
            if j >= 2:
                pe.wait_ge(sem("flip_f"), flips_before(name) + j - 1)
            for k in range(2):
                for t in range(TILES):
                    last = nc.tensor.matmul(ps[:, 4 + j % 2, (k * TILES + t) * P:(k * TILES + t + 1) * P],
                                            src(2 * j + k, t), right(t), start=True, stop=True)
            last.then_inc(sem("flip_t"), 1)

        def flip_pe(pe, name, src, n_pairs, right, first_wait):
            first_wait()
            for j in range(n_pairs):
                flip_pair(pe, name, src, right, j)

        def flip_hooks(pe, L, name, src, right, first_wait):
            n_pairs = FLIPS[name]
            flipped = [0]

            def until(n):
                while flipped[0] < min(n, n_pairs):
                    flip_pair(pe, name, src, right, flipped[0])
                    flipped[0] += 1

            def pairs_for(g):
                kt, n_k = L.groups[min(g, L.per - 1)]
                return (kt + n_k + 1) // 2

            def before(g):
                if g == 0:
                    first_wait()
                until(n_pairs if g >= RING - 1 else pairs_for(g + 1))
                pe.wait_ge(sem("flip_lo"), flips_before(name) + pairs_for(g))
            return {g: (lambda g=g: before(g)) for g in range(L.per)}

        def flip_dve(dve, name, n_pairs, scale, shift, hi, lo):
            m = flips_before(name)

            def low(j):
                dve.wait_ge(sem("flip_hi"), m + j + 1)
                nc.vector.tensor_tensor(lo[:, 2 * j:2 * j + 2, :], tmp_f(j), hi[:, 2 * j:2 * j + 2, :].bitcast(F32),
                                        ALU.subtract).then_inc(sem("flip_lo"), 1)
            for j in range(n_pairs):
                dve.wait_ge(sem("flip_t"), m + j + 1)
                if j >= 2:
                    dve.wait_ge(sem("flip_lo"), m + j - 1)
                for k in range(2):
                    kt = 2 * j + k
                    f = tmp_f(j)[:, k, :]
                    src = ps[:, 4 + j % 2, k * SEQ:(k + 1) * SEQ]
                    if shift is None:
                        last = nc.vector.tensor_scalar(f, src, scale(kt), None, ALU.mult)
                    else:
                        last = nc.vector.tensor_scalar(f, src, scale(kt), shift(kt), ALU.mult, ALU.add)
                last.then_inc(sem("flip_f"), 1)
                if j >= 1:
                    low(j - 1)
            low(n_pairs - 1)

        def flip_act(act, name, n_pairs, hi):
            for j in range(n_pairs):
                act.wait_ge(sem("flip_f"), flips_before(name) + j + 1)
                nc.scalar.activation(hi[:, 2 * j:2 * j + 2, :], tmp_f(j), ACT.Copy).then_inc(sem("flip_hi"), 1)

        def tmp_f(j):
            return tmp[:, j % 2, :].rearrange("p (k s) -> p k s", k=2)

        def c_of(name, first=0):
            return lambda kt: C[name][:, first + kt:first + kt + 1]

        KV, Q, UQ, UK = layers["kv"], layers["q"], layers["uq"], layers["uk"]
        LAT = Q_RANK
        kv_cols = [(OFF_K, CHUNK), (OFF_K + CHUNK, CHUNK), (OFF_V, CHUNK), (OFF_V + CHUNK, CHUNK),
                   (OFF_CKV, KV_RANK + ROPE)]
        q_cols = [(0, CHUNK), (CHUNK, CHUNK), (OFF_CQ, Q_RANK)]

        def proj_sp(sp):
            for n, (c0, w) in enumerate(kv_cols):
                load_chunk(sp, KV, n, c0, w)
            for n, (c0, w) in enumerate(q_cols):
                load_chunk(sp, Q, n, c0, w)

        def copy_pair(eng, L, n, c, buf, w, count):
            if eng is nc.scalar:
                nc.scalar.activation(buf[:, :, 0:w], ps[:, acc_pair(c):acc_pair(c) + 2, 0:w], ACT.Copy
                                     ).then_inc(sem(f"acc_free{c % 2}"), 1)
            else:
                nc.vector.tensor_copy(buf[:, :, 0:w], ps[:, acc_pair(c):acc_pair(c) + 2, 0:w]
                                      ).then_inc(sem(f"acc_free{c % 2}"), 1)

        stores = []
        for n, (c0, w) in enumerate(kv_cols):
            stores.append((KV, n, KV.c0 + 2 * n, True, PROJ, c0, w))
        for n, (c0, w) in enumerate(q_cols):
            stores.append((Q, n, Q.c0 + n, False, PROJ[SEQ:2 * SEQ], c0, w))
        for n in range(3):
            stores.append((UQ, n, UQ.c0 + n, False, PQ, n * CHUNK, CHUNK))
        for n in range(4):
            stores.append((UK, n, UK.c0 + 2 * n, True, PKV, n * CHUNK, CHUNK))

        def store_act(act, m):
            L, n, c, both, dst, c0, w = stores[m]
            chunk_done(act, L, n)
            if m >= 1:
                act.wait_ge(sem("stored_x"), 16 * m)
            copy_pair(nc.scalar, L, n, c, stg[0], w, m)
            act.wait_ge(sem(f"acc_free{c % 2}"), c // 2 + 1)
            x_rows = dst[SEQ:2 * SEQ] if both else dst
            act.dma_start(tok(x_rows[:, c0:c0 + w]), stg[0][:, :, 0:w]).then_inc(sem("stored_x"), 16)
            if both:
                act.wait_ge(sem(f"acc_free{(c + 1) % 2}"), (c + 1) // 2 + 1)
                act.dma_start(tok(dst[0:SEQ, c0:c0 + w]), stg[1][:, :, 0:w]).then_inc(sem("stored_c"), 16)

        def store_dve(dve, m):
            L, n, c, both, dst, c0, w = stores[m]
            if both:
                chunk_done(dve, L, n)
                before = sum(s[3] for s in stores[:m])
                if before:
                    dve.wait_ge(sem("stored_c"), 16 * before)
                copy_pair(nc.vector, L, n, c + 1, stg[1], w, m)

        def proj_stream(eng, split, store):
            m = 0
            for L, cols in ((KV, kv_cols), (Q, q_cols)):
                for n, (c0, w) in enumerate(cols):
                    hooks = {} if m == 0 else {3: (lambda m=m: store(eng, m - 1))}
                    split_chunk(split, eng, L, n, w, hooks=hooks, skip=3 if m == 0 else 0)
                    m += 1

        def presplit(split, eng, L, n=3, w=CHUNK):
            for g in range(n):
                split(eng, L, 0, g, w)

        def proj_pe(pe):
            hx = (tile_of(a_hi), tile_of(a_lo))
            hc = (tile_of(b_hi), tile_of(b_lo))
            wait_flipped(pe, "n1")
            wait_flipped(pe, "n1c")
            for n, (c0, w) in enumerate(kv_cols):
                matmul_chunk(pe, KV, n, KV.c0 + 2 * n, [hx, hc], w)
            for n, (c0, w) in enumerate(q_cols):
                matmul_chunk(pe, Q, n, Q.c0 + n, [hx], w)

        put = region(B0, X0)
        LAT0 = flips_before("lat")
        lat_q = put("lat_q", [P, TILES, Q_RANK])
        lat_kv = put("lat_kv", [P, 2 * TILES, KV_RANK])
        n_stored_proj = len(kv_cols) + len(q_cols)

        def lat_sp(sp):
            for n in range(3):
                load_chunk(sp, UQ, n, n * CHUNK)
            load_chunk(sp, UK, 0, 0)
            sp.wait_ge(sem("stored_x"), 16 * n_stored_proj)
            sp.wait_ge(sem("stored_c"), 16 * len(kv_cols))
            sp.dma_start(lat_q[:], tok(PROJ[SEQ:2 * SEQ, OFF_CQ:OFF_CQ + Q_RANK])).then_inc(sem("lat_in"), 16)
            sp.dma_start(lat_kv[:], tok(PROJ[:, OFF_CKV:OFF_CKV + KV_RANK])).then_inc(sem("lat_in"), 16)
            for n in range(1, 4):
                load_chunk(sp, UK, n, n * CHUNK)

        def lat_act(act):
            store_act(act, n_stored_proj - 1)
            act.wait_ge(sem("lat_in"), 32)
            for t in range(2):
                nc.scalar.activation(sq_scratch(Q_RANK), lat_q[:, t, :], ACT.Square, accum_out=stat[:, 4 + t:5 + t]
                                     ).then_inc(sem("lat_ss"), 1)
                act.wait_ge(sem("lat_ss"), t + 1)
            for t in range(4):
                nc.scalar.activation(sq_scratch(KV_RANK), lat_kv[:, t, :], ACT.Square, accum_out=stat[:, 6 + t:7 + t]
                                     ).then_inc(sem("lat_ss"), 1)
                act.wait_ge(sem("lat_ss"), 3 + t)
            nc.scalar.activation(stat[:, 4:6], stat[:, 4:6], ACT.Sqrt, bias=C["eps"], scale=1.0 / Q_RANK).then_inc(sem("lat_rms"), 1)
            nc.scalar.activation(stat[:, 6:10], stat[:, 6:10], ACT.Sqrt, bias=C["eps"], scale=1.0 / KV_RANK).then_inc(sem("lat_rms"), 1)
            for m in range(7):
                act.wait_ge(sem("flip_f"), LAT0 + m + 1)
                nc.scalar.activation(lat_hi(m), lat_f(m), ACT.Copy).then_inc(sem("flip_hi"), 1)
            for n in range(3):
                split_hi(act, UQ, n, 0)
            split_hi(act, UK, 0, 0)
            for n in range(3):
                store_act(act, n_stored_proj + n)
            for n in range(4):
                if n:
                    split_hi(act, UK, n, 0)
                store_act(act, n_stored_proj + 3 + n)

        lat_t = [("q", 0, 0), ("q", 1, 0), ("q", 2, 0), ("kv", 0, 0), ("kv", 1, 0), ("kv", 0, 1), ("kv", 1, 1)]

        def lat_f(m):
            return tmp[:, m % 2, 0:SEQ]

        def lat_hi(m):
            return a_hi[:, m, :]

        def lat_pe(pe):
            pe.wait_ge(sem("lat_scaled"), 1)
            for m, (kind, r, is_ctx) in enumerate(lat_t):
                if m >= 2:
                    pe.wait_ge(sem("flip_f"), LAT0 + m - 1)
                for t in range(TILES):
                    if kind == "q":
                        src = lat_q[:, t, r * P:(r + 1) * P]
                    else:
                        src = lat_kv[:, (0 if is_ctx else TILES) + t, r * P:(r + 1) * P]
                    last = nc.tensor.transpose(ps[:, 4 + m % 2, t * P:(t + 1) * P], src, ident[:])
                last.then_inc(sem("flip_t"), 1)
            wait_flipped(pe, "lat")
            hx = (tile_of(a_hi), tile_of(a_lo))
            for n in range(3):
                matmul_chunk(pe, UQ, n, UQ.c0 + n, [hx])
            kx = (tile_of(a_hi, 3), tile_of(a_lo, 3))
            kc = (tile_of(a_hi, 5), tile_of(a_lo, 5))
            for n in range(4):
                matmul_chunk(pe, UK, n, UK.c0 + 2 * n, [kx, kc])

        def lat_dve(dve, chain):
            store_dve(dve, n_stored_proj - 1)
            dve.wait_ge(sem("lat_rms"), 2)
            chain.done(nc.vector.reciprocal(stat[:, 4:10], stat[:, 4:10]))
            for t in range(2):
                nc.vector.tensor_scalar(lat_q[:, t, :], lat_q[:, t, :], stat[:, 4 + t:5 + t], None, ALU.mult)
            for t in range(4):
                last = nc.vector.tensor_scalar(lat_kv[:, t, :], lat_kv[:, t, :], stat[:, 6 + t:7 + t], None, ALU.mult)
            last.then_inc(sem("lat_scaled"), 1)

            def low(m):
                dve.wait_ge(sem("flip_hi"), LAT0 + m + 1)
                nc.vector.tensor_tensor(a_lo[:, m, :], lat_f(m), lat_hi(m).bitcast(F32), ALU.subtract
                                        ).then_inc(sem("flip_lo"), 1)
            for m, (kind, r, is_ctx) in enumerate(lat_t):
                dve.wait_ge(sem("flip_t"), LAT0 + m + 1)
                if m >= 2:
                    dve.wait_ge(sem("flip_lo"), LAT0 + m - 1)
                w = C["q_norm_w" if kind == "q" else "kv_norm_w"][:, r:r + 1]
                nc.vector.tensor_scalar(lat_f(m), ps[:, 4 + m % 2, 0:SEQ], w, None, ALU.mult).then_inc(sem("flip_f"), 1)
                if m:
                    low(m - 1)
            low(len(lat_t) - 1)
            for n in range(3):
                split_lo(dve, UQ, n, 0)
            split_lo(dve, UK, 0, 0)
            for n in range(4):
                if n:
                    split_lo(dve, UK, n, 0)
                store_dve(dve, n_stored_proj + 3 + n)

        N_LATE = (N_MOD - 2) * D // CHUNK
        assert N_LATE == 2 * HEADS and RING == KT // GROUP
        POOL_COLS = 128
        SPLIT = CHUNK - POOL_COLS
        W0 = base + RING * GROUP * CHUNK * 4
        macc = place("macc", [P, N_LATE * CHUNK], at=W0)
        msl = [raw, [place(f"mod_slot{g}", [P, GROUP, CHUNK], at=W0 + (RING + g) * GROUP * CHUNK * 4)
                     for g in range(RING)]]
        late_row = place("late_row", [P, N_LATE * CHUNK], at=W0 + RING * GROUP * CHUNK * 4)
        rows_l = place("rows_late", [P, P], at=B0 - P * 4)
        ones = place("ones", [P, P], at=S0 + TILES * CHUNK * 4)
        put = region(B0 - 2 * (SPLIT + GROUP * POOL_COLS) * 4, B0)
        run = [put(f"run{j}", [P, SPLIT]) for j in range(2)]
        run_p, prod_p = (put(n, [P, GROUP, POOL_COLS]) for n in ("run_p", "prod_p"))

        def late_load(sp, m, i=None):
            for g in range(RING):
                if m >= 2 or i is not None:
                    sp.wait_ge(sem("late_used"), at(RING * (m - 2) + g + 1, i, 2 * RING))
                c0 = 2 * D + m * CHUNK if i is None else i * (2 * CHUNK) + (2 * D + m * CHUNK)
                sp.dma_start(msl[m % 2][g][:], A["w_ada"][0][g * GROUP * P:(g + 1) * GROUP * P, bass.ds(c0, CHUNK)]
                             .rearrange("(k p) n -> p k n", p=P)).then_inc(sem(f"late_in{m % 2}"), 16)

        def late_at(m, c0, n, i):
            return macc[:, bass.ds(m * CHUNK + c0 if i is None else i * (2 * CHUNK) + (m * CHUNK + c0), n)]

        def late_dve(dve, chain, m, g, i=None):
            if g == 0:
                dve.wait_ge(sem(f"late_in{m % 2}"), at(16 * RING * (m // 2 + 1), i, 16 * RING))
            if g or m >= 1 or i is not None:
                dve.wait_ge(sem("late_sum"), at(RING * m + g, i, 2 * RING))
            for k in range(GROUP):
                w, cs, acc = msl[m % 2][g][:, k, 0:SPLIT], condf[:, g * GROUP + k, 0:1], run[k % 2][:]
                if k == GROUP // 2:
                    chain.done(last)
                if g == 0 and k < 2:
                    last = nc.vector.tensor_scalar(acc, w, cs, None, ALU.mult)
                else:
                    last = nc.vector.scalar_tensor_tensor(acc, w, cs, acc, ALU.mult, ALU.add)
            if g == RING - 1:
                chain.done(last)
                last = nc.vector.tensor_tensor(late_at(m, 0, SPLIT, i), run[0][:], run[1][:], ALU.add)
            last.then_inc(sem("late_sum"), 1)

        def late_pool(pool, chain, m, i=None):
            for g in range(RING):
                if g == 0:
                    pool.wait_ge(sem(f"late_in{m % 2}"), at(16 * RING * (m // 2 + 1), i, 16 * RING))
                if g or m >= 1 or i is not None:
                    pool.wait_ge(sem("late_used"), at(RING * m + g, i, 2 * RING))
                w = msl[m % 2][g][:, :, SPLIT:]
                cs = condf[:, g * GROUP:(g + 1) * GROUP, 0:1].to_broadcast([P, GROUP, POOL_COLS])
                if g:
                    chain.done(nc.gpsimd.tensor_tensor(prod_p[:], w, cs, ALU.mult))
                pool.wait_ge(sem("late_sum"), at(RING * m + g + 1, i, 2 * RING))
                if g == 0:
                    last = nc.gpsimd.tensor_tensor(run_p[:], w, cs, ALU.mult)
                else:
                    last = nc.gpsimd.tensor_tensor(run_p[:], run_p[:], prod_p[:], ALU.add)
                if g == RING - 1:
                    chain.done(last)
                    half = GROUP // 2
                    chain.done(nc.gpsimd.tensor_tensor(prod_p[:, 0:half], run_p[:, 0:half], run_p[:, half:], ALU.add))
                    last = nc.gpsimd.tensor_tensor(late_at(m, SPLIT, POOL_COLS, i), prod_p[:, 0], prod_p[:, 1], ALU.add)
                last.then_inc(sem("late_used"), 1)

        def late_rows_sp(sp):
            sp.wait_ge(sem("late_used"), RING * N_LATE)
            sp.dma_start(late_row[0:1, :], A["b_ada"][:, 2 * D:]).then_inc(sem("late_b"), 16)

        def late_rows_pe(pe):
            pe.wait_ge(sem("late_sum"), RING * N_LATE)
            pe.wait_ge(sem("late_used"), RING * N_LATE)
            pe.wait_ge(sem("at_dve"), 4)
            pe.wait_ge(sem("at_o"), 4 * HEADS)
            for q in range(N_LATE // 4):
                if q >= 2:
                    pe.wait_ge(sem("late_row"), q - 1)
                for b in range(4):
                    last = nc.tensor.matmul(ps[:, 4 * (q % 2) + b, :], ones[:],
                                            macc[:, (4 * q + b) * CHUNK:(4 * q + b + 1) * CHUNK], start=True, stop=True)
                last.then_inc(sem("late_total"), 1)

        def late_rows_dve(dve):
            dve.wait_ge(sem("late_b"), 16)
            for q in range(N_LATE // 4):
                dve.wait_ge(sem("late_total"), q + 1)
                r = late_row[0:1, q * D:(q + 1) * D]
                nc.vector.tensor_tensor(r, ps[0:1, 4 * (q % 2):4 * (q % 2) + 4, :].rearrange("a b n -> a (b n)"), r,
                                        ALU.add).then_inc(sem("late_row"), 1)

        def late_store(act):
            for q in range(N_LATE // 4):
                act.wait_ge(sem("late_row"), q + 1)
                act.dma_start(MOD[0:1, (2 + q) * D:(3 + q) * D], late_row[0:1, q * D:(q + 1) * D]
                              ).then_inc(sem("late_stored"), 16)

        def late_cols_sp(sp):
            sp.wait_ge(sem("late_stored"), 16 * N_LATE // 4)
            sp.dma_start(rows_l[0:32, :], MOD[0, 3 * D:5 * D].rearrange("(r p) -> r p", p=P)).then_inc(sem("late_cols"), 16)

        def late_cols_pe(pe):
            pe.wait_ge(sem("late_cols"), 16)
            nc.tensor.transpose(ps[:, 6, 0:32], rows_l[0:32, :], ident[0:32, 0:32]).then_inc(sem("late_t"), 1)

        def late_cols_dve(dve, chain):
            dve.wait_ge(sem("late_t"), 1)
            at_col = sum(n for tile in row_tiles[:4] for _, n in tile)
            chain.done(nc.vector.tensor_copy(col[:, at_col:at_col + 32], ps[:, 6, 0:32]))
            chain.done(nc.vector.scalar_tensor_tensor(C["m2"], C["s2"], 1.0, C["norm2_w"], ALU.add, ALU.mult))

        put = region(B0, X0)
        put_a = region(A0, B0)
        n_keys = 2 * TILES
        q_in = [put(f"q_in{i}", [P, TILES, NOPE + ROPE]) for i in range(2)]
        k_in = [put(f"k_in{i}", [P, n_keys, HD]) for i in range(2)]
        v_in = [put(f"v_in{i}", [P, n_keys, HD]) for i in range(2)]
        qT = [put(f"qT{i}", [P, SEQ]) for i in range(2)]
        qrT = [put(f"qrT{i}", [P, SEQ]) for i in range(2)]
        kT = [put(f"kT{i}", [P, CHUNK]) for i in range(2)]
        krT = put("krT", [P, CHUNK])
        ex = [put(f"ex{i}", [P, 2, CHUNK]) for i in range(2)]
        wt = [put(f"wt{i}", [P, CHUNK]) for i in range(2)]
        wT = [put(f"wT{i}", [P, n_keys, P]) for i in range(2)]
        o_all = put_a("o_all", [P, TILES, D])
        rope_c = put_a("rope_c", [P, TILES, HD])
        rope_s = put_a("rope_s", [P, TILES, HD])
        rm = [put_a(f"rope_m{i}", [P, 2, TILES * HD]) for i in range(2)]
        kr_in = put_a("kr_in", [P, n_keys, ROPE])
        lam_in = put_a("lam_in", [P, 4, HALF])
        mx = [put_a(f"mx{i}", [P, 8]) for i in range(2)]
        ssum = put_a("ssum", [P, TILES * HEADS])
        lamt = put_a("lamt", [P, 4])
        WO = layers["wo"]

        def ev(v, i):
            return v if i is None else v + i * 2

        def ev2(v, i):
            return v if i is None else v + i * 4

        def head_col(h, i, width):
            return h * width if i is None else h * width + i * (2 * width)

        def att_load_qk(eng, h, i=None):
            par = h % 2
            if h < HEADS:
                w = head_col(h, i, HD)
                w = w if i is None else eng.snap(w)
                srcs = (PROJ[SEQ:2 * SEQ, bass.ds(w, HD)], PROJ[:, OFF_K:][:, bass.ds(w, HD)])
                dsts = (q_in[par][:, :, 0:HD], k_in[par][:])
            else:
                wq, wk = head_col(h - HEADS, i, NOPE + ROPE), head_col(h - HEADS, i, NOPE + VD)
                if i is not None:
                    wq, wk = eng.snap(wq), eng.snap(wk)
                srcs = (PQ[:, bass.ds(wq, NOPE + ROPE)], PKV[:, bass.ds(wk, NOPE)])
                dsts = (q_in[par][:], k_in[par][:])
            for d, s_ in zip(dsts, srcs):
                eng.dma_start(d, tok(s_)).then_inc(sem(f"at_qk_in{par}"), 16)

        def att_load_v(sp, h, i=None):
            if h < HEADS:
                w = head_col(h, i, HD)
                src = PROJ[:, OFF_V:][:, bass.ds(w if i is None else sp.snap(w), HD)]
            else:
                w = head_col(h - HEADS, i, NOPE + VD)
                src = PKV[:, NOPE:][:, bass.ds(w if i is None else sp.snap(w), VD)]
            if h >= 2:
                sp.wait_ge(sem("at_pv"), ev2(2 * (h - 1), i))
            sp.dma_start(v_in[h % 2][:], tok(src)).then_inc(sem(f"at_v_in{h % 2}"), 16)

        def att_sp(sp):
            sp.wait_ge(sem("stored_x"), 16 * len(stores))
            sp.wait_ge(sem("stored_c"), 16 * (len(kv_cols) + 4))
            sp.dma_start(rope_c[:], tok(A["const_rope_c"])).then_inc(sem("at_tab"), 16)
            sp.dma_start(rope_s[:], tok(A["const_rope_s"])).then_inc(sem("at_tab"), 16)
            for j, name in enumerate(("lambda_q1", "lambda_k1", "lambda_q2", "lambda_k2")):
                sp.dma_start(lam_in[:, j, :], A[name].to_broadcast([P, HALF])).then_inc(sem("at_tab"), 16)
            sp.dma_start(kr_in[:], tok(PROJ[:, OFF_KR:OFF_KR + ROPE])).then_inc(sem("at_tab"), 16)
            for h in range(2):
                att_load_qk(sp, h)
                att_load_v(sp, h)
            sp.wait_ge(sem("piece_used"), WO.p0)
            late_load(sp, 0)
            late_load(sp, 1)

            def ahead(h, i=None):
                att_load_v(sp, h, i)
                late_load(sp, h, i)
            for first, turns in ((2, 3), (8, 4)):
                with sp.Fori(0, turns) as i:
                    ahead(first, i)
                    ahead(first + 1, i)
            sp.wait_ge(sem("late_used"), RING * (N_LATE - 1))
            load_chunk(sp, WO, 0, 0)
            late_rows_sp(sp)

        def rotate(chain, name, parts, i=None):
            for b, (x, c, s_) in enumerate(parts):
                n = x.shape[1] * x.shape[2]
                m = rm[b][:, :, 0:n]

                def halves(v):
                    return v.rearrange("p t (b h f) -> p t b h f", h=2, f=16)
                m0 = m[:, 0, :].rearrange("p (t n) -> p t n", t=x.shape[1])
                m1 = halves(m[:, 1, :].rearrange("p (t n) -> p t n", t=x.shape[1]))
                nc.gpsimd.tensor_tensor(m0, x, c, ALU.mult)
                for h in range(2):
                    for t in range(x.shape[1]):
                        last = nc.gpsimd.tensor_tensor(m1[:, t, :, h, :], halves(x)[:, t, :, 1 - h, :],
                                                       halves(s_)[:, t, :, h, :], ALU.mult)
            chain.done(last)
            for b, (x, c, s_) in enumerate(parts):
                n = x.shape[1] * x.shape[2]
                last = nc.gpsimd.tensor_tensor(x, rm[b][:, 0, 0:n].rearrange("p (t n) -> p t n", t=x.shape[1]),
                                               rm[b][:, 1, 0:n].rearrange("p (t n) -> p t n", t=x.shape[1]), ALU.add)
            last.then_inc(sem(name), 1)

        def att_rope(pool, chain, h, i=None):
            par = h % 2
            pool.wait_ge(sem(f"at_qk_in{par}"), at(32 * (h // 2 + 1), i, 32))
            if h >= 1 or i is not None:
                pool.wait_ge(sem("at_roped"), ev(h, i))
            if h < HEADS:
                rotate(chain, "at_roped", [(q_in[par][:, :, 0:HD], rope_c[:], rope_s[:]),
                                           (k_in[par][:, TILES:n_keys, :], rope_c[:], rope_s[:])])
            else:
                rotate(chain, "at_roped", [(q_in[par][:, :, NOPE:], rope_c[:, :, 0:ROPE], rope_s[:, :, 0:ROPE])])

        def att_pool(pool, chain):
            pool.wait_ge(sem("at_tab"), 16 * 7)
            rotate(chain, "kr_roped", [(kr_in[:, TILES:n_keys, :], rope_c[:, :, 0:ROPE], rope_s[:, :, 0:ROPE])])
            pool.wait_ge(sem("kr_roped"), 1)
            for h in range(3):
                att_rope(pool, chain, h)

            def step(h, i=None):
                att_rope(pool, chain, h, i)
                late_pool(pool, chain, h - 3, i)
            step(3)
            for first, turns, then in ((4, 2, 8), (9, 3, 15)):
                with pool.Fori(0, turns) as i:
                    chain.begin(i, 0, 2 * (1 + (RING - 1) + 2))
                    step(first, i)
                    step(first + 1, i)
                    chain.end(turns)
                step(then)
            for m in range(2 * HEADS - 3, 2 * HEADS):
                late_pool(pool, chain, m)

        def att_flip(pe, h, i=None):
            par = h % 2
            pe.wait_ge(sem("at_roped"), ev(h + 1, i))
            if h >= 1 or i is not None:
                pe.wait_ge(sem("at_qT"), ev(h, i))
                pe.wait_ge(sem("at_kT"), ev(h, i))
            for t in range(TILES):
                nc.tensor.transpose(ps[:, 4, t * P:(t + 1) * P], q_in[par][:, t, 0:HD], ident[:])
                if h >= HEADS:
                    nc.tensor.transpose(ps[0:ROPE, 4, SEQ + t * P:SEQ + (t + 1) * P], q_in[par][:, t, NOPE:], ident[:])
            for t in range(n_keys):
                last = nc.tensor.transpose(ps[:, 5, t * P:(t + 1) * P], k_in[par][:, t, :], ident[:])
            last.then_inc(sem("at_flip"), 1)

        def att_scores(pe, h, t, i=None):
            par, u = h % 2, 2 * h + t
            if t == 0:
                pe.wait_ge(sem("at_qT"), ev(h + 1, i))
                pe.wait_ge(sem("at_kT"), ev(h + 1, i))
            if u >= 2:
                pe.wait_ge(sem("at_exp"), ev2(u - 1, i))
            cols = slice(t * P, (t + 1) * P)
            if h < HEADS:
                nc.tensor.matmul(ps[:, 2 * t, :], qT[par][0:HALF, cols], kT[par][0:HALF, :], start=True, stop=True)
                nc.tensor.matmul(ps[:, 2 * t + 1, :], qT[par][HALF:HD, cols], kT[par][HALF:HD, :], start=True,
                                 stop=True).then_inc(sem("at_sc"), 1)
            else:
                if h == HEADS and t == 0:
                    pe.wait_ge(sem("at_dve"), 2)
                nc.tensor.matmul(ps[:, 2 * t, :], qT[par][:, cols], kT[par][:], start=True, stop=False)
                nc.tensor.matmul(ps[:, 2 * t, :], qrT[par][:, cols], krT[:], start=False, stop=True
                                 ).then_inc(sem("at_sc"), 1)

        def att_wt(pe, u, i=None):
            latent = u >= 2 * HEADS
            pe.wait_ge(sem("at_w"), ev2(u + 1, i))
            if u >= 1:
                pe.wait_ge(sem("at_wT"), ev2(u, i))
            src = ex[u % 2][:, 0, :] if latent else wt[u % 2][:]
            for k in range(n_keys):
                last = nc.tensor.transpose(ps[:, 6, k * P:(k + 1) * P], src[:, k * P:(k + 1) * P], ident[:])
            last.then_inc(sem("at_wflip"), 1)

        def att_pv(pe, u, i=None):
            par = (u // 2) % 2
            pe.wait_ge(sem("at_wT"), ev2(u + 1, i))
            if u % 2 == 0:
                pe.wait_ge(sem(f"at_v_in{par}"), at(16 * (u // 4 + 1), i, 16))
            if u >= 1:
                pe.wait_ge(sem("at_o"), ev2(u, i))
            for k in range(n_keys):
                last = nc.tensor.matmul(ps[:, 7, 0:HD], wT[u % 2][:, k, :], v_in[par][:, k, :], start=k == 0,
                                        stop=k == n_keys - 1)
            last.then_inc(sem("at_pv"), 1)

        def att_head_pe(pe, h, i=None, flip_next=True):
            att_scores(pe, h, 0, i)
            if h >= 1:
                att_wt(pe, 2 * h - 1, i)
                att_pv(pe, 2 * h - 1, i)
            att_scores(pe, h, 1, i)
            if flip_next:
                att_flip(pe, h + 1, i)
            att_wt(pe, 2 * h, i)
            att_pv(pe, 2 * h, i)

        def over_heads(eng, emit, chain=None, per=0):
            for first in (0, HEADS):
                emit(first)
                with eng.Fori(0, 3) as i:
                    if chain:
                        chain.begin(i, 0, per[first])
                    emit(first + 1, i)
                    emit(first + 2, i)
                    if chain:
                        chain.end(3)
                emit(first + 7)

        def att_pe(pe):
            pe.wait_ge(sem("kr_roped"), 1)
            for t in range(n_keys):
                last = nc.tensor.transpose(ps[0:ROPE, 5, t * P:(t + 1) * P], kr_in[:, t, :], ident[:])
            last.then_inc(sem("kr_flip"), 1)
            pe.wait_ge(sem("at_dve"), 2)
            att_flip(pe, 0)
            over_heads(pe, lambda h, i=None: att_head_pe(pe, h, i, h != 2 * HEADS - 1))
            att_wt(pe, 4 * HEADS - 1)
            att_pv(pe, 4 * HEADS - 1)
            late_rows_pe(pe)

        def att_qT(act, h, i=None):
            par = h % 2
            act.wait_ge(sem("at_flip"), ev(h + 1, i))
            if h >= 2:
                act.wait_ge(sem("at_sc"), ev2(2 * (h - 1), i))
            first = nc.scalar.activation(qT[par][:], ps[:, 4, 0:SEQ], ACT.Copy)
            if h >= HEADS:
                first = nc.scalar.activation(qrT[par][0:ROPE, :], ps[0:ROPE, 4, SEQ:2 * SEQ], ACT.Copy)
            first.then_inc(sem("at_qT"), 1)

        def att_exp(act, u, i=None):
            latent = u >= 2 * HEADS
            par = u % 2
            act.wait_ge(sem("at_max"), ev2(u + 1, i))
            if u >= 2:
                act.wait_ge(sem("at_wflip"), ev2(u - 1, i))
            for j in range(1 if latent else 2):
                last = nc.scalar.activation(ex[par][:, j, :], ps[:, 2 * par + j, :], ACT.Exp,
                                            bias=mx[par][:, 2 + j:3 + j], scale=MLA_SCALE if latent else DA_SCALE,
                                            accum_out=mx[par][:, 4 + j:5 + j])
            last.then_inc(sem("at_exp"), 1)

        def att_wT(act, u, i=None):
            act.wait_ge(sem("at_wflip"), ev2(u + 1, i))
            if u >= 2:
                act.wait_ge(sem("at_pv"), ev2(u - 1, i))
            nc.scalar.activation(wT[u % 2][:].rearrange("p k q -> p (k q)"), ps[:, 6, :], ACT.Copy
                                 ).then_inc(sem("at_wT"), 1)

        def att_head_act(act, h, i=None):
            if h >= 1:
                att_wT(act, 2 * h - 1, i)
            att_exp(act, 2 * h, i)
            att_exp(act, 2 * h + 1, i)
            if h != 2 * HEADS - 1:
                att_qT(act, h + 1, i)
            if h < 2 * HEADS - 3:
                att_load_qk(act, h + 3, i)
            att_wT(act, 2 * h, i)

        def att_act(act):
            act.wait_ge(sem("at_dve"), 1)
            nc.scalar.activation(lamt[:, 0:2], lamt[:, 2:4], ACT.Exp).then_inc(sem("lam_exp"), 1)
            att_qT(act, 0)
            att_load_qk(act, 2)
            att_head_act(act, 0)
            for first, straight in ((1, (5, 6, 7, 8)), (HEADS + 1, (13, 14, 15))):
                with act.Fori(0, 2) as i:
                    att_head_act(act, first, i)
                    att_head_act(act, first + 1, i)
                for h in straight:
                    att_head_act(act, h)
            att_wT(act, 4 * HEADS - 1)
            act.wait_ge(sem("at_dve"), 3)
            nc.scalar.activation(ssum[:], ssum[:], ACT.Sqrt, bias=C["eps"], scale=1.0 / HD).then_inc(sem("o_rms"), 1)

        def att_kT(dve, h, i=None):
            par = h % 2
            dve.wait_ge(sem("at_flip"), ev(h + 1, i))
            if h >= 2:
                dve.wait_ge(sem("at_sc"), ev2(2 * (h - 1), i))
            nc.vector.tensor_copy(kT[par][:], ps[:, 5, :]).then_inc(sem("at_kT"), 1)

        def att_max(dve, chain, u, i=None):
            latent = u >= 2 * HEADS
            par = u % 2
            n = 1 if latent else 2
            dve.wait_ge(sem("at_sc"), ev2(u + 1, i))
            chain.done(nc.vector.reduce_max(mx[par][:, 0:n], ps[:, 2 * par:2 * par + n, :], AX))
            nc.vector.tensor_scalar(mx[par][:, 2:2 + n], mx[par][:, 0:n], -(MLA_SCALE if latent else DA_SCALE), None,
                                    ALU.mult).then_inc(sem("at_max"), 1)

        def att_weights(dve, chain, u, i=None):
            latent = u >= 2 * HEADS
            par = u % 2
            dve.wait_ge(sem("at_exp"), ev2(u + 1, i))
            n = 1 if latent else 2
            if latent:
                nc.vector.reciprocal(mx[par][:, 6:7], mx[par][:, 4:5]).then_inc(sem("at_w"), 1)
                return
            chain.done(nc.vector.reciprocal(mx[par][:, 6:8], mx[par][:, 4:6]))
            chain.done(nc.vector.tensor_scalar(mx[par][:, 7:8], mx[par][:, 7:8], C["lam"], None, ALU.mult))
            if u >= 2:
                dve.wait_ge(sem("at_wflip"), ev2(u - 1, i))
            chain.done(nc.vector.tensor_scalar(wt[par][:], ex[par][:, 1, :], mx[par][:, 7:8], None, ALU.mult))
            nc.vector.scalar_tensor_tensor(wt[par][:], ex[par][:, 0, :], mx[par][:, 6:7], wt[par][:], ALU.mult, ALU.add
                                           ).then_inc(sem("at_w"), 1)

        def att_out(dve, u, i=None):
            h, t = u // 2, u % 2
            dve.wait_ge(sem("at_pv"), ev2(u + 1, i))
            dst = o_all[:, t, bass.ds(head_col(h, i, HD), HD)]
            if u < 2 * HEADS:
                nc.vector.tensor_copy(dst, ps[:, 7, 0:HD]).then_inc(sem("at_o"), 1)
            else:
                nc.vector.tensor_scalar(dst, ps[:, 7, 0:HD], mx[t][:, 6:7], None, ALU.mult).then_inc(sem("at_o"), 1)

        def att_head_dve(dve, chain, h, i=None):
            def late(g):
                if h >= 1:
                    late_dve(dve, chain, h - 1, g, i)
            att_max(dve, chain, 2 * h, i)
            if h >= 1:
                att_out(dve, 2 * h - 1, i)
            late(0)
            att_weights(dve, chain, 2 * h, i)
            att_max(dve, chain, 2 * h + 1, i)
            late(1)
            if h != 2 * HEADS - 1:
                att_kT(dve, h + 1, i)
            late(2)
            att_weights(dve, chain, 2 * h + 1, i)
            att_out(dve, 2 * h, i)
            late(3)

        def att_dve(dve, chain):
            dve.wait_ge(sem("at_tab"), 16 * 7)
            chain.done(nc.vector.tensor_tensor(lam_in[:, 0:4:2, :], lam_in[:, 0:4:2, :], lam_in[:, 1:4:2, :], ALU.mult))
            nc.vector.reduce_sum(lamt[:, 2:4], lam_in[:, 0:4:2, :], AX).then_inc(sem("at_dve"), 1)
            for i in range(2):
                nc.vector.memset(qrT[i][:], 0.0)
            chain.done(nc.vector.memset(krT[:], 0.0))
            dve.wait_ge(sem("kr_flip"), 1)
            nc.vector.tensor_copy(krT[0:ROPE, :], ps[0:ROPE, 5, :]).then_inc(sem("at_dve"), 1)
            dve.wait_ge(sem("lam_exp"), 1)
            chain.done(nc.vector.tensor_tensor(lamt[:, 2:3], lamt[:, 1:2], lamt[:, 0:1], ALU.subtract))
            chain.done(nc.vector.tensor_scalar(C["lam"], lamt[:, 2:3], -LAMBDA_INIT, None, ALU.add))
            att_kT(dve, 0)
            late_n = 2 * (RING + 1)
            over_heads(dve, lambda h, i=None: att_head_dve(dve, chain, h, i), chain, {0: 16 + late_n, HEADS: 4 + late_n})
            att_out(dve, 4 * HEADS - 1)
            for g in range(RING):
                late_dve(dve, chain, 2 * HEADS - 1, g)
            dve.wait_ge(sem("at_o"), 4 * HEADS)
            da = o_all[:, :, 0:DA_W]
            chain.done(nc.vector.tensor_tensor(sq[:].rearrange("p (t n) -> p t n", t=TILES), da, da, ALU.mult))
            nc.vector.reduce_sum(ssum[:], sq[:].rearrange("p (h d) -> p h d", d=HD), AX).then_inc(sem("at_dve"), 1)
            dve.wait_ge(sem("at_dve"), 3)
            nc.vector.memset(ones[:], 1.0).then_inc(sem("at_dve"), 1)
            late_rows_dve(dve)
            dve.wait_ge(sem("o_rms"), 1)
            chain.done(nc.vector.reciprocal(ssum[:], ssum[:]))
            for t in range(TILES):
                v = o_all[:, t, 0:DA_W].rearrange("p (h d) -> p h d", d=HD)
                r = ssum[:, t * HEADS:(t + 1) * HEADS].unsqueeze(2).to_broadcast([P, HEADS, HD])
                last = nc.vector.tensor_tensor(v, v, r, ALU.mult)
            chain.done(last)
            nc.vector.tensor_scalar(C["subln_w"], C["subln_w"], 1.0 - LAMBDA_INIT, None, ALU.mult
                                    ).then_inc(sem("at_dve"), 1)
            dve.wait_ge(sem("at_dve"), 5)

        gate = [place(f"gate{i}", [P, CHUNK], at=S0 + i * CHUNK * 4) for i in range(2)]
        gated = tmp

        def gate_load(sp, m, first, n):
            if m >= 2:
                sp.wait_ge(sem("res_mul"), m - 1)
            sp.dma_start(gate[m % 2][:], MOD[0:1, first + n * CHUNK:first + (n + 1) * CHUNK].to_broadcast([P, CHUNK])
                         ).then_inc(sem(f"gate_in{m % 2}"), 16)

        def residual(dve, chain, L, n, m):
            c = L.c0 + n
            chunk_done(dve, L, n)
            dve.wait_ge(sem(f"gate_in{m % 2}"), 16 * (m // 2 + 1))
            g = gate[m % 2][:].unsqueeze(1).to_broadcast([P, TILES, CHUNK])
            nc.vector.tensor_tensor(gated[:], ps[:, acc_pair(c):acc_pair(c) + 2, :], g, ALU.mult
                                    ).then_inc(sem("res_mul"), 1)
            dve.wait_ge(sem("res_mul"), m + 1)
            cols = slice(n * CHUNK, (n + 1) * CHUNK)
            nc.vector.tensor_tensor(X[:, :, cols], X[:, :, cols], gated[:], ALU.add
                                    ).then_inc(sem(f"acc_free{c % 2}"), 1)

        def x_ready(eng, L):
            c = L.c0 + L.chunks
            for k in (c - 2, c - 1):
                eng.wait_ge(sem(f"acc_free{k % 2}"), k // 2 + 1)

        mix = (tile_of(b_hi), tile_of(b_lo))
        hx = (tile_of(a_hi), tile_of(a_lo))

        def wo_sp(sp):
            sp.wait_ge(sem("at_dve"), 3)
            sp.wait_ge(sem("late_stored"), 16 * N_LATE // 4)
            for n in range(4):
                gate_load(sp, n, 2 * D, n)
                if n:
                    load_chunk(sp, WO, n, n * CHUNK)

        def wo_pe(pe, hooks):
            for n in range(4):
                matmul_chunk(pe, WO, n, WO.c0 + n, [mix], hooks=hooks if n == 0 else {})

        def wo_act(act):
            for n in range(4):
                split_chunk(split_hi, act, WO, n, skip=3 if n == 0 else 0)

        def wo_dve(dve, chain):
            for n in range(4):
                hooks = {3: lambda: residual(dve, chain, WO, n - 1, n - 1)} if n else {}
                split_chunk(split_lo, dve, WO, n, hooks=hooks, skip=3 if n == 0 else 0)

        UP = [layers["up0"], layers["up1"]]
        DOWN = [layers["down0"], layers["down1"]]
        for L in UP:
            assert L.c0 % 2 == 0
        ff = tmp[:].rearrange("p a (k s) -> p (a k) s", s=SEQ)

        def ff_pair(q, j):
            return j + (UP[0].chunks // 2 if q else 0)

        def up_load(sp, q):
            L = UP[q]
            for h in range(2):
                load_chunk(sp, L, h, FF_PARTS[q][0] * P + h * D_FF)
            with sp.Fori(1, L.chunks // 2) as i:
                for h in range(2):
                    load_chunk(sp, L, h, i * CHUNK + (FF_PARTS[q][0] * P + h * D_FF), i=i, step=2 * L.per)

        def up_copy(act, q, n, i=None):
            L = UP[q]
            chunk_done(act, L, n, i, 2 * L.per)
            done = ff_pair(q, n // 2)
            if done >= 1 or i is not None:
                act.wait_ge(sem(f"ff_flip{n % 2}"), at(done, i, 1))
            if q == 1 and n == 0 and i is None:
                act.wait_ge(sem("res_mul"), 8)
            c = L.c0 + n
            nc.scalar.activation(stg[n % 2][:], ps[:, acc_pair(c):acc_pair(c) + 2, :], ACT.Copy
                                 ).then_inc(sem(f"acc_free{c % 2}"), 1)

        def up_flip(pe, q, n, i=None):
            c = UP[q].c0 + n
            done = ff_pair(q, n // 2)
            pe.wait_ge(sem(f"acc_free{c % 2}"), at(c // 2 + 1, i, 1))
            if done >= 1 or i is not None:
                pe.wait_ge(sem(("ff_conv", "ff_mul")[n % 2]), at(done, i, 1))
            for k in range(CT):
                for t in range(TILES):
                    last = nc.tensor.transpose(ps[:, 4 + 2 * (n % 2) + k // 2, (k % 2) * SEQ + t * P:(k % 2) * SEQ + (t + 1) * P],
                                               stg[n % 2][:, t, k * P:(k + 1) * P], ident[:])
            last.then_inc(sem(f"ff_flip{n % 2}"), 1)

        def up_conv(dve, chain, q, j, i=None):
            done = ff_pair(q, j)
            dve.wait_ge(sem("ff_flip0"), at(done + 1, i, 1))
            if done >= 1 or i is not None:
                dve.wait_ge(sem("ff_lo"), at(done, i, 1))
            kt = FF_PARTS[q][0] + j * CT if i is None else i * CT + (FF_PARTS[q][0] + j * CT)

            def w(name, k):
                a = kt + k
                return C[name][:, bass.ds(a, 1)]
            src = [ps[:, 4 + k // 2, (k % 2) * SEQ:(k % 2 + 1) * SEQ] for k in range(CT)]
            for k in range(CT):
                last = nc.vector.tensor_scalar(ff[:, k, :], src[k], w("conv_w1", k), w("conv_b", k), ALU.mult, ALU.add)
            chain.done(last)
            for k in range(CT):
                last = nc.vector.scalar_tensor_tensor(ff[:, k, 1:SEQ], src[k][:, 0:SEQ - 1], w("conv_w0", k),
                                                      ff[:, k, 1:SEQ], ALU.mult, ALU.add)
            chain.done(last)
            for k in range(CT):
                last = nc.vector.scalar_tensor_tensor(ff[:, k, 0:SEQ - 1], src[k][:, 1:SEQ], w("conv_w2", k),
                                                      ff[:, k, 0:SEQ - 1], ALU.mult, ALU.add)
            last.then_inc(sem("ff_conv"), 1)

        def up_silu(act, q, j, i=None):
            act.wait_ge(sem("ff_conv"), at(ff_pair(q, j) + 1, i, 1))
            nc.scalar.activation(ff, ff, ACT.Silu).then_inc(sem("ff_silu"), 1)

        def up_mul(dve, q, j, i=None):
            done = ff_pair(q, j)
            dve.wait_ge(sem("ff_silu"), at(done + 1, i, 1))
            dve.wait_ge(sem("ff_flip1"), at(done + 1, i, 1))
            nc.vector.tensor_tensor(tmp[:], tmp[:], ps[:, 6:8, :], ALU.mult).then_inc(sem("ff_mul"), 1)

        def b_tiles(buf, j, i):
            a = j * CT if i is None else i * CT + j * CT
            return buf[:, bass.ds(a, CT), :]

        def up_hi(act, q, j, i=None):
            if j == 0 and i is None and q == 1:
                chunk_done(act, DOWN[0], 3)
            act.wait_ge(sem("ff_mul"), at(ff_pair(q, j) + 1, i, 1))
            nc.scalar.activation(b_tiles(b_hi, j, i), ff, ACT.Copy).then_inc(sem("ff_hi"), 1)

        def up_lo(dve, q, j, i=None):
            dve.wait_ge(sem("ff_hi"), at(ff_pair(q, j) + 1, i, 1))
            nc.vector.tensor_tensor(b_tiles(b_lo, j, i), ff, b_tiles(b_hi, j, i).bitcast(F32), ALU.subtract
                                    ).then_inc(sem("ff_lo"), 1)

        def up_pe(pe, q, hooks={}):
            L = UP[q]
            for h in range(2):
                matmul_chunk(pe, L, h, L.c0 + h, [hx], hooks={} if h else hooks)
            with pe.Fori(1, L.chunks // 2) as i:
                kw = dict(i=i, step=2 * L.per, cstep=2)
                matmul_chunk(pe, L, 0, L.c0, [hx], hooks={2: lambda: up_flip(pe, q, -2, i), "end": lambda: up_flip(pe, q, -1, i)}, **kw)
                matmul_chunk(pe, L, 1, L.c0 + 1, [hx], **kw)

        def up_act(act, q, skip, first_hook=None):
            L = UP[q]
            split_chunk(split_hi, act, L, 0, skip=skip)
            split_chunk(split_hi, act, L, 1, hooks={3: lambda: up_copy(act, q, 0)})
            with act.Fori(1, L.chunks // 2) as i:
                kw = dict(i=i, step=2 * L.per)
                split_chunk(split_hi, act, L, 0, hooks={3: lambda: up_copy(act, q, -1, i)}, **kw)
                split_chunk(split_hi, act, L, 1, hooks={
                    1: lambda: up_silu(act, q, -1, i),
                    3: lambda: (up_hi(act, q, -1, i), up_copy(act, q, 0, i))}, **kw)

        def up_dve(dve, chain, q, skip, first_hooks={}):
            L = UP[q]
            split_chunk(split_lo, dve, L, 0, skip=skip, hooks=first_hooks)
            split_chunk(split_lo, dve, L, 1)
            with dve.Fori(1, L.chunks // 2) as i:
                kw = dict(i=i, step=2 * L.per)
                chain.begin(i, 1, 2)
                split_chunk(split_lo, dve, L, 0, hooks={"end": lambda: up_conv(dve, chain, q, -1, i)}, **kw)
                split_chunk(split_lo, dve, L, 1, hooks={2: lambda: up_mul(dve, q, -1, i), "end": lambda: up_lo(dve, q, -1, i)}, **kw)
                chain.end(L.chunks // 2)

        def down_pe(pe, q):
            L, U = DOWN[q], UP[q]
            last = U.chunks // 2 - 1
            up_flip(pe, q, U.chunks - 2)
            up_flip(pe, q, U.chunks - 1)

            def own_inputs():
                pe.wait_ge(sem("ff_lo"), ff_pair(q, last) + 1)
            first = next(g for g, (kt, n) in enumerate(L.groups) if kt + n > last * CT)
            pe.wait_ge(sem("ff_lo"), ff_pair(q, last))
            for n in range(4):
                matmul_chunk(pe, L, n, L.c0 + n, [mix], hooks={first: own_inputs} if n == 0 else {})

        def down_act(act, q):
            L, U = DOWN[q], UP[q]
            last = U.chunks // 2 - 1
            split_chunk(split_hi, act, L, 0, hooks={
                3: lambda: (up_copy(act, q, U.chunks - 1), up_silu(act, q, last)), 4: lambda: up_hi(act, q, last)})
            for n in range(1, 4):
                split_chunk(split_hi, act, L, n)

        def down_dve(dve, chain, q):
            L, U = DOWN[q], UP[q]
            last = U.chunks // 2 - 1
            split_chunk(split_lo, dve, L, 0, hooks={
                3: lambda: (up_conv(dve, chain, q, last), up_mul(dve, q, last)), 4: lambda: up_lo(dve, q, last)})
            for n in range(1, 4):
                split_chunk(split_lo, dve, L, n, hooks={3: lambda: residual(dve, chain, L, n - 1, 4 + 4 * q + n - 1)})

        def down_sp(sp, q):
            L = DOWN[q]
            for n in range(4):
                load_chunk(sp, L, n, n * CHUNK)
                if n == 0:
                    sp.wait_ge(sem("ff_flip0"), ff_pair(q, UP[q].chunks // 2 - 1) + 1)
                    sp.wait_ge(sem("ff_flip1"), ff_pair(q, UP[q].chunks // 2 - 1) + 1)
                gate_load(sp, 4 + 4 * q + n, 5 * D, n)

        final_w = place("final_w_sb", [P, D], at=B0)

        def final_sp(sp):
            chunk_done(sp, DOWN[1], 3)
            sp.dma_start(final_w[:], A["final_w"].rearrange("(a n) -> a n", a=1).to_broadcast([P, D])
                         ).then_inc(sem("norm_w_in"), 16)

        def final_dve(dve, chain):
            wait_rms(dve, "fn")
            chain.done(nc.vector.reciprocal(stat[:, 12:14], stat[:, 12:14]))
            dve.wait_ge(sem("norm_w_in"), 16)
            for t in range(TILES):
                last = nc.vector.scalar_tensor_tensor(X[:, t, :], X[:, t, :], stat[:, 12 + t:13 + t], final_w[:],
                                                      ALU.mult, ALU.mult)
            last.then_inc(sem("x3"), 1)

        CV, GT, RW, HO = (layers[n] for n in ("conv", "gates", "raw", "hout"))
        SI, SO = layers["scin"], layers["scout"]
        dn_w = place("dn_conv", [P, A_QKV // P, 4], at=B0)
        N_Z = DN_V * DN_D // CHUNK
        BLOCKS_AT, SOLVE_AT = 2, 8

        def raw_column(m):
            return OFF_AZ + m * CHUNK if m < N_Z else OFF_B + (m - N_Z) * CHUNK

        def hyb_sp(sp):
            sp.wait_ge(sem("x3"), 1)
            sp.dma_start(dn_w[:], A["dn_conv_w_2"][0].rearrange("(k p) j -> p k j", p=P)).then_inc(sem("conv_w_in"), 16)
            for n in range(2):
                load_chunk(sp, CV, n, n * CHUNK)
            with sp.Fori(1, CV.chunks // 2) as i:
                for h in range(2):
                    load_chunk(sp, CV, h, i * (2 * CHUNK) + h * CHUNK, i=i, step=2 * CV.per)
            load_chunk(sp, GT, 0, OFF_GATES, 2 * DN_V)
            for m in range(2):
                load_chunk(sp, RW, m, raw_column(m))
            gates_sp(sp)
            load_chunk(sp, RW, 2, raw_column(2))
            sp.wait_ge(sem("grow_stored"), 16)
            blk_load(sp, 0)
            blk_load(sp, 1)
            for m in range(3, SOLVE_AT):
                load_chunk(sp, RW, m, raw_column(m))
                for h in range(2 * (m - BLOCKS_AT), min(2 * (m - BLOCKS_AT + 1), DN_QK)):
                    blk_load(sp, h)
            solve_sp(sp)
            with sp.Fori(SOLVE_AT // 2, RW.chunks // 2) as i:
                for h in range(2):
                    load_chunk(sp, RW, h, i * (2 * CHUNK) + (OFF_B + (h - N_Z) * CHUNK), i=i, step=2 * RW.per)

        def cv_copy(act, n, i=None):
            chunk_done(act, CV, n, i, 2 * CV.per)
            if n >= 2 or i is not None:
                act.wait_ge(sem(f"cv_stored{n % 2}"), at(16 * (n // 2), i, 16))
            c = CV.c0 + n
            nc.scalar.activation(stg[n % 2][:], ps[:, acc_pair(c):acc_pair(c) + 2, :], ACT.Copy
                                 ).then_inc(sem(f"acc_free{c % 2}"), 1)

        def cv_flip(pe, n, i=None):
            c = CV.c0 + n
            pe.wait_ge(sem(f"acc_free{c % 2}"), at(c // 2 + 1, i, 1))
            if n >= 1 or i is not None:
                pe.wait_ge(sem("cv_conv"), at(n, i, 2))
            for k in range(CT):
                for t in range(TILES):
                    last = nc.tensor.transpose(ps[:, 4 + k // 2, (k % 2) * SEQ + t * P:(k % 2) * SEQ + (t + 1) * P],
                                               stg[n % 2][:, t, k * P:(k + 1) * P], ident[:])
            last.then_inc(sem("cv_flip"), 1)

        def causal_conv(dve, chain, weights, taps):
            src = [ps[:, 4 + k // 2, (k % 2) * SEQ:(k % 2 + 1) * SEQ] for k in range(CT)]
            for back in range(taps):
                for k in range(CT):
                    w = weights(k, taps - 1 - back)
                    if back == 0:
                        last = nc.vector.tensor_scalar(ff[:, k, :], src[k], w, None, ALU.mult)
                    else:
                        last = nc.vector.scalar_tensor_tensor(ff[:, k, back:SEQ], src[k][:, 0:SEQ - back], w,
                                                              ff[:, k, back:SEQ], ALU.mult, ALU.add)
                if back < taps - 1:
                    chain.done(last)
            return last

        def cv_conv(dve, chain, n, i=None):
            dve.wait_ge(sem("cv_flip"), at(n + 1, i, 2))
            if n >= 1 or i is not None:
                dve.wait_ge(sem("cv_back"), at(n, i, 2))
            kt = n * CT if i is None else i * (2 * CT) + n * CT

            def w(k, tap):
                a = kt + k
                return dn_w[:, bass.ds(a, 1), tap]
            causal_conv(dve, chain, w, 4).then_inc(sem("cv_conv"), 1)

        def cv_silu(act, n, i=None):
            act.wait_ge(sem("cv_conv"), at(n + 1, i, 2))
            nc.scalar.activation(ff, ff, ACT.Silu).then_inc(sem("cv_silu"), 1)

        def cv_back(pe, n, i=None):
            pe.wait_ge(sem("cv_silu"), at(n + 1, i, 2))
            if n >= 1 or i is not None:
                pe.wait_ge(sem("cv_out"), at(n, i, 2))
            for t in range(TILES):
                for k in range(CT):
                    last = nc.tensor.transpose(ps[:, 6 + t, k * P:(k + 1) * P], ff[:, k, t * P:(t + 1) * P], ident[:])
            last.then_inc(sem("cv_back"), 1)

        def cv_out(dve, n, i=None):
            dve.wait_ge(sem("cv_back"), at(n + 1, i, 2))
            nc.vector.tensor_copy(stg[n % 2][:], ps[:, 6:8, :]).then_inc(sem("cv_out"), 1)

        def cv_store(act, n, i=None):
            act.wait_ge(sem("cv_out"), at(n + 1, i, 2))
            c0 = n * CHUNK if i is None else i * (2 * CHUNK) + n * CHUNK
            act.dma_start(tok(CONV[:, bass.ds(c0, CHUNK)]), stg[n % 2][:]).then_inc(sem(f"cv_stored{n % 2}"), 16)

        def raw_store(act, m, i=None):
            chunk_done(act, RW, m, i, 2 * RW.per)
            par = m % 2
            if m < 2 and i is None:
                act.wait_ge(sem(f"cv_stored{par}"), 16 * CV.chunks // 2)
            else:
                act.wait_ge(sem(f"raw_stored{par}"), at(16 * (m // 2), i, 16))
            c = RW.c0 + m
            nc.scalar.activation(stg[par][:], ps[:, acc_pair(c):acc_pair(c) + 2, :], ACT.Copy
                                 ).then_inc(sem(f"acc_free{c % 2}"), 1)
            c0 = m * CHUNK if i is None else i * (2 * CHUNK) + m * CHUNK
            act.wait_ge(sem(f"acc_free{c % 2}"), at(c // 2 + 1, i, 1))
            act.dma_start(tok(RAW[:, bass.ds(c0, CHUNK)]), stg[par][:]).then_inc(sem(f"raw_stored{par}"), 16)

        def pairs_in(m):
            h = 2 * (m - BLOCKS_AT)
            return (h, h + 1) if 0 <= h < DN_QK else None

        def run_hooks(*steps):
            return lambda: [step() for step in steps]

        def hyb_act(act):
            split_chunk(split_hi, act, CV, 0, skip=3)
            split_chunk(split_hi, act, CV, 1, hooks={3: lambda: cv_copy(act, 0)})
            with act.Fori(1, CV.chunks // 2) as i:
                for h in range(2):
                    first = {3: run_hooks(lambda: cv_copy(act, h - 1, i), lambda: cv_silu(act, h - 2, i)),
                             "end": lambda: cv_store(act, h - 2, i)}
                    split_chunk(split_hi, act, CV, h, i=i, step=2 * CV.per, hooks=first)
            n = CV.chunks
            split_chunk(split_hi, act, GT, 0, 2 * DN_V, hooks={
                2: lambda: cv_silu(act, n - 2), 3: lambda: cv_copy(act, n - 1), "end": lambda: cv_store(act, n - 2)})
            split_chunk(split_hi, act, RW, 0, hooks={2: lambda: cv_silu(act, n - 1), 3: lambda: cv_store(act, n - 1)})
            split_chunk(split_hi, act, RW, 1, hooks={1: lambda: gates_act_1(act), 3: lambda: raw_store(act, 0),
                                                     "end": lambda: gates_act_2(act)})
            for m in range(2, SOLVE_AT):
                hooks = {1: [], 2: [], 3: [lambda: raw_store(act, m - 1)], "end": []}
                if m == 2:
                    hooks[1].append(lambda: gates_act_3(act))
                if pairs_in(m - 1):
                    b = pairs_in(m - 1)[1]
                    hooks[1].append(lambda: blk_exp(act, b))
                    hooks[3] += [lambda: blk_store(act, b - 1), lambda: blk_store(act, b)]
                if pairs_in(m):
                    a = pairs_in(m)[0]
                    hooks[2].append(lambda: blk_copy(act, a))
                    hooks[3].append(lambda: blk_exp(act, a))
                    hooks["end"].append(lambda: blk_copy(act, a + 1))
                split_chunk(split_hi, act, RW, m, hooks={g: run_hooks(*steps) for g, steps in hooks.items()})
            with act.Fori(SOLVE_AT // 2, RW.chunks // 2) as i:
                for h in range(2):
                    split_chunk(split_hi, act, RW, h, i=i, step=2 * RW.per, hooks={3: lambda: raw_store(act, h - 1, i)})
            raw_store(act, RW.chunks - 1)

        def zero_blocks(dve):
            for par in range(2):
                dve.wait_ge(sem(f"blk_stored{par}"), 32 * 4)
            for par in range(2):
                nc.vector.memset(ub[par][:], 0.0)
                last = nc.vector.memset(qb[par][:], 0.0)
            last.then_inc(sem("dl_zero"), 1)

        def hyb_dve(dve, chain):
            split_chunk(split_lo, dve, CV, 0, skip=3)
            dve.wait_ge(sem("conv_w_in"), 32)
            split_chunk(split_lo, dve, CV, 1)
            with dve.Fori(1, CV.chunks // 2) as i:
                chain.begin(i, 1, 6)
                for h in range(2):
                    split_chunk(split_lo, dve, CV, h, i=i, step=2 * CV.per, hooks={
                        3: lambda: cv_conv(dve, chain, h - 2, i), "end": lambda: cv_out(dve, h - 2, i)})
                chain.end(CV.chunks // 2)
            n = CV.chunks
            split_chunk(split_lo, dve, GT, 0, 2 * DN_V, hooks={
                1: lambda: cv_conv(dve, chain, n - 2), "end": lambda: cv_out(dve, n - 2)})
            split_chunk(split_lo, dve, RW, 0, hooks={
                1: lambda: cv_conv(dve, chain, n - 1), 3: lambda: cv_out(dve, n - 1), "end": lambda: gates_dve_1(dve)})
            split_chunk(split_lo, dve, RW, 1, hooks={1: lambda: gates_dve_2(dve, chain), 2: lambda: gates_dve_3(dve, chain),
                                                     3: lambda: gates_dve_4(dve, chain)})
            steps = solve_steps(dve, chain)
            for m in range(2, RW.chunks):
                hooks = {1: [], 2: [], "end": []}
                if m == 2:
                    hooks[1].append(lambda: gates_dve_5(dve, chain))
                if pairs_in(m - 1):
                    b = pairs_in(m - 1)[1]
                    hooks[1].append(lambda: blk_masked(dve, chain, b))
                if pairs_in(m):
                    a = pairs_in(m)[0]
                    hooks[2].append(lambda: blk_diff(dve, chain, a))
                    hooks["end"] += [lambda: blk_masked(dve, chain, a), lambda: blk_diff(dve, chain, a + 1)]
                if m == SOLVE_AT - 1:
                    hooks["end"].append(lambda: zero_blocks(dve))
                if m >= SOLVE_AT:
                    hooks = {g: [lambda: next(steps, None), lambda: next(steps, None)] for g in range(RW.per)}
                split_chunk(split_lo, dve, RW, m, hooks={g: run_hooks(*steps_) for g, steps_ in hooks.items()})
            for _ in steps:
                pass
            nc.vector.memset(stat[:, 20:21], 0.0).then_inc(sem("solved"), 1)

        def hyb_pe(pe, hooks):
            matmul_chunk(pe, CV, 0, CV.c0, [hx], hooks=hooks)
            matmul_chunk(pe, CV, 1, CV.c0 + 1, [hx], hooks={"end": lambda: cv_flip(pe, 0)})
            with pe.Fori(1, CV.chunks // 2) as i:
                for h in range(2):
                    matmul_chunk(pe, CV, h, CV.c0 + h, [hx], i=i, step=2 * CV.per, cstep=2, hooks={
                        3: lambda: cv_back(pe, h - 2, i), "end": lambda: cv_flip(pe, h - 1, i)})
            n = CV.chunks
            matmul_chunk(pe, GT, 0, GT.c0, [hx], 2 * DN_V, hooks={3: lambda: cv_back(pe, n - 2), "end": lambda: cv_flip(pe, n - 1)})
            matmul_chunk(pe, RW, 0, RW.c0, [hx], hooks={3: lambda: cv_back(pe, n - 1)})
            matmul_chunk(pe, RW, 1, RW.c0 + 1, [hx], hooks={3: lambda: gates_sums(pe), "end": lambda: gates_flip(pe)})
            for m in range(2, SOLVE_AT):
                hooks = {}
                if pairs_in(m):
                    a = pairs_in(m)[0]
                    hooks = {2: run_hooks(lambda: blk_flip(pe, a)),
                             3: run_hooks(lambda: blk_prod(pe, a), lambda: blk_flip(pe, a + 1)),
                             "end": run_hooks(lambda: blk_prod(pe, a + 1))}
                matmul_chunk(pe, RW, m, RW.c0 + m, [hx], hooks=hooks)
            with pe.Fori(SOLVE_AT // 2, RW.chunks // 2) as i:
                for h in range(2):
                    matmul_chunk(pe, RW, h, RW.c0 + h, [hx], i=i, step=2 * RW.per, cstep=2)

        def load_chunk_first(sp, L):
            for g in range(RING):
                load_piece(sp, L, L.p0 + g, *L.groups[g], 0)

        put = region(B0, X0)
        put_s = region(S0 + 2 * TILES * CHUNK * 4, S1)
        NH = DN_V
        qk_all = put("qk_all", [P, TILES, 2 * DN_QK * DN_D])
        tri = put("tri", [P, P])
        ones_half = [put(f"ones_half{b}", [P, P]) for b in range(2)]
        gcT = put("gcT", [NH, SEQ])
        BLK0 = B0 + (TILES * 2 * DN_QK * DN_D + 3 * P + SEQ) * 4
        g_in = put_s("g_in", [P, TILES, 2 * NH])
        a_log = put_s("a_log", [P, NH])
        dt_b = put_s("dt_b", [P, NH])
        tri_t = put_s("tri_t", [P, DN_CHUNK])
        names = ("beta", "z", "az_", "sp", "g", "gc", "gl", "eg", "ekd", "f_qg", "f_kb", "f_kd", "t0", "t1")
        G = {n: put_s("gate_" + n, [P, TILES, NH]) for n in names}
        r_qk = put_s("r_qk", [P, TILES, 2 * DN_QK])
        egl = put_s("egl", [P, 2 * TILES, NH])

        def gates_sp(sp):
            sp.wait_ge(sem("cv_back"), CV.chunks)
            for par in range(2):
                sp.wait_ge(sem(f"cv_stored{par}"), 16 * CV.chunks // 2)
            sp.dma_start(qk_all[:], tok(CONV[:, 0:2 * DN_QK * DN_D])).then_inc(sem("qk_all_in"), 16)
            sp.dma_start(a_log[:], A["dn_a_log_2"].to_broadcast([P, NH])).then_inc(sem("gates_in"), 16)
            sp.dma_start(dt_b[:], A["dn_dt_bias_2"].to_broadcast([P, NH])).then_inc(sem("gates_in"), 16)
            sp.dma_start(tri[:], A["const_tri"]).then_inc(sem("gates_in"), 16)
            for b in range(2):
                sp.dma_start(ones_half[b][:], A["const_half"][b]).then_inc(sem("gates_in"), 16)
            sp.dma_start(tri_t[:], A["const_tri_t"]).then_inc(sem("gates_in"), 16)

        def gates_act_1(act):
            act.wait_ge(sem("g_dve"), 1)
            nc.scalar.activation(G["beta"][:], g_in[:, :, 0:NH], ACT.Sigmoid).then_inc(sem("g_act"), 1)
            nc.scalar.activation(G["az_"][:], G["z"][:], ACT.Abs).then_inc(sem("g_act"), 1)
            act.wait_ge(sem("g_act"), 2)
            nc.scalar.activation(G["t0"][:], G["az_"][:], ACT.Exp, scale=-1.0).then_inc(sem("g_act"), 1)
            nc.scalar.activation(a_log[:], a_log[:], ACT.Exp).then_inc(sem("g_act"), 1)
            act.wait_ge(sem("g_act"), 3)
            nc.scalar.activation(G["sp"][:], G["t0"][:], ACT.Ln, bias=1.0).then_inc(sem("g_act"), 1)

        def gates_act_2(act):
            act.wait_ge(sem("g_dve"), 4)
            nc.scalar.activation(G["eg"][:], G["gc"][:], ACT.Exp).then_inc(sem("g_act"), 1)
            nc.scalar.activation(egl[:], egl[:], ACT.Exp).then_inc(sem("g_act"), 1)
            nc.scalar.activation(G["ekd"][:], G["t1"][:], ACT.Exp).then_inc(sem("g_act"), 1)
            nc.scalar.activation(r_qk[:], r_qk[:], ACT.Sqrt, bias=C["eps"]).then_inc(sem("g_act"), 1)

        def gates_act_3(act):
            act.wait_ge(sem("g_dve"), 5)
            act.dma_start(GROW, gcT[:]).then_inc(sem("grow_stored"), 16)

        def gates_sums(pe):
            pe.wait_ge(sem("g_dve"), 3)
            for t in range(TILES):
                nc.tensor.matmul(ps[:, 4, t * NH:(t + 1) * NH], tri[:], G["g"][:, t, :], start=True, stop=True)
                for b in range(2):
                    last = nc.tensor.matmul(ps[:, 5, (2 * t + b) * NH:(2 * t + b + 1) * NH], ones_half[b][:], G["g"][:, t, :],
                                            start=True, stop=True)
            last.then_inc(sem("g_pe"), 1)

        def gates_flip(pe):
            pe.wait_ge(sem("g_dve"), 4)
            for t in range(TILES):
                last = nc.tensor.transpose(ps[0:NH, 6, t * P:(t + 1) * P], G["gc"][:, t, :], ident[:])
            last.then_inc(sem("g_pe"), 1)

        def gates_square(pool):
            pool.wait_ge(sem("qk_all_in"), 16)
            nc.gpsimd.tensor_tensor(qk_all[:], qk_all[:], qk_all[:], ALU.mult).then_inc(sem("g_sq"), 1)

        def gates_dve_1(dve):
            chunk_done(dve, GT, 0)
            dve.wait_ge(sem("cv_back"), CV.chunks)
            a = acc_pair(GT.c0)
            freed = sem(f"acc_free{GT.c0 % 2}")
            nc.vector.tensor_copy(g_in[:], ps[:, a:a + 2, 0:2 * NH]).then_inc(freed, 1)
            dve.wait_ge(freed, GT.c0 // 2 + 1)
            dve.wait_ge(sem("gates_in"), 16 * 6)
            dt = dt_b[:].unsqueeze(1).to_broadcast([P, TILES, NH])
            nc.vector.tensor_tensor(G["z"][:], g_in[:, :, NH:], dt, ALU.add).then_inc(sem("g_dve"), 1)

        def gates_dve_2(dve, chain):
            dve.wait_ge(sem("g_sq"), 1)
            nc.vector.reduce_sum(r_qk[:].rearrange("p t h -> p (t h)"),
                                 qk_all[:].rearrange("p t (h d) -> p (t h) d", d=DN_D), AX).then_inc(sem("g_dve"), 1)

        def gates_dve_3(dve, chain):
            dve.wait_ge(sem("g_act"), 5)
            chain.done(nc.vector.scalar_tensor_tensor(G["sp"][:], G["z"][:], 0.0, G["sp"][:], ALU.max, ALU.add))
            al = a_log[:].unsqueeze(1).to_broadcast([P, TILES, NH])
            chain.done(nc.vector.tensor_tensor(G["g"][:], G["sp"][:], al, ALU.mult))
            nc.vector.tensor_scalar(G["g"][:], G["g"][:], -1.0, None, ALU.mult).then_inc(sem("g_dve"), 1)

        def gates_dve_4(dve, chain):
            dve.wait_ge(sem("g_pe"), 1)
            nc.vector.tensor_copy(G["gc"][:].rearrange("p t h -> p (t h)"), ps[:, 4, 0:TILES * NH])
            chain.done(nc.vector.tensor_copy(egl[:].rearrange("p n h -> p (n h)"), ps[:, 5, 0:2 * TILES * NH]))
            for b in range(2):
                half = slice(b * DN_CHUNK, (b + 1) * DN_CHUNK)
                last = nc.vector.tensor_tensor(G["t1"][half], egl[half, b::2, :], G["gc"][half], ALU.subtract)
            last.then_inc(sem("g_dve"), 1)

        def gates_dve_5(dve, chain):
            dve.wait_ge(sem("g_pe"), 2)
            nc.vector.tensor_copy(gcT[:], ps[0:NH, 6, 0:SEQ]).then_inc(sem("g_dve"), 1)
            dve.wait_ge(sem("g_act"), 9)
            chain.done(nc.vector.reciprocal(r_qk[:], r_qk[:]))
            chain.done(nc.vector.tensor_scalar(r_qk[:, :, 0:DN_QK], r_qk[:, :, 0:DN_QK], DN_D ** -0.5, None, ALU.mult))

            def pairs(v):
                return v.rearrange("p t (h v) -> p t h v", v=2)

            def both(v):
                return v.unsqueeze(3).to_broadcast([P, TILES, DN_QK, 2])
            rq, rk = r_qk[:, :, 0:DN_QK], r_qk[:, :, DN_QK:]
            for t in range(TILES):
                def v(n):
                    return pairs(G[n][:])[:, t]
                nc.vector.tensor_tensor(v("f_qg"), v("eg"), both(rq)[:, t], ALU.mult)
                nc.vector.tensor_tensor(v("f_kd"), v("ekd"), both(rk)[:, t], ALU.mult)
                nc.vector.tensor_tensor(v("f_kb"), v("eg"), both(rk)[:, t], ALU.mult)
            chain.done(nc.vector.tensor_copy(G["t0"][:], G["beta"][:]))
            nc.vector.tensor_tensor(G["f_kb"][:], G["f_kb"][:], G["beta"][:], ALU.mult).then_inc(sem("g_dve"), 1)
            dve.wait_ge(sem("g_dve"), 6)

        put = region(BLK0, X0)
        dq = [put(f"dq{i}", [P, 2, TILES, DN_D]) for i in range(2)]
        grow = [put(f"grow{i}", [P, 2, TILES, DN_CHUNK]) for i in range(2)]
        dqkT = [put(f"dqkT{i}", [P, 2, SEQ]) for i in range(2)]
        dd, dmax, dmin, dec, decT = (put(n, [P, 2, TILES, DN_CHUNK]) for n in ("dd", "dmax", "dmin", "dec", "decT"))
        am = [put(f"am{i}", [P, 2, TILES, DN_CHUNK]) for i in range(2)]
        qm = [put(f"qm{i}", [P, 2, TILES, DN_CHUNK]) for i in range(2)]

        def pairs_of_heads(eng, emit, chain=None, per=0, between=()):
            emit(0)
            emit(1)
            for step in between:
                step()
            with eng.Fori(1, 4) as i:
                if chain:
                    chain.begin(i, 1, per)
                emit(0, i)
                emit(1, i)
                if chain:
                    chain.end(4)

        def nth(h, i, unit):
            return h * unit if i is None else i * (2 * unit) + h * unit

        def blk_load(sp, h):
            par = h % 2
            if h >= 2:
                sp.wait_ge(sem("blk_flip"), h - 1)
                sp.wait_ge(sem("blk_diff"), h - 1)
            for j in range(2):
                sp.dma_start(dq[par][:, j], tok(CONV[:, (j * DN_QK + h) * DN_D:(j * DN_QK + h + 1) * DN_D])
                             ).then_inc(sem(f"blk_in{par}"), 16)
            for b in range(2):
                src = GROW[2 * h:2 * h + 2, :].rearrange("v (t b j) -> b v t j", t=TILES, b=2)[b:b + 1]
                sp.dma_start(grow[par][b * DN_CHUNK:(b + 1) * DN_CHUNK], src.to_broadcast([DN_CHUNK, 2, TILES, DN_CHUNK])
                             ).then_inc(sem(f"blk_in{par}"), 16)

        def head_pair(v, h, i):
            return v[:, :, bass.ds(nth(h, i, 2), 2)].rearrange("p t v -> p v t")

        def blk_scale(pool, h):
            par = h % 2
            pool.wait_ge(sem(f"blk_in{par}"), 64 * (h // 2 + 1))
            for j in range(2):
                r_ = r_qk[:, :, j * DN_QK + h:j * DN_QK + h + 1].to_broadcast([P, TILES, DN_D])
                last = nc.gpsimd.tensor_tensor(dq[par][:, j], dq[par][:, j], r_, ALU.mult)
            last.then_inc(sem("blk_scaled"), 1)

        def blk_flip(pe, h):
            pe.wait_ge(sem("blk_scaled"), h + 1)
            if h >= 1:
                pe.wait_ge(sem("blk_T"), h)
            for j in range(2):
                for t in range(TILES):
                    last = nc.tensor.transpose(ps[:, 4, (2 * j + t) * P:(2 * j + t + 1) * P], dq[h % 2][:, j, t], ident[:])
            last.then_inc(sem("blk_flip"), 1)

        def blk_prod(pe, h):
            par = h % 2
            pe.wait_ge(sem("blk_T"), h + 1)
            if h >= 1:
                pe.wait_ge(sem("blk_done"), h)
            for t in range(TILES):
                for b in range(2):
                    c = slice(t * P + b * DN_CHUNK, t * P + (b + 1) * DN_CHUNK)
                    o = slice(b * DN_CHUNK, (b + 1) * DN_CHUNK)
                    f = slice(t * DN_CHUNK, (t + 1) * DN_CHUNK)
                    nc.tensor.matmul(ps[o, 5, f], dqkT[par][:, 1, c], dqkT[par][:, 1, c], start=True, stop=True)
                    last = nc.tensor.matmul(ps[o, 6, f], dqkT[par][:, 1, c], dqkT[par][:, 0, c], start=True, stop=True)
            last.then_inc(sem("blk_prod"), 1)

        def blk_copy(act, h):
            act.wait_ge(sem("blk_flip"), h + 1)
            if h >= 2:
                act.wait_ge(sem("blk_prod"), h - 1)
            nc.scalar.activation(dqkT[h % 2][:].rearrange("p j s -> p (j s)"), ps[:, 4, :], ACT.Copy).then_inc(sem("blk_T"), 1)

        def blk_exp(act, h):
            act.wait_ge(sem("blk_diff"), h + 1)
            nc.scalar.activation(dec[:], dmax[:], ACT.Exp, scale=-1.0)
            nc.scalar.activation(decT[:], dmin[:], ACT.Exp).then_inc(sem("blk_dec"), 1)

        def blk_store(act, h):
            par = h % 2
            act.wait_ge(sem("blk_done"), h + 1)
            for dst, src in ((AM, am), (QM, qm)):
                act.dma_start(dst[2 * h:2 * h + 2].rearrange("v t p j -> p v t j"), src[par][:]
                              ).then_inc(sem(f"blk_stored{par}"), 16)

        blk_shape = [P, 2, TILES, DN_CHUNK]

        def blk_diff(dve, chain, h):
            par = h % 2
            dve.wait_ge(sem(f"blk_in{par}"), 64 * (h // 2 + 1))
            gc = head_pair(G["gc"], h, None).unsqueeze(3).to_broadcast(blk_shape)
            chain.done(nc.vector.tensor_tensor(dd[:], grow[par][:], gc, ALU.subtract))
            nc.vector.tensor_scalar(dmax[:], dd[:], 0.0, None, ALU.max)
            nc.vector.tensor_scalar(dmin[:], dd[:], 0.0, None, ALU.min).then_inc(sem("blk_diff"), 1)

        def blk_masked(dve, chain, h):
            par = h % 2
            dve.wait_ge(sem("blk_prod"), h + 1)
            dve.wait_ge(sem("blk_dec"), h + 1)
            if h >= 2:
                dve.wait_ge(sem(f"blk_stored{par}"), 32 * (h // 2))

            def prod(bank):
                return ps[:, bank, 0:P].rearrange("p (t j) -> p t j", t=TILES).unsqueeze(1).to_broadcast(blk_shape)
            mask = tri_t[:].unsqueeze(1).unsqueeze(1).to_broadcast(blk_shape)
            beta = head_pair(G["beta"], h, None).unsqueeze(3).to_broadcast(blk_shape)
            nc.vector.tensor_tensor(am[par][:], prod(5), dec[:], ALU.mult)
            chain.done(nc.vector.tensor_tensor(qm[par][:], prod(6), decT[:], ALU.mult))
            nc.vector.tensor_tensor(am[par][:], am[par][:], beta, ALU.mult)
            nc.vector.tensor_tensor(qm[par][:], qm[par][:], mask, ALU.mult).then_inc(sem("blk_done"), 1)

        put = region(B0, X0)
        a_sys = put("a_sys", [P, DN_CHUNK, DN_CHUNK])
        u_sys = put("u_sys", [P, DN_CHUNK // 2, DN_CHUNK])
        upd = put("upd", [P, 560])

        def solve_sp(sp):
            for par in range(2):
                sp.wait_ge(sem(f"blk_stored{par}"), 32 * 4)
            src = AM.rearrange("h t (b i) j -> (h t b) (i j)", b=2)
            for b in range(2):
                sp.dma_start(a_sys[b * n_sys:(b + 1) * n_sys].rearrange("s i j -> s (i j)"), src).then_inc(sem("a_in"), 16)
            sp.dma_start(u_sys[:], A["const_u"]).then_inc(sem("a_in"), 16)

        def solve_steps(dve, chain):
            dve.wait_ge(sem("a_in"), 48)
            for j in range(DN_CHUNK - 1):
                n_c, n_i = j // 2 + 1, DN_CHUNK - 1 - j
                a = a_sys[:, j + 1:, j].unsqueeze(1).to_broadcast([P, n_c, n_i])
                u = u_sys[:, 0:n_c, j:j + 1].to_broadcast([P, n_c, n_i])
                o = upd[:, 0:n_c * n_i].rearrange("p (c i) -> p c i", c=n_c)
                chain.done(nc.vector.tensor_tensor(o, a, u, ALU.mult))
                chain.done(nc.vector.tensor_tensor(u_sys[:, 0:n_c, j + 1:], u_sys[:, 0:n_c, j + 1:], o, ALU.subtract))
                yield

        def solve_act(act):
            act.wait_ge(sem("solved"), 1)
            dst = UM.rearrange("h t (s c b) i -> b (h t s) c i", s=2, b=2)
            for b in range(2):
                act.dma_start(dst[b], u_sys[b * n_sys:(b + 1) * n_sys]).then_inc(sem("u_stored"), 16)

        SOLVE_BYTES = (DN_CHUNK * DN_CHUNK * 3 // 2 + 560) * 4
        put = region(B0 + SOLVE_BYTES, X0)
        put_a = region(A0 + D * TILES * 4, B0)
        y_b = put_a("y_b", [P, TILES, SW_HEADS * HD])
        sc_q = [put(f"sc_q{i}", [P, 2, TILES, DN_D]) for i in range(2)]
        sc_v = [put(f"sc_v{i}", [P, TILES, 2, DN_D]) for i in range(2)]
        ub = [put(f"ub{i}", [P, 2, TILES, P]) for i in range(2)]
        qb = [put(f"qb{i}", [P, 2, TILES, P]) for i in range(2)]
        put = region(B0, B0 + SOLVE_BYTES)
        q_g, k_b, k_d, v_b = ([put(f"{n}{i}", [P, 2, TILES, DN_D]) for i in range(2)] for n in ("q_g", "k_b", "k_d", "v_b"))
        q_gT = [put(f"q_gT{i}", [P, 2, TILES, P]) for i in range(2)]
        wTn = [put(f"wTn{i}", [P, 2, TILES, P]) for i in range(2)]
        st = put("state", [P, 2, DN_D])
        LOADED_BYTES = 4 * 2 * (2 * TILES * P) * 4
        put = region(B0 + SOLVE_BYTES + LOADED_BYTES, X0)
        vn = [put(f"vn{b}", [P, 2, DN_D]) for b in range(2)]
        fshape = [P, 2, TILES, DN_D]

        def dl_load(sp, h, i=None):
            par = h % 2
            if i is not None:
                sp.wait_ge(sem("dl_used"), at(h - 1, i, 2))
            for j in range(2):
                sp.dma_start(sc_q[par][:, j], tok(CONV[:, j * DN_QK * DN_D:][:, bass.ds(nth(h, i, DN_D), DN_D)])
                             ).then_inc(sem(f"dl_in{par}"), 16)
            sp.dma_start(sc_v[par][:].rearrange("p t v d -> p t (v d)"),
                         tok(CONV[:, 2 * DN_QK * DN_D:][:, bass.ds(nth(h, i, 2 * DN_D), 2 * DN_D)])
                         ).then_inc(sem(f"dl_in{par}"), 16)
            for dst, m in ((qb[par], QM), (ub[par], UM)):
                if m is UM and h == 0 and i is None:
                    sp.wait_ge(sem("u_stored"), 32)
                for b in range(2):
                    half = slice(b * DN_CHUNK, (b + 1) * DN_CHUNK)
                    sp.dma_start(dst[half, :, :, half],
                                 m[bass.ds(nth(h, i, 2), 2), :, half, :].rearrange("v t p j -> p v t j")
                                 ).then_inc(sem(f"dl_in{par}"), 16)

        def delta_sp(sp):
            sp.wait_ge(sem("dl_zero"), 1)
            pairs_of_heads(sp, lambda h, i=None: dl_load(sp, h, i), between=(lambda: z_sp(sp),))

        def dl_pool(pool, h, i=None):
            par = h % 2
            pool.wait_ge(sem(f"dl_in{par}"), at(16 * 7 * (h // 2 + 1), i, 16 * 7))
            if i is not None:
                pool.wait_ge(sem("dl_used"), at(h - 1, i, 2))

            def f(n):
                return head_pair(G[n], h, i).unsqueeze(3).to_broadcast(fshape)
            q_, k_ = (sc_q[par][:, j].unsqueeze(1).to_broadcast(fshape) for j in range(2))
            nc.gpsimd.tensor_tensor(k_b[par][:], k_, f("f_kb"), ALU.mult)
            nc.gpsimd.tensor_tensor(q_g[par][:], q_, f("f_qg"), ALU.mult)
            nc.gpsimd.tensor_tensor(v_b[par][:], sc_v[par][:].rearrange("p t v d -> p v t d"), f("beta"), ALU.mult)
            nc.gpsimd.tensor_tensor(k_d[par][:], k_, f("f_kd"), ALU.mult).then_inc(sem("dl_scaled"), 1)

        def dl_flips(pe, h, i=None):
            par = h % 2
            pe.wait_ge(sem("dl_scaled"), at(h + 1, i, 2))
            if h >= 1 or i is not None:
                pe.wait_ge(sem("dl_T"), at(h, i, 2))
            for v in range(2):
                for t in range(TILES):
                    c = slice((2 * v + t) * P, (2 * v + t + 1) * P)
                    nc.tensor.transpose(ps[:, 4, c], q_g[par][:, v, t], ident[:])
                    last = nc.tensor.matmul(ps[:, 5, c], k_b[par][:, v, t], ub[par][:, v, t], start=True, stop=True)
            last.then_inc(sem("dl_flip"), 1)

        def dl_pe(pe, h, i=None, is_last=False):
            par = h % 2
            n0 = 2 * TILES
            for n in range(n0):
                if n == 2 and not is_last:
                    dl_flips(pe, h + 1, i)
                t, b = n // 2, n % 2
                B3 = (6, 7, 0) if n % 2 == 0 else (1, 2, 3)
                if n == 0:
                    pe.wait_ge(sem("dl_T"), at(h + 1, i, 2))
                for v in range(2):
                    o = ps[:, B3[0], v * P:(v + 1) * P]
                    nc_last = nc.tensor.matmul(o, ub[par][:, v, t], v_b[par][:, v, t], start=True, stop=n == 0)
                    if n:
                        if v == 0:
                            pe.wait_ge(sem("dl_state"), at(n0 * h + n, i, 2 * n0))
                        nc_last = nc.tensor.matmul(o, wTn[par][:, v, t], st[:, v], start=False, stop=True)
                nc_last.then_inc(sem("dl_new"), 1)
                if n >= 2 or h >= 1 or i is not None:
                    pe.wait_ge(sem("dl_out"), at(n0 * h + n - 1, i, 2 * n0))
                pe.wait_ge(sem("dl_vn"), at(n0 * h + n + 1, i, 2 * n0))
                for v in range(2):
                    up = nc.tensor.matmul(ps[:, B3[2], v * P:(v + 1) * P], k_d[par][:, v, t], vn[b][:, v], start=True, stop=True)
                up.then_inc(sem("dl_up"), 1)
                for v in range(2):
                    o = ps[:, B3[1], v * P:(v + 1) * P]
                    if n:
                        nc.tensor.matmul(o, q_gT[par][:, v, t], st[:, v], start=True, stop=False)
                    last = nc.tensor.matmul(o, qb[par][:, v, t], vn[b][:, v], start=n == 0, stop=True)
                last.then_inc(sem("dl_o"), 1)

        def dl_copies(act, h, i=None):
            par, n0 = h % 2, 2 * TILES
            act.wait_ge(sem("dl_flip"), at(h + 1, i, 2))
            if h >= 2:
                act.wait_ge(sem("dl_o"), at(n0 * (h - 1), i, 2 * n0))
            nc.scalar.activation(q_gT[par][:].rearrange("p v t s -> p (v t s)"), ps[:, 4, :], ACT.Copy)
            nc.scalar.activation(wTn[par][:].rearrange("p v t s -> p (v t s)"), ps[:, 5, :], ACT.Copy, scale=-1.0
                                 ).then_inc(sem("dl_T"), 1)

        def dl_act(act, h, i=None, is_last=False):
            n0 = 2 * TILES
            for n in range(n0):
                if n == 2 and not is_last:
                    dl_copies(act, h + 1, i)
                t, b = n // 2, n % 2
                half = slice(b * DN_CHUNK, (b + 1) * DN_CHUNK)
                bank = 7 if n % 2 == 0 else 2
                act.wait_ge(sem("dl_o"), at(n0 * h + n + 1, i, 2 * n0))
                nc.scalar.activation(o_all[half, t, bass.ds(nth(h, i, 2 * DN_D), 2 * DN_D)], ps[half, bank, 0:2 * DN_D],
                                     ACT.Copy).then_inc(sem("dl_out"), 1)
            nc.scalar.activation(stat[:, 21:22], stat[:, 20:21], ACT.Copy).then_inc(sem("dl_used"), 1)

        def delta_heads(eng, ahead, emit):
            ahead(eng, 0)
            emit(eng, 0)
            with eng.Fori(0, 3) as i:
                emit(eng, 1, i)
                emit(eng, 2, i)
            emit(eng, DN_QK - 1, None, True)

        def dl_dve(dve, h, i=None):
            n0 = 2 * TILES
            for n in range(n0):
                t, b = n // 2, n % 2
                half = slice(b * DN_CHUNK, (b + 1) * DN_CHUNK)
                B3 = (6, 7, 0) if n % 2 == 0 else (1, 2, 3)
                dve.wait_ge(sem("dl_new"), at(n0 * h + n + 1, i, 2 * n0))
                if n >= 2 or h >= 1 or i is not None:
                    dve.wait_ge(sem("dl_o"), at(n0 * h + n - 1, i, 2 * n0))
                nc.vector.tensor_copy(vn[b][half].rearrange("p v d -> p (v d)"), ps[half, B3[0], 0:2 * DN_D]
                                      ).then_inc(sem("dl_vn"), 1)
                dve.wait_ge(sem("dl_up"), at(n0 * h + n + 1, i, 2 * n0))
                if n:
                    dve.wait_ge(sem("dl_o"), at(n0 * h + n + 1, i, 2 * n0))
                elif h >= 1 or i is not None:
                    dve.wait_ge(sem("dl_o"), at(n0 * h, i, 2 * n0))
                for v in range(2):
                    u = ps[:, B3[2], v * P:(v + 1) * P]
                    if n == 0:
                        last = nc.vector.tensor_copy(st[:, v], u)
                    else:
                        decay = egl[:, n, bass.ds(at(2 * h + v, i, 4), 1)]
                        last = nc.vector.scalar_tensor_tensor(st[:, v], st[:, v], decay, u, ALU.mult, ALU.add)
                last.then_inc(sem("dl_state"), 1)

        z_a = place("z_a", [P, TILES, D], at=W0)
        sq_a = place("sq_a", [P, TILES, D], at=W0 + TILES * D * 4)
        z_b = place("z_b", [P, TILES, SW_HEADS * HD], at=W0 + 2 * TILES * D * 4)
        ss_a = place("ss_a", [P, TILES * NH], at=W0 + (2 * D + SW_HEADS * HD) * TILES * 4)

        def z_sp(sp):
            sp.wait_ge(sem("piece_used"), HO.p0)
            for par in range(2):
                sp.wait_ge(sem(f"raw_stored{par}"), 16 * RW.chunks // 2)
            sp.dma_start(z_a[:], tok(RAW[:, 0:D])).then_inc(sem("z_in"), 16)
            sp.dma_start(z_b[:], tok(RAW[:, W_RAW - SW_HEADS * HD:W_RAW])).then_inc(sem("z_in"), 16)

        def out_pool(pool):
            pool.wait_ge(sem("dl_out"), 4 * DN_QK)
            nc.gpsimd.tensor_tensor(sq_a[:], o_all[:], o_all[:], ALU.mult).then_inc(sem("out_pool"), 1)
            pool.wait_ge(sem("out_act"), 1)
            nc.gpsimd.tensor_tensor(z_a[:], z_a[:], o_all[:], ALU.mult).then_inc(sem("out_pool"), 1)

        def out_act(act):
            act.wait_ge(sem("z_in"), 32)
            nc.scalar.activation(z_a[:], z_a[:], ACT.Silu)
            nc.scalar.activation(z_b[:], z_b[:], ACT.Silu).then_inc(sem("out_act"), 1)

        def out_dve_1(dve):
            dve.wait_ge(sem("out_pool"), 1)
            nc.vector.reduce_sum(ss_a[:], sq_a[:].rearrange("p t (h d) -> p (t h) d", d=DN_D), AX).then_inc(sem("out_dve"), 1)

        def out_rms(act):
            act.wait_ge(sem("out_dve"), 1)
            nc.scalar.activation(ss_a[:], ss_a[:], ACT.Sqrt, bias=C["eps"], scale=1.0 / DN_D).then_inc(sem("out_act"), 1)

        def out_dve_2(dve, chain):
            dve.wait_ge(sem("out_act"), 2)
            chain.done(nc.vector.reciprocal(ss_a[:], ss_a[:]))
            dve.wait_ge(sem("out_pool"), 2)
            v = z_a[:].rearrange("p t (h d) -> p (t h) d", d=DN_D)
            chain.done(nc.vector.tensor_tensor(o_all[:].rearrange("p t (h d) -> p (t h) d", d=DN_D), v,
                                               ss_a[:].unsqueeze(2).to_broadcast([P, TILES * NH, DN_D]), ALU.mult))

        def out_dve_3(dve):
            dve.wait_ge(sem("out_act"), 1)
            dve.wait_ge(sem("sw_o"), 4 * 4)
            nc.vector.tensor_tensor(y_b[:], y_b[:], z_b[:], ALU.mult).then_inc(sem("out_dve"), 1)
            dve.wait_ge(sem("out_dve"), 2)

        put = region(B0, X0)
        KEYS = SEQ
        WQ = SW_GROUPS * SEQ
        sq_in = [put(f"sw_q{i}", [P, TILES, SW_GROUPS, HD]) for i in range(2)]
        sk_in = [put(f"sw_k{i}", [P, TILES, HD]) for i in range(2)]
        sv_in = [put(f"sw_v{i}", [P, TILES, HD]) for i in range(2)]
        sqkT = [put(f"sw_T{i}", [P, 2 * CHUNK]) for i in range(2)]
        sw_mask = put("sw_mask", [P, TILES, WQ])
        sw_s = [put(f"sw_s{i}", [P, WQ]) for i in range(2)]
        sw_pT = [put(f"sw_pT{i}", [P, TILES, P]) for i in range(2)]
        put_s2 = region(S0, S1)
        RD = 32
        sw_c = put_s2("sw_c", [P, TILES, RD])
        sw_n = put_s2("sw_n", [P, TILES, RD])
        sw_m0 = put_s2("sw_m0", [P, TILES, SW_GROUPS + 1, RD])
        sw_m1 = put_s2("sw_m1", [P, TILES, SW_GROUPS + 1, RD])
        smx = [put_s2(f"smx{i}", [P, 8]) for i in range(2)]

        def sw_load(sp, h, i=None):
            par = h % 2
            if i is not None:
                sp.wait_ge(sem("sw_pv"), at(2 * (h - 1), i, 4))
            for g in range(SW_GROUPS):
                c0 = D + g * SW_HEADS * HD
                sp.dma_start(sq_in[par][:, :, g], tok(RAW[:, c0:][:, bass.ds(nth(h, i, HD), HD)])
                             ).then_inc(sem(f"sw_in{par}"), 16)
            for dst, c0 in ((sk_in, D + W_BQ), (sv_in, D + W_BQ + SW_HEADS * HD)):
                sp.dma_start(dst[par][:], tok(RAW[:, c0:][:, bass.ds(nth(h, i, HD), HD)])).then_inc(sem(f"sw_in{par}"), 16)

        def sw_sp(sp):
            sp.wait_ge(sem("dl_out"), 4 * DN_QK)
            sp.wait_ge(sem("dl_used"), DN_QK)
            sp.wait_ge(sem("dl_state"), 4 * DN_QK)
            sp.dma_start(sw_mask[:], A["const_sw_mask"]).then_inc(sem("sw_tab"), 16)
            sp.dma_start(sw_c[:], tok(A["const_sw_c"])).then_inc(sem("sw_tab"), 16)
            sp.dma_start(sw_n[:], tok(A["const_sw_s"])).then_inc(sem("sw_tab"), 16)
            pairs_of_heads(sp, lambda h, i=None: sw_load(sp, h, i))

        def sw_rope(pool, chain, h, i=None):
            par = h % 2
            pool.wait_ge(sem(f"sw_in{par}"), at(80 * (h // 2 + 1), i, 80))
            if h >= 1 or i is not None:
                pool.wait_ge(sem("sw_roped"), at(h, i, 2))
            f = RD // 2
            for t in range(TILES):
                q_, k_ = sq_in[par][:, t, :, 0:RD], sk_in[par][:, t, 0:RD]
                cq = sw_c[:, t, :].unsqueeze(1).to_broadcast([P, SW_GROUPS, RD])
                nc.gpsimd.tensor_tensor(sw_m0[:, t, 0:SW_GROUPS], q_, cq, ALU.mult)
                nc.gpsimd.tensor_tensor(sw_m0[:, t, SW_GROUPS], k_, sw_c[:, t, :], ALU.mult)
                for j in range(2):
                    a, b = slice(j * f, (j + 1) * f), slice((1 - j) * f, (2 - j) * f)
                    sn = sw_n[:, t, a].unsqueeze(1).to_broadcast([P, SW_GROUPS, f])
                    nc.gpsimd.tensor_tensor(sw_m1[:, t, 0:SW_GROUPS, a], q_[:, :, b], sn, ALU.mult)
                    last = nc.gpsimd.tensor_tensor(sw_m1[:, t, SW_GROUPS, a], k_[:, b], sw_n[:, t, a], ALU.mult)
            chain.done(last)
            for t in range(TILES):
                nc.gpsimd.tensor_tensor(sq_in[par][:, t, :, 0:RD], sw_m0[:, t, 0:SW_GROUPS], sw_m1[:, t, 0:SW_GROUPS], ALU.add)
                last = nc.gpsimd.tensor_tensor(sk_in[par][:, t, 0:RD], sw_m0[:, t, SW_GROUPS], sw_m1[:, t, SW_GROUPS], ALU.add)
            last.then_inc(sem("sw_roped"), 1)

        def sw_flip(pe, h, i=None):
            par = h % 2
            pe.wait_ge(sem("sw_roped"), at(h + 1, i, 2))
            if h >= 1 or i is not None:
                pe.wait_ge(sem("sw_T"), at(h, i, 2))
            for g in range(SW_GROUPS):
                for t in range(TILES):
                    nc.tensor.transpose(ps[:, 4 + g // 2, (g % 2) * SEQ + t * P:(g % 2) * SEQ + (t + 1) * P],
                                        sq_in[par][:, t, g], ident[:])
            for t in range(TILES):
                last = nc.tensor.transpose(ps[:, 5, SEQ + t * P:SEQ + (t + 1) * P], sk_in[par][:, t], ident[:])
            last.then_inc(sem("sw_flip"), 1)

        def sw_scores(pe, h, t, i=None):
            par, u = h % 2, 2 * h + t
            pe.wait_ge(sem("sw_T"), at(h + 1, i, 2))
            if u >= 2 or i is not None:
                pe.wait_ge(sem("sw_masked"), at(u - 1, i, 4))
            kT_ = sqkT[par][:, SW_GROUPS * SEQ:]
            for g in range(SW_GROUPS):
                last = nc.tensor.matmul(ps[:, 2 * t + g // 2, (g % 2) * SEQ:(g % 2 + 1) * SEQ],
                                        sqkT[par][:, g * SEQ + t * P:g * SEQ + (t + 1) * P], kT_, start=True, stop=True)
            last.then_inc(sem("sw_sc"), 1)

        def sw_pv(pe, u, i=None):
            par = (u // 2) % 2
            pe.wait_ge(sem("sw_w"), at(u + 1, i, 4))
            if u >= 1 or i is not None:
                pe.wait_ge(sem("sw_wT"), at(u, i, 4))
            for t in range(TILES):
                last = nc.tensor.transpose(ps[:, 6, t * P:(t + 1) * P], sw_s[u % 2][:, t * P:(t + 1) * P], ident[:])
            last.then_inc(sem("sw_wflip"), 1)
            pe.wait_ge(sem("sw_wT"), at(u + 1, i, 4))
            if u >= 1 or i is not None:
                pe.wait_ge(sem("sw_o"), at(u, i, 4))
            for t in range(TILES):
                last = nc.tensor.matmul(ps[:, 7, 0:HD], sw_pT[u % 2][:, t], sv_in[par][:, t], start=t == 0, stop=t == TILES - 1)
            last.then_inc(sem("sw_pv"), 1)

        def sw_pe(pe):
            def head(h, i=None):
                sw_flip(pe, h, i)
                sw_scores(pe, h, 0, i)
                if h >= 1 or i is not None:
                    sw_pv(pe, 2 * h - 1, i)
                sw_scores(pe, h, 1, i)
                sw_pv(pe, 2 * h, i)
            pairs_of_heads(pe, head)
            sw_pv(pe, 2 * SW_HEADS - 1)

        def sw_act(act):
            def sT(h, i=None):
                act.wait_ge(sem("sw_flip"), at(h + 1, i, 2))
                if i is not None:
                    act.wait_ge(sem("sw_sc"), at(2 * (h - 1), i, 4))
                nc.scalar.activation(sqkT[h % 2][:], ps[:, 4:6, :].rearrange("p a n -> p (a n)"), ACT.Copy
                                     ).then_inc(sem("sw_T"), 1)

            def ex_(u, i=None):
                act.wait_ge(sem("sw_max"), at(u + 1, i, 4))
                nc.scalar.activation(sw_s[u % 2][:], sw_s[u % 2][:], ACT.Exp, bias=smx[u % 2][:, 1:2], scale=SW_SCALE,
                                     accum_out=smx[u % 2][:, 2:3]).then_inc(sem("sw_exp"), 1)

            def pT(u, i=None):
                act.wait_ge(sem("sw_wflip"), at(u + 1, i, 4))
                if u >= 2 or i is not None:
                    act.wait_ge(sem("sw_pv"), at(u - 1, i, 4))
                nc.scalar.activation(sw_pT[u % 2][:].rearrange("p k q -> p (k q)"), ps[:, 6, 0:SEQ], ACT.Copy
                                     ).then_inc(sem("sw_wT"), 1)

            def head(h, i=None):
                sT(h, i)
                if h >= 1 or i is not None:
                    pT(2 * h - 1, i)
                ex_(2 * h, i)
                pT(2 * h, i)
                ex_(2 * h + 1, i)
            pairs_of_heads(act, head, between=(lambda: out_act(act), lambda: out_rms(act)))
            pT(2 * SW_HEADS - 1)

        def sw_dve(dve, chain):
            def scores(u, i=None):
                par = u % 2
                dve.wait_ge(sem("sw_sc"), at(u + 1, i, 4))
                if u >= 2 or i is not None:
                    dve.wait_ge(sem("sw_wflip"), at(u - 1, i, 4))
                nc.vector.tensor_tensor(sw_s[par][:], ps[:, 2 * par:2 * par + 2, :].rearrange("p a n -> p (a n)")[:, 0:WQ],
                                        sw_mask[:, par, :], ALU.add).then_inc(sem("sw_masked"), 1)
                dve.wait_ge(sem("sw_masked"), at(u + 1, i, 4))
                chain.done(nc.vector.reduce_max(smx[par][:, 0:1], sw_s[par][:], AX))
                nc.vector.tensor_scalar(smx[par][:, 1:2], smx[par][:, 0:1], -SW_SCALE, None, ALU.mult).then_inc(sem("sw_max"), 1)

            def weights(u, i=None):
                s_ = sw_s[u % 2]
                dve.wait_ge(sem("sw_exp"), at(u + 1, i, 4))
                nc.vector.reciprocal(smx[u % 2][:, 3:4], smx[u % 2][:, 2:3])
                chain.done(nc.vector.tensor_tensor(s_[:, 0:SEQ], s_[:, 0:SEQ], s_[:, SEQ:2 * SEQ], ALU.add))
                nc.vector.tensor_tensor(s_[:, 0:SEQ], s_[:, 0:SEQ], s_[:, 2 * SEQ:3 * SEQ], ALU.add).then_inc(sem("sw_w"), 1)

            def output(u, i=None):
                h, t = u // 2, u % 2
                dve.wait_ge(sem("sw_pv"), at(u + 1, i, 4))
                nc.vector.tensor_scalar(y_b[:, t, bass.ds(nth(h, i, HD), HD)], ps[:, 7, 0:HD], smx[t][:, 3:4], None,
                                        ALU.mult).then_inc(sem("sw_o"), 1)

            def head(h, i=None):
                scores(2 * h, i)
                if h >= 1 or i is not None:
                    output(2 * h - 1, i)
                weights(2 * h, i)
                scores(2 * h + 1, i)
                output(2 * h, i)
                weights(2 * h + 1, i)
            dve.wait_ge(sem("sw_tab"), 48)
            pairs_of_heads(dve, head, chain, 8, (lambda: out_dve_1(dve), lambda: out_dve_2(dve, chain)))
            output(2 * SW_HEADS - 1)

        def plain_residual(dve, L, n):
            c = L.c0 + n
            chunk_done(dve, L, n)
            cols = slice(n * CHUNK, (n + 1) * CHUNK)
            nc.vector.tensor_tensor(X[:, :, cols], X[:, :, cols], ps[:, acc_pair(c):acc_pair(c) + 2, :], ALU.add
                                    ).then_inc(sem(f"acc_free{c % 2}"), 1)

        def plain_pe(pe, L, skip_wait=None):
            for n in range(4):
                matmul_chunk(pe, L, n, L.c0 + n, [mix], hooks=skip_wait if n == 0 and skip_wait else {})

        def plain_sp(sp, L, skip=0):
            for n in range(4):
                load_chunk(sp, L, n, n * CHUNK, skip=skip if n == 0 else 0)

        def plain_act(act, L, skip, hooks={}):
            for n in range(4):
                split_chunk(split_hi, act, L, n, skip=skip if n == 0 else 0, hooks=hooks if n == 0 else {})

        def plain_dve(dve, L, skip, hooks={}):
            for n in range(4):
                split_chunk(split_lo, dve, L, n, skip=skip if n == 0 else 0,
                            hooks={3: lambda: plain_residual(dve, L, n - 1)} if n else hooks)
            plain_residual(dve, L, 3)

        sc_w = place("sc_conv", [P, SC_KT, 3])
        SB = 4 * SI.per

        def sc_acc(n):
            a = acc_pair(SI.c0 + n)
            return ps[:, a:a + 2, :]

        def sc_freed(n):
            return sem(f"acc_free{(SI.c0 + n) % 2}")

        def sc_sp(sp):
            order = (SC_W, 2 * SC_W, 0, 3 * SC_W)
            for n, c0 in enumerate(order):
                load_chunk(sp, SI, n, c0)
            with sp.Fori(0, SC_W // CHUNK - 1) as i:
                for n, c0 in enumerate(order):
                    load_chunk(sp, SI, n + 4, i * CHUNK + (CHUNK + c0), i=i, step=SB)

        def sc_c(act, i=None):
            chunk_done(act, SI, 0, i, SB)
            if i is not None:
                act.wait_ge(sem("sc_flip"), i)
            nc.scalar.activation(stg[0][:], sc_acc(0), ACT.Copy).then_inc(sc_freed(0), 1)

        def sc_u(dve, i=None):
            chunk_done(dve, SI, 1, i, SB)
            dve.wait_ge(sc_freed(0), at(SI.c0 // 2 + 1, i, 2))
            nc.vector.tensor_tensor(stg[0][:], stg[0][:], sc_acc(1), ALU.mult).then_inc(sc_freed(1), 1)

        def sc_b(act, i=None):
            chunk_done(act, SI, 2, i, SB)
            if i is not None:
                act.wait_ge(sem("sc_flip"), i)
            nc.scalar.activation(stg[1][:], sc_acc(2), ACT.Copy).then_inc(sc_freed(2), 1)

        def sc_z(act, i):
            act.wait_ge(sem("piece_used"), at(SI.p0, i, SB))
            nc.scalar.activation(tmp[:], sc_acc(3), ACT.Silu).then_inc(sc_freed(3), 1)

        def sc_bz(dve, i):
            dve.wait_ge(sc_freed(3), i * 2 + ((SI.c0 + 3) // 2 - 1))
            nc.vector.tensor_tensor(stg[1][:], stg[1][:], tmp[:], ALU.mult).then_inc(sem("sc_bz"), 1)

        def sc_flip(pe, i, first=False):
            pe.wait_ge(sem("sc_bz"), i)
            if not first:
                pe.wait_ge(sem("sc_mul"), i - 1)
            for j in range(2):
                for k in range(CT):
                    for t in range(TILES):
                        last = nc.tensor.transpose(
                            ps[:, 4 + 2 * j + k // 2, (k % 2) * SEQ + t * P:(k % 2) * SEQ + (t + 1) * P],
                            stg[j][:, t, k * P:(k + 1) * P], ident[:])
            last.then_inc(sem("sc_flip"), 1)

        def sc_conv(dve, chain, i):
            dve.wait_ge(sem("sc_flip"), i)

            def w(k, tap):
                a = i * CT + (k - CT)
                return sc_w[:, bass.ds(a, 1), tap]
            chain.done(causal_conv(dve, chain, w, 3))
            nc.vector.tensor_tensor(tmp[:], tmp[:], ps[:, 6:8, :], ALU.mult).then_inc(sem("sc_mul"), 1)

        def sc_hi(act, i):
            act.wait_ge(sem("sc_mul"), i)
            nc.scalar.activation(b_hi[:, bass.ds(i * CT - CT, CT), :], ff, ACT.Copy).then_inc(sem("sc_hi"), 1)

        def sc_lo(dve, i):
            dve.wait_ge(sem("sc_hi"), i)
            nc.vector.tensor_tensor(b_lo[:, bass.ds(i * CT - CT, CT), :], ff, b_hi[:, bass.ds(i * CT - CT, CT), :].bitcast(F32),
                                    ALU.subtract).then_inc(sem("sc_lo"), 1)

        N_SC = SC_W // CHUNK

        def sc_act(act):
            def turn(i, first_skip=0):
                kw = dict(i=i, step=SB)
                split_chunk(split_hi, act, SI, 0, skip=first_skip, hooks={} if i is None else {3: lambda: sc_z(act, i)}, **kw)
                split_chunk(split_hi, act, SI, 1, hooks={3: lambda: sc_c(act, i)}, **kw)
                split_chunk(split_hi, act, SI, 2, hooks={} if i is None else {1: lambda: sc_hi(act, i)}, **kw)
                split_chunk(split_hi, act, SI, 3, hooks={3: lambda: sc_b(act, i)}, **kw)
            turn(None, 3)
            with act.Fori(1, N_SC) as i:
                turn(i)

        def sc_dve(dve, chain):
            def turn(i, first_skip=0):
                kw = dict(i=i, step=SB)
                split_chunk(split_lo, dve, SI, 0, skip=first_skip, hooks={} if i is None else {"end": lambda: sc_bz(dve, i)}, **kw)
                split_chunk(split_lo, dve, SI, 1, hooks={} if i is None else {3: lambda: sc_conv(dve, chain, i)}, **kw)
                h = {3: lambda: sc_u(dve, i)}
                if i is not None:
                    h[2] = lambda: sc_lo(dve, i)
                split_chunk(split_lo, dve, SI, 2, hooks=h, **kw)
                split_chunk(split_lo, dve, SI, 3, **kw)
            turn(None, 3)
            with dve.Fori(1, N_SC) as i:
                chain.begin(i, 1, 3)
                turn(i)
                chain.end(N_SC)

        def sc_pe(pe, first_hooks):
            def turn(i):
                kw = dict(i=i, step=SB, cstep=4)
                for n in range(4):
                    h = {1: lambda: sc_flip(pe, i)} if n == 1 and i is not None else {}
                    if n == 0 and i is None:
                        h = first_hooks
                    matmul_chunk(pe, SI, n, SI.c0 + n, [hx], hooks=h, **kw)
            turn(None)
            with pe.Fori(1, 2) as i:
                kw = dict(i=i, step=SB, cstep=4)
                for n in range(4):
                    h = {1: lambda: sc_flip(pe, i, True)} if n == 1 else {}
                    matmul_chunk(pe, SI, n, SI.c0 + n, [hx], hooks=h, **kw)
            with pe.Fori(2, N_SC) as i:
                turn(i)

        def sc_last_pe(pe):
            sc_flip(pe, N_SC)

            def own_inputs():
                pe.wait_ge(sem("sc_lo"), N_SC)
            pe.wait_ge(sem("sc_lo"), N_SC - 1)
            first = next(g for g, (kt, n) in enumerate(SO.groups) if kt + n > (N_SC - 1) * CT)
            plain_pe(pe, SO, {first: own_inputs})

        put = region(A0, B0)
        w_last = put("w_last", [P, D])
        y_out = put("y_out", [P, TILES, D])

        def last_sp(sp):
            chunk_done(sp, SI, SI.chunks - 1)
            sp.dma_start(w_last[:], A["final_norm_w_2"].rearrange("(a n) -> a n", a=1).to_broadcast([P, D])
                         ).then_inc(sem("norm_w_in"), 16)
            for t in range(TILES):
                sp.wait_ge(sem("y_out"), t + 1)
                sp.dma_start(out[t * P:(t + 1) * P, :], y_out[:, t, :]).then_inc(sem("out_stored"), 16)
            sp.wait_ge(sem("out_stored"), 16 * TILES)

        def last_dve(dve, chain):
            wait_rms(dve, "ln")
            chain.done(nc.vector.reciprocal(stat[:, 18:20], stat[:, 18:20]))
            dve.wait_ge(sem("norm_w_in"), 32)
            for t in range(TILES):
                nc.vector.scalar_tensor_tensor(y_out[:, t, :], X[:, t, :], stat[:, 18 + t:19 + t], w_last[:],
                                               ALU.mult, ALU.mult).then_inc(sem("y_out"), 1)

        x_tiles = [X[:, t, :] for t in range(TILES)]
        x_at = lambda kt, t: X[:, t, kt * P:(kt + 1) * P]

        block = ctx.enter_context(nc.Block())

        @block.sync
        def _(sp):
            ada_sp(sp)
            cols_sp(sp)
            proj_sp(sp)
            lat_sp(sp)
            att_sp(sp)
            wo_sp(sp)
            late_cols_sp(sp)
            up_load(sp, 0)
            down_sp(sp, 0)
            up_load(sp, 1)
            down_sp(sp, 1)
            final_sp(sp)
            sp.dma_start(sc_w[:], A["sc_conv_w_2"][0].rearrange("(k p) j -> p k j", p=P)).then_inc(sem("conv_w_in"), 16)
            hyb_sp(sp)
            load_chunk_first(sp, HO)
            delta_sp(sp)
            sw_sp(sp)
            plain_sp(sp, HO, RING)
            sc_sp(sp)
            plain_sp(sp, SO)
            last_sp(sp)

        @block.gpsimd
        def _(pool):
            chain = Count(pool, sem("pool_chain"))
            att_pool(pool, chain)
            gates_square(pool)
            pool.wait_ge(sem("g_dve"), 6)
            for h in range(DN_QK):
                blk_scale(pool, h)
            pairs_of_heads(pool, lambda h, i=None: dl_pool(pool, h, i))
            pool.wait_ge(sem("sw_tab"), 48)

            def swr(h, i=None):
                sw_rope(pool, chain, h, i)
            swr(0)
            swr(1)
            out_pool(pool)
            with pool.Fori(1, 4) as i:
                chain.begin(i, 1, 2)
                swr(0, i)
                swr(1, i)
                chain.end(4)

        @block.scalar
        def _(act):
            ada_act(act)
            presplit(split_hi, act, KV)
            act.wait_ge(sem("x_in"), 16)
            act.wait_ge(sem("cols"), 1)
            norm_stats_act(act, "n1", [X[:, t, :] for t in range(TILES)], D, 0)
            flip_act(act, "n1", KT // 2, a_hi)
            act.wait_ge(sem("ctx_in"), 32)
            norm_stats_act(act, "n1c", [ctx_in[t][:] for t in range(TILES)], D, 2)
            flip_act(act, "n1c", KT // 2, b_hi)
            proj_stream(act, split_hi, store_act)
            lat_act(act)
            att_act(act)
            late_store(act)
            act.wait_ge(sem("late_stored"), 16 * N_LATE // 4)
            presplit(split_hi, act, WO)
            flip_act(act, "mix", KT // 2, b_hi)
            wo_act(act)
            presplit(split_hi, act, UP[0])
            x_ready(act, WO)
            norm_stats_act(act, "n2", [X[:, t, :] for t in range(TILES)], D, 10)
            flip_act(act, "n2", KT // 2, a_hi)
            up_act(act, 0, 3)
            down_act(act, 0)
            up_act(act, 1, 0)
            down_act(act, 1)
            x_ready(act, DOWN[1])
            norm_stats_act(act, "fn", x_tiles, D, 12)
            presplit(split_hi, act, CV)
            act.wait_ge(sem("x3"), 1)
            norm_stats_act(act, "n3", x_tiles, D, 14)
            flip_act(act, "n3", KT // 2, a_hi)
            hyb_act(act)
            solve_act(act)
            delta_heads(act, dl_copies, dl_act)
            sw_act(act)
            presplit(split_hi, act, HO)
            flip_act(act, "mix2", MIX_KT // 2, b_hi)
            plain_act(act, HO, 3)
            presplit(split_hi, act, SI)
            x_ready(act, HO)
            norm_stats_act(act, "n4", x_tiles, D, 16)
            flip_act(act, "n4", KT // 2, a_hi)
            sc_act(act)
            plain_act(act, SO, 0, {3: lambda: sc_z(act, N_SC), 4: lambda: sc_hi(act, N_SC)})
            x_ready(act, SO)
            norm_stats_act(act, "ln", x_tiles, D, 18)

        @block.vector
        def _(dve):
            chain = Count(dve, sem("dve_chain"))
            ada_dve(dve, chain)
            presplit(split_lo, dve, KV)
            cols_dve(dve, chain)
            norm_diag_dve(dve, "n1", TILES, 0, chain)
            flip_dve(dve, "n1", KT // 2, c_of("m1"), c_of("sh1"), a_hi, a_lo)
            norm_diag_dve(dve, "n1c", TILES, 2, chain)
            flip_dve(dve, "n1c", KT // 2, c_of("m1c"), c_of("sh1c"), b_hi, b_lo)
            proj_stream(dve, split_lo, store_dve)
            lat_dve(dve, chain)
            att_dve(dve, chain)
            presplit(split_lo, dve, WO)
            flip_dve(dve, "mix", KT // 2, lambda kt: C["subln_w"] if kt < HEADS else 1.0, None, b_hi, b_lo)
            wo_dve(dve, chain)
            residual(dve, chain, WO, 3, 3)
            presplit(split_lo, dve, UP[0])
            late_cols_dve(dve, chain)
            norm_diag_dve(dve, "n2", TILES, 10, chain)
            flip_dve(dve, "n2", KT // 2, c_of("m2"), c_of("sh2"), a_hi, a_lo)
            up_dve(dve, chain, 0, 3)
            down_dve(dve, chain, 0)
            up_dve(dve, chain, 1, 0, first_hooks={3: lambda: residual(dve, chain, DOWN[0], 3, 7)})
            down_dve(dve, chain, 1)
            residual(dve, chain, DOWN[1], 3, 11)
            final_dve(dve, chain)
            presplit(split_lo, dve, CV)
            norm_diag_dve(dve, "n3", TILES, 14, chain)
            flip_dve(dve, "n3", KT // 2, c_of("norm_w_2"), None, a_hi, a_lo)
            hyb_dve(dve, chain)
            dve.wait_ge(sem("u_stored"), 32)
            for par in range(2):
                last = nc.vector.memset(vn[par][:], 0.0)
            chain.done(last)
            pairs_of_heads(dve, lambda h, i=None: dl_dve(dve, h, i))
            sw_dve(dve, chain)
            out_dve_3(dve)
            presplit(split_lo, dve, HO)
            flip_dve(dve, "mix2", MIX_KT // 2, lambda kt: C["dn_norm_w_2"] if kt < DN_V else 1.0, None, b_hi, b_lo)
            plain_dve(dve, HO, 3)
            presplit(split_lo, dve, SI)
            norm_diag_dve(dve, "n4", TILES, 16, chain)
            flip_dve(dve, "n4", KT // 2, c_of("norm_w_2", 16), None, a_hi, a_lo)
            sc_dve(dve, chain)
            plain_dve(dve, SO, 0, {3: lambda: (sc_bz(dve, N_SC), sc_conv(dve, chain, N_SC)), 4: lambda: sc_lo(dve, N_SC)})
            last_dve(dve, chain)

        @block.tensor
        def _(pe):
            ada_pe(pe)
            cols_pe(pe)
            flip_pe(pe, "n1", lambda kt, t: X[:, t, kt * P:(kt + 1) * P], KT // 2, lambda t: diag[:, t, :],
                    lambda: wait_diag(pe, "n1"))
            flip_pe(pe, "n1c", lambda kt, t: ctx_in[t][:, kt * P:(kt + 1) * P], KT // 2, lambda t: diag[:, t, :],
                    lambda: wait_diag(pe, "n1c"))
            proj_pe(pe)
            lat_pe(pe)
            att_pe(pe)
            wo_pe(pe, flip_hooks(pe, WO, "mix", lambda kt, t: o_all[:, t, kt * P:(kt + 1) * P], lambda t: ident[:],
                                 lambda: pe.wait_ge(sem("at_dve"), 5)))
            late_cols_pe(pe)
            up_pe(pe, 0, flip_hooks(pe, UP[0], "n2", x_at, lambda t: diag[:, t, :], lambda: wait_diag(pe, "n2")))
            down_pe(pe, 0)
            up_pe(pe, 1)
            down_pe(pe, 1)
            hyb_pe(pe, flip_hooks(pe, CV, "n3", x_at, lambda t: diag[:, t, :], lambda: wait_diag(pe, "n3")))
            delta_heads(pe, dl_flips, dl_pe)
            sw_pe(pe)
            plain_pe(pe, HO, flip_hooks(pe, HO, "mix2", lambda kt, t: o_all[:, t, kt * P:(kt + 1) * P] if kt < DN_V else
                                        y_b[:, t, (kt - DN_V) * P:(kt - DN_V + 1) * P], lambda t: ident[:],
                                        lambda: pe.wait_ge(sem("out_dve"), 2)))
            sc_pe(pe, flip_hooks(pe, SI, "n4", x_at, lambda t: diag[:, t, :], lambda: wait_diag(pe, "n4")))
            sc_last_pe(pe)


def constants():
    sel = np.zeros((4, P), np.float32)
    sel[[0, 2], 0] = sel[[1, 3], 1] = 1.0
    n_f = ROPE // 4
    inv = np.float32(10000.0) ** (-np.arange(n_f, dtype=np.float32) / n_f)
    rows, cols = np.arange(SEQ) // 64, np.arange(SEQ) % 64
    ang = np.stack([rows[:, None].astype(np.float32) * inv, cols[:, None].astype(np.float32) * inv], 1)
    c = np.stack([np.cos(ang), np.cos(ang)], 2).reshape(SEQ, ROPE)
    s = np.stack([-np.sin(ang), np.sin(ang)], 2).reshape(SEQ, ROPE)
    i, j = np.arange(P)[:, None], np.arange(P)[None, :]
    tri = ((i <= j) & (i // DN_CHUNK == j // DN_CHUNK)).astype(np.float32)
    half = np.stack([np.broadcast_to(i // DN_CHUNK == b, (P, P)) for b in range(2)]).astype(np.float32)
    tri_t = (np.arange(DN_CHUNK)[None, :] >= i % DN_CHUNK).astype(np.float32)
    cc, ii = np.arange(DN_CHUNK // 2)[None, :, None], np.arange(DN_CHUNK)[None, None, :]
    u0 = (ii == 2 * cc + (np.arange(P) // DN_CHUNK)[:, None, None]).astype(np.float32)
    q_at = np.arange(SEQ)[:, None]
    back = q_at - np.arange(SEQ)[None, :]
    seen = [(back >= 0) & (back % dil == 0) & (back // dil <= 128) for _, dil in SW_PATTERNS]
    mask = np.where(np.stack(seen, 1), 0.0, MASKED).astype(np.float32).reshape(TILES, P, -1).transpose(1, 0, 2)
    n_r = 16
    inv2 = np.power(np.float32(500000.0), -np.arange(n_r, dtype=np.float32) * np.float32(2.0) / np.float32(2 * n_r))
    ang2 = np.arange(SEQ, dtype=np.float32)[:, None] * inv2[None, :].astype(np.float32)
    extra = {"const_tri": tri, "const_half": half, "const_tri_t": tri_t, "const_u": u0,
             "const_sw_mask": np.ascontiguousarray(mask),
             "const_sw_c": np.concatenate([np.cos(ang2)] * 2, 1).astype(np.float32),
             "const_sw_s": np.concatenate([-np.sin(ang2), np.sin(ang2)], 1).astype(np.float32)}
    return {**extra, "const_sel": sel, "const_ident": np.eye(P, dtype=np.float32),
            "const_rope_c": np.tile(c, 2).astype(np.float32), "const_rope_s": np.tile(s, 2).astype(np.float32)}


def kernel(**inputs):
    import concourse.bacc as bacc
    from concourse.bass_utils import run_bass_kernel_spmd

    nc = bacc.Bacc("TRN2", target_bir_lowering=False, num_devices=1)
    arrays, aps = {}, {}
    for name, a in {**inputs, **constants()}.items():
        a = np.ascontiguousarray(a)
        arrays[f"in_{name}"] = a
        aps[name] = nc.dram_tensor(f"in_{name}", a.shape, mybir.dt.from_np(a.dtype), kind="ExternalInput").ap()
    out = nc.dram_tensor("out_0", (1, SEQ, D), F32, kind="ExternalOutput").ap()
    build_program(nc, aps, out[0])
    r = run_bass_kernel_spmd(nc, [arrays], core_ids=[0])
    return r.results[0]["out_0"]
```
